# Optimizing a Trainium2 kernel written in Bass

```python
import jax, jax.numpy as jnp
from jax import lax
import numpy as np

D_MODEL = 1024
BATCH = 1
SEQ = 2048
DEPTH = 1

GRID_W = 64
CTX_LEN = 256
ROPE_THETA = 10000.0
Q_BLOCK = 128
EPS = 1e-6

MLA_HEADS = 6
MLA_NOPE = 64
MLA_ROPE = 32
MLA_V = 64
MLA_Q_RANK = 256
MLA_KV_RANK = 128
GQA_HEADS = 6
GQA_KV_HEADS = 2
GQA_HEAD_DIM = 64
CONV_WIDTH = 256
D_FF = 4 * D_MODEL

MLA_OUT = MLA_HEADS * MLA_V
GQA_OUT = GQA_HEADS * GQA_HEAD_DIM
MIX_WIDTH = MLA_OUT + GQA_OUT + CONV_WIDTH
GQA_KV_W = GQA_KV_HEADS * GQA_HEAD_DIM

KV_COLS = MLA_KV_RANK + MLA_ROPE + 2 * GQA_KV_W
Q_COLS = MLA_Q_RANK + GQA_HEADS * GQA_HEAD_DIM
IN_COLS = KV_COLS + Q_COLS + 3 * CONV_WIDTH

ALPHA = (2.0 * DEPTH) ** 0.25
BETA = (8.0 * DEPTH) ** -0.25
N_MOD = 6

kernel_name = "hybrid_mla_gqa_shortconv_dit_trunk"

def layer_norm(x, g, b):
    xf = x.astype(jnp.float32)
    mu = xf.mean(-1, keepdims=True)
    var = jnp.square(xf - mu).mean(-1, keepdims=True)
    return ((xf - mu) * lax.rsqrt(var + EPS)).astype(x.dtype) * g + b

def rms_norm(x, g):
    xf = x.astype(jnp.float32)
    return (xf * lax.rsqrt(jnp.square(xf).mean(-1, keepdims=True) + EPS)).astype(x.dtype) * g

def axial_rope(row, col, dim):
    n_freq = dim // 4
    inv = ROPE_THETA ** (-jnp.arange(n_freq, dtype=jnp.float32) / n_freq)
    ang = jnp.concatenate([row[:, None].astype(jnp.float32) * inv,
                           col[:, None].astype(jnp.float32) * inv], axis=-1)
    return jnp.cos(ang), jnp.sin(ang)

def apply_rope(x, cs):
    cos = cs[0][None, :, None, :].astype(x.dtype)
    sin = cs[1][None, :, None, :].astype(x.dtype)
    x1, x2 = x[..., 0::2], x[..., 1::2]
    return jnp.stack([x1 * cos - x2 * sin, x1 * sin + x2 * cos], axis=-1).reshape(x.shape)

def block_attention(q, k, v, n_kv):
    B, S, H, dq = q.shape
    dv = v.shape[-1]
    G = H // n_kv
    nb = S // Q_BLOCK
    scale = dq ** -0.5
    qb = jnp.moveaxis(q.reshape(B, nb, Q_BLOCK, n_kv, G, dq), 1, 0)

    def one_block(qblk):
        s = jnp.einsum('bqkgd,blkd->bkgql', qblk, k).astype(jnp.float32) * scale
        p = jax.nn.softmax(s, axis=-1).astype(v.dtype)
        return jnp.einsum('bkgql,blkd->bqkgd', p, v)

    o = lax.map(one_block, qb)
    return jnp.moveaxis(o, 0, 1).reshape(B, S, H * dv)

def short_conv(u, w):
    up = jnp.pad(u, ((0, 0), (1, 1), (0, 0)))
    return up[:, :-2] * w[0] + up[:, 1:-1] * w[1] + up[:, 2:] * w[2]

def kv_side(h, g_ckv, w_ukv, g_kn, ropes):
    B, L, _ = h.shape
    o = 0
    c_kv = h[..., o:o + MLA_KV_RANK]; o += MLA_KV_RANK
    k_pe = h[..., o:o + MLA_ROPE].reshape(B, L, 1, MLA_ROPE); o += MLA_ROPE
    g_k = h[..., o:o + GQA_KV_W].reshape(B, L, GQA_KV_HEADS, GQA_HEAD_DIM); o += GQA_KV_W
    g_v = h[..., o:o + GQA_KV_W].reshape(B, L, GQA_KV_HEADS, GQA_HEAD_DIM)
    kv = (rms_norm(c_kv, g_ckv) @ w_ukv).reshape(B, L, MLA_HEADS, MLA_NOPE + MLA_V)
    k_nope, m_v = kv[..., :MLA_NOPE], kv[..., MLA_NOPE:]
    g_k = rms_norm(g_k, g_kn)
    if ropes is not None:
        k_pe = apply_rope(k_pe, ropes[0])
        g_k = apply_rope(g_k, ropes[1])
    m_k = jnp.concatenate([k_nope, jnp.broadcast_to(k_pe, (B, L, MLA_HEADS, MLA_ROPE))], axis=-1)
    return (m_k, m_v, g_k, g_v)

def mixer_out(h, kv, g_cq, w_uq, g_qn, w_conv, w_o, ropes):
    B, L, _ = h.shape
    hq = h[..., KV_COLS:KV_COLS + Q_COLS]
    mq = (rms_norm(hq[..., :MLA_Q_RANK], g_cq) @ w_uq).reshape(B, L, MLA_HEADS, MLA_NOPE + MLA_ROPE)
    q_nope, q_pe = mq[..., :MLA_NOPE], mq[..., MLA_NOPE:]
    gq = rms_norm(hq[..., MLA_Q_RANK:].reshape(B, L, GQA_HEADS, GQA_HEAD_DIM), g_qn)
    if ropes is not None:
        q_pe = apply_rope(q_pe, ropes[0])
        gq = apply_rope(gq, ropes[1])
    mq = jnp.concatenate([q_nope, q_pe], axis=-1)
    mo = block_attention(mq, kv[0], kv[1], MLA_HEADS)
    go = block_attention(gq, kv[2], kv[3], GQA_KV_HEADS)
    hc = h[..., KV_COLS + Q_COLS:]
    ch = hc[..., :CONV_WIDTH]
    cb = hc[..., CONV_WIDTH:2 * CONV_WIDTH]
    cc = hc[..., 2 * CONV_WIDTH:]
    co = cb * short_conv(cc * ch, w_conv)
    return jnp.concatenate([mo, go, co], axis=-1) @ w_o

def sq_relu_mlp(u, w1, w2):
    return jnp.square(jax.nn.relu(u @ w1)) @ w2

def setup_inputs(seed: int = 0) -> dict:
    key = jax.random.key(seed)
    ks = jax.random.split(key, 24)
    nrm = jax.random.normal
    f32 = jnp.float32
    d = D_MODEL
    return {
        "x": nrm(ks[0], (BATCH, SEQ, d), f32),
        "c": nrm(ks[1], (BATCH, d), f32),
        "ctx": nrm(ks[2], (BATCH, CTX_LEN, d), f32),
        "c_ctx": nrm(ks[3], (d,), f32),
        "w_ada": nrm(ks[4], (DEPTH, d, N_MOD * d), f32) * (0.5 * d ** -0.5),
        "b_ada": nrm(ks[5], (DEPTH, N_MOD * d), f32) * 0.01,
        "w_in": nrm(ks[6], (DEPTH, d, IN_COLS), f32) * d ** -0.5,
        "g_cq": 1.0 + 0.1 * nrm(ks[7], (DEPTH, MLA_Q_RANK), f32),
        "w_uq": nrm(ks[8], (DEPTH, MLA_Q_RANK, MLA_HEADS * (MLA_NOPE + MLA_ROPE)), f32) * MLA_Q_RANK ** -0.5,
        "g_ckv": 1.0 + 0.1 * nrm(ks[9], (DEPTH, MLA_KV_RANK), f32),
        "w_ukv": nrm(ks[10], (DEPTH, MLA_KV_RANK, MLA_HEADS * (MLA_NOPE + MLA_V)), f32) * MLA_KV_RANK ** -0.5,
        "g_qn": 1.0 + 0.1 * nrm(ks[11], (DEPTH, GQA_HEAD_DIM), f32),
        "g_kn": 1.0 + 0.1 * nrm(ks[12], (DEPTH, GQA_HEAD_DIM), f32),
        "w_conv": nrm(ks[13], (DEPTH, 3, CONV_WIDTH), f32) * 3.0 ** -0.5,
        "w_o": nrm(ks[14], (DEPTH, MIX_WIDTH, d), f32) * (BETA * MIX_WIDTH ** -0.5),
        "ln1_g": 1.0 + 0.1 * nrm(ks[15], (DEPTH, d), f32),
        "ln1_b": 0.02 * nrm(ks[16], (DEPTH, d), f32),
        "w_mlp1": nrm(ks[17], (DEPTH, d, D_FF), f32) * d ** -0.5,
        "w_mlp2": nrm(ks[18], (DEPTH, D_FF, d), f32) * (BETA * D_FF ** -0.5),
        "ln2_g": 1.0 + 0.1 * nrm(ks[19], (DEPTH, d), f32),
        "ln2_b": 0.02 * nrm(ks[20], (DEPTH, d), f32),
    }

def reference(x, c, ctx, c_ctx, w_ada, b_ada, w_in, g_cq, w_uq, g_ckv, w_ukv, g_qn, g_kn,
              w_conv, w_o, ln1_g, ln1_b, w_mlp1, w_mlp2, ln2_g, ln2_b):
    B, S, D = x.shape
    ROWS = S // GRID_W
    row = jnp.broadcast_to(jnp.arange(ROWS)[:, None], (ROWS, GRID_W)).reshape(-1)
    col = jnp.broadcast_to(jnp.arange(GRID_W)[None, :], (ROWS, GRID_W)).reshape(-1)
    ropes = (axial_rope(row, col, MLA_ROPE), axial_rope(row, col, GQA_HEAD_DIM))

    z = ctx
    sc = jax.nn.silu(c)
    sz = jax.nn.silu(c_ctx)
    for l in range(DEPTH):
        update_ctx = l < DEPTH - 1
        mx = (sc @ w_ada[l] + b_ada[l]).reshape(B, N_MOD, D)[:, :, None, :]
        mz = (sz @ w_ada[l] + b_ada[l]).reshape(N_MOD, D)

        u_z = z * (1.0 + mz[1]) + mz[0]
        h_z = u_z @ w_in[l] if update_ctx else u_z @ w_in[l][:, :KV_COLS]
        kv_z = kv_side(h_z[..., :KV_COLS], g_ckv[l], w_ukv[l], g_kn[l], None)

        u_x = x * (1.0 + mx[:, 1]) + mx[:, 0]
        h_x = u_x @ w_in[l]
        kv_x = kv_side(h_x[..., :KV_COLS], g_ckv[l], w_ukv[l], g_kn[l], ropes)
        kv_all = tuple(jnp.concatenate([a, b], axis=1) for a, b in zip(kv_z, kv_x))
        y_x = mixer_out(h_x, kv_all, g_cq[l], w_uq[l], g_qn[l], w_conv[l], w_o[l], ropes)
        x = layer_norm(ALPHA * x + mx[:, 2] * y_x, ln1_g[l], ln1_b[l])
        y_x = sq_relu_mlp(x * (1.0 + mx[:, 4]) + mx[:, 3], w_mlp1[l], w_mlp2[l])
        x = layer_norm(ALPHA * x + mx[:, 5] * y_x, ln2_g[l], ln2_b[l])

        if update_ctx:
            y_z = mixer_out(h_z, kv_z, g_cq[l], w_uq[l], g_qn[l], w_conv[l], w_o[l], None)
            z = layer_norm(ALPHA * z + mz[2] * y_z, ln1_g[l], ln1_b[l])
            y_z = sq_relu_mlp(z * (1.0 + mz[4]) + mz[3], w_mlp1[l], w_mlp2[l])
            z = layer_norm(ALPHA * z + mz[5] * y_z, ln2_g[l], ln2_b[l])
    return x


_drawn_inputs = setup_inputs


def setup_inputs(seed=0):
    import zlib

    import numpy as np

    out = dict(_drawn_inputs(seed))
    spreads = {}
    factors = {'ctx': 8.0,
     'c_ctx': 8.0,
     'b_ada': 6.302,
     'g_cq': 8.0,
     'w_uq': 7.373,
     'g_ckv': 8.0,
     'g_qn': 8.0,
     'g_kn': 8.0,
     'ln1_b': 2.875,
     'ln2_b': 2.957}
    for name, (base, spread) in spreads.items():
        noise = np.random.default_rng([zlib.crc32(name.encode()), seed]).standard_normal(out[name].shape)
        drawn = base * np.exp(spread * noise) if base else spread * noise
        out[name] = __import__('jax').numpy.asarray(drawn.astype(out[name].dtype))
    for name, factor in factors.items():
        out[name] = (out[name] * factor).astype(out[name].dtype)
    return out
```

```python
from contextlib import ExitStack

import numpy as np
import concourse.bass as bass
from concourse import mybir

F32 = mybir.dt.float32
F32R = mybir.dt.float32r
ACT = mybir.ActivationFunctionType
ALU = mybir.AluOpType
AX = mybir.AxisListType

P = 128
D = 1024
T = 2048
CTX = 256
KEYS = CTX + T
KD = D // P
TT = T // P
CT = CTX // P
KT = KEYS // P
HM = 6
HG = 6
HKV = 2
DH = 64
NOPE, ROPE = 64, 32
QK = NOPE + ROPE
QR, KVR = 256, 128
CW = 256
FF = 4 * D
EPS = 1e-6
ALPHA = 2.0 ** 0.25
O_KPE, O_GV, O_CKV, O_GK, O_GQ, O_CQ, O_CH, O_CB, O_CC = 0, 32, 160, 288, 416, 800, 1056, 1312, 1568
NCOL = O_CC + CW
BANKS = [(0, 416), (416, 384), (800, 512), (1312, 512)]
NORM = NCOL - 3 * CW - O_CKV
QB = 512
NQB = T // QB


class Shared:
    pass


def need(eng, sem, value):
    if not isinstance(value, int) or value > 0:
        eng.wait_ge(sem, value)


def stage_modulate(nc, g, a):
    with ExitStack() as ctx:
        sb = lambda n, s, d=F32: ctx.enter_context(nc.sbuf_tensor(n, s, d))
        sem = lambda n: ctx.enter_context(nc.semaphore(n))
        SLOTS = 8
        w = sb("ada_w", [P, SLOTS, KD, P])
        cond = sb("cond", [P, KD * 2])
        en = sb("cond_e", [P, KD * 2])
        ps = ctx.enter_context(nc.psum_tensor("ada_ps", [P, 512], F32))
        cond_in, const_in, e_done, silu_step = sem("m_cond_in"), sem("m_const_in"), sem("m_e"), sem("m_silu_step")
        w_in = [sem(f"m_w_in{s}") for s in range(SLOTS)]
        w_used, biased = sem("m_w_used"), sem("m_biased")
        ident_set = sem("m_ident")
        block = ctx.enter_context(nc.Block())

        @block.sync
        def _(sp):
            sp.dma_start(cond[:, :], a["cond"]).then_inc(cond_in, 16)
            sp.dma_start(g.b_ada[:, :], a["b_ada"]).then_inc(const_in, 16)
            sp.dma_start(g.gcol[:, :], a["gcol"]).then_inc(const_in, 16)
            for m in range(2 * SLOTS):
                s = m % SLOTS
                if m >= SLOTS:
                    sp.wait_ge(w_used, m - SLOTS + 1)
                sp.dma_start(w[:, s], a["w_ada"][:, m * P:(m + 1) * P].rearrange("(k p) c -> p k c", p=P)).then_inc(w_in[s], 16)
            sp.wait_ge(const_in, 32)

        @block.gpsimd
        def _(pool):
            nc.gpsimd.memset(g.ident[:, :], 0.0).then_inc(ident_set, 1)
            nc.gpsimd.memset(g.ones[:, :], 1.0).then_inc(ident_set, 1)
            pool.wait_ge(ident_set, 2)
            nc.gpsimd.affine_select(out=g.ident[:, :], in_=g.ident[:, :], compare_op=ALU.not_equal, fill=1.0,
                                    base=0, pattern=[[-1, P]], channel_multiplier=1).then_inc(ident_set, 1)

        @block.scalar
        def _(act):
            act.wait_ge(cond_in, 16)
            nc.scalar.activation(en[:, :], cond[:, :], ACT.Exp, scale=-1.0).then_inc(e_done, 1)
            act.wait_ge(ident_set, 3)
            nc.scalar.activation(g.ident_r[:, :], g.ident[:, :], ACT.Copy).then_inc(e_done, 1)

        @block.vector
        def _(dve):
            dve.wait_ge(e_done, 1)
            nc.vector.tensor_scalar(en[:, :], en[:, :], 1.0, None, ALU.add).then_inc(silu_step, 1)
            dve.wait_ge(silu_step, 1)
            nc.vector.reciprocal(en[:, :], en[:, :]).then_inc(silu_step, 1)
            dve.wait_ge(silu_step, 2)
            nc.vector.tensor_tensor(g.cond[:, :], cond[:, :], en[:, :], ALU.mult).then_inc(silu_step, 1)
            dve.wait_ge(const_in, 32)
            dve.wait_ge(w_used, 2 * SLOTS)
            nc.vector.tensor_tensor(g.mods[:, 0:16, :], ps[:, 0:32].rearrange("p (m c) -> p m c", c=2),
                                    g.b_ada[:, 0:16, None].to_broadcast([P, 16, 2]), ALU.add).then_inc(biased, 1)
            dve.wait_ge(biased, 1)
            nc.vector.tensor_scalar(g.mods[:, 8:16, :], g.mods[:, 8:16, :], 1.0, None, ALU.add).then_inc(biased, 1)

        @block.tensor
        def _(pe):
            pe.wait_ge(silu_step, 3)
            for m in range(2 * SLOTS):
                pe.wait_ge(w_in[m % SLOTS], 16 * (m // SLOTS + 1))
                for k in range(KD):
                    mm = nc.tensor.matmul(ps[:, 2 * m:2 * m + 2], w[:, m % SLOTS, k], g.cond[:, 2 * k:2 * k + 2],
                                          start=(k == 0), stop=(k == KD - 1))
                mm.then_inc(w_used, 1)



def stage_project(nc, g, a):
    with ExitStack() as ctx:
        sb = lambda n, s, d=F32: ctx.enter_context(nc.sbuf_tensor(n, s, d))
        ps = lambda n, s: ctx.enter_context(nc.psum_tensor(n, s, F32))
        sem = lambda n: ctx.enter_context(nc.semaphore("p_" + n))
        w_hi, w_lo = sb("win_hi", [P, KD, NCOL], F32R), sb("win_lo", [P, KD, NCOL], F32R)
        xt = [sb(f"xt{i}", [P, KD, P]) for i in range(2)]
        u_hi = [sb(f"u_hi{i}", [P, KD, P], F32R) for i in range(2)]
        u_lo = [sb(f"u_lo{i}", [P, KD, P], F32R) for i in range(2)]
        h = [sb(f"h{i}", [P, NCOL]) for i in range(2)]
        sq = sb("sq", [P, NORM])
        g_row = sb("g_row", [P, 8 * DH])
        cs = sb("cs", [P, TT, 96])
        rt = sb("rope_t", [P, 4, 256])
        kpt = sb("kpe_t", [P, 4, 16])
        rot = sb("rot", [P, 8 * DH])
        kper = sb("kper", [P, ROPE])
        conv_p = sb("conv_p", [P, CW])
        ss, var, rstd, tmp = (sb(n, [P, 10]) for n in ("ss", "var", "rstd", "ntmp"))
        inv_n = sb("inv_n", [P, 10])
        a_hi, a_lo = sb("a_hi", [P, 3, P], F32R), sb("a_lo", [P, 3, P], F32R)
        b_hi, b_lo = sb("b_hi", [P, 4, P], F32R), sb("b_lo", [P, 4, P], F32R)
        c_st = sb("c_st", [P, 4, P])
        k_hi, k_lo = sb("k_hi", [ROPE, P], F32R), sb("k_lo", [ROPE, P], F32R)
        v_st = sb("v_st", [P, 2, P], F32R)
        main = ps("p_main", [P, 4, 512])
        tr_a, tr_b, tr_c, tr_k = (ps(n, [P, 512]) for n in ("tr_a", "tr_b", "tr_c", "tr_k"))

        wraw_in = [sem(f"wraw_in{s}") for s in range(2)]
        w_hi_set, w_lo_set, tables_in = sem("w_hi"), sem("w_lo"), sem("tables_in")
        x_in = [sem(f"x_in{s}") for s in range(2)]
        modulated, uhi_set, ulo_set = sem("modulated"), sem("uhi"), sem("ulo")
        bank_done, bank_out = sem("bank_done"), sem("bank_out")
        squared, var_set, std_set, step = sem("squared"), sem("var_set"), sem("std_set"), sem("dve_step")
        normed, rotated, pool_step, pool_done = sem("normed"), sem("rotated"), sem("pool_step"), sem("pool_done")
        turned, hi_out, lo_out, stored = sem("turned"), sem("hi_out"), sem("lo_out"), sem("stored")
        v_hi_set, v_lo_set = sem("v_hi"), sem("v_lo")
        block = ctx.enter_context(nc.Block())

        STORES_C, STORES_X = 7, 13
        STEPS_C, STEPS_X = 9, 11

        def before(n, per_ctx, per_x):
            if isinstance(n, int) and n < CT:
                return per_ctx * n
            return (n - CT) * per_x + per_ctx * CT

        banks_before = lambda n: before(n, 1, len(BANKS))
        stores_before = lambda n: before(n, 16 * STORES_C, 16 * STORES_X)

        def schedule(eng, split, work, out):
            for n in range(CT):
                split(n, n, n // 2)
                work(n, n, False)
                out(n, n, False)
            split(CT, CT, CT // 2)

            def step(i, c):
                n = i * 2 + c
                if c < CT + TT - 1:
                    split(n + 1, c + 1, i + (c + 1) // 2)
                work(n, c, True)
                if c > CT:
                    out(n - 1, c - 1, True)
            step(0, CT)
            with eng.Fori(0, (TT - 2) // 2) as i:
                step(i, CT + 1)
                step(i, CT + 2)
            step(0, CT + TT - 1)
            out(CT + TT - 1, CT + TT - 1, True)

        @block.sync
        def _(sp):
            sp.dma_start(g_row[:, :], a["g_heads"]).then_inc(tables_in, 16)
            sp.dma_start(inv_n[:, :], a["inv_n"]).then_inc(tables_in, 16)
            sp.dma_start(cs[:, :, :], a["cs_tok"]).then_inc(tables_in, 16)
            for n in range(CT):
                sp.dma_start(xt[n][:, :, :], a["ctx_t"][n]).then_inc(x_in[n], 16)
            for k in range(KD):
                need(sp, w_lo_set, k - 1)
                sp.dma_start(h[k % 2][:, :], a["w_in"][k * P:(k + 1) * P, :]).then_inc(wraw_in[k % 2], 16)

            def load(n, c):
                sp.wait_ge(ulo_set, n - 1)
                s = c % 2
                sp.dma_start(xt[s][:, :, :], a["x_t"][bass.ds(n - CT, 1)].rearrange("o p k t -> p (o k) t")).then_inc(x_in[s], 16)

            def store(n, is_x):
                sp.wait_ge(hi_out, n + 1)
                sp.wait_ge(lo_out, n + 1)
                sp.wait_ge(v_lo_set, n + 1)
                raw = lambda t: t.bitcast(F32)
                tok = bass.ds(n * P, P)
                for part, (ta, tb, tk) in enumerate(((a_hi, b_hi, k_hi), (a_lo, b_lo, k_lo))):
                    sp.dma_start(g.ckv[part][:, tok], raw(ta[:, 0])).then_inc(stored, 16)
                    sp.dma_start(g.kg[part][:, tok], raw(tb[:, 0])).then_inc(stored, 16)
                    sp.dma_start(g.kpe[part][:, tok], raw(tk[:, :])).then_inc(stored, 16)
                sp.dma_start(g.vg[:, bass.ds(n, 1)].rearrange("p o a c -> p (o a) c"), raw(v_st[:, :, :])).then_inc(stored, 16)
                if is_x:
                    q = bass.ds((n - CT) * P, P)
                    for part, (ta, tb) in enumerate(((a_hi, b_hi), (a_lo, b_lo))):
                        sp.dma_start(g.cq[part][:, :, q].rearrange("c p t -> p c t"), raw(ta[:, 1:3])).then_inc(stored, 16)
                        sp.dma_start(g.qg[part][:, q].rearrange("(c p) t -> p c t", p=P), raw(tb[:, 1:4])).then_inc(stored, 16)
                    sp.dma_start(g.conv_p[:, :, q].rearrange("c p t -> p c t"), c_st[:, 0:2]).then_inc(stored, 16)
                    sp.dma_start(g.conv_b[:, :, q].rearrange("c p t -> p c t"), c_st[:, 2:4]).then_inc(stored, 16)

            for n in range(CT):
                store(n, False)
                load(n + CT, n + CT)

            def step(i, c):
                n = i * 2 + c
                if c < CT + TT - 2:
                    load(n + 2, c)
                if c > CT:
                    store(n - 1, True)
            step(0, CT)
            with sp.Fori(0, (TT - 4) // 2) as i:
                step(i, CT + 1)
                step(i, CT + 2)
            for c in range(CT + TT - 3, CT + TT):
                step(0, c)
            store(CT + TT - 1, True)
            sp.wait_ge(stored, stores_before(CT + TT))

        @block.scalar
        def _(act):
            for k in range(KD):
                act.wait_ge(wraw_in[k % 2], 16 * (k // 2 + 1))
                nc.scalar.activation(w_hi[:, k], h[k % 2][:, :], ACT.Copy).then_inc(w_hi_set, 1)
            act.wait_ge(w_lo_set, KD)

            def split(n, c, pair):
                act.wait_ge(modulated, n + 1)
                need(act, bank_done, banks_before(n - 1))
                nc.scalar.activation(u_hi[c % 2][:, :, :], xt[c % 2][:, :, :], ACT.Copy).then_inc(uhi_set, 1)

            def work(n, c, is_x):
                at, hs = banks_before(n), h[c % 2]
                banks = len(BANKS) if is_x else 1
                need(act, turned, n - 1)
                need(act, v_lo_set, n - 1)
                for b in range(banks):
                    act.wait_ge(bank_done, at + (b + 1))
                    c0, cn = BANKS[b]
                    nc.scalar.activation(hs[:, c0:c0 + cn], main[:, b, 0:cn], ACT.Copy).then_inc(bank_out, 1)
                act.wait_ge(bank_out, at + banks)
                need(act, var_set, n)
                width = NORM if is_x else KVR + HKV * DH
                nc.scalar.activation(sq[:, 0:width], hs[:, O_CKV:O_CKV + width], ACT.Square).then_inc(squared, 1)
                act.wait_ge(var_set, n + 1)
                nc.scalar.activation(rstd[:, :], var[:, :], ACT.Sqrt).then_inc(std_set, 1)

            def out(n, c, is_x):
                act.wait_ge(turned, n + 1)
                need(act, stored, stores_before(n))
                for q in range(3 if is_x else 1):
                    nc.scalar.activation(a_hi[:, q], tr_a[:, q * P:(q + 1) * P], ACT.Copy, scale=g.gcol[:, q:q + 1])
                nb = 4 if is_x else 1
                nc.scalar.activation(b_hi[:, 0:nb], tr_b[:, 0:nb * P].rearrange("p (c t) -> p c t", t=P), ACT.Copy)
                if is_x:
                    nc.scalar.activation(c_st[:, :], tr_c[:, :].rearrange("p (c t) -> p c t", t=P), ACT.Copy)
                nc.scalar.activation(k_hi[:, :], tr_k[0:ROPE, 0:P], ACT.Copy).then_inc(hi_out, 1)
                nc.scalar.activation(v_st[:, 0, :], h[c % 2][:, O_GV:O_GV + P], ACT.Copy).then_inc(v_hi_set, 1)
            schedule(act, split, work, out)

        @block.vector
        def _(dve):
            for k in range(KD):
                dve.wait_ge(w_hi_set, k + 1)
                nc.vector.tensor_tensor(w_lo[:, k], h[k % 2][:, :], w_hi[:, k], ALU.subtract).then_inc(w_lo_set, 1)
            nc.vector.memset(ss[:, :], 1.0).then_inc(normed, 1)
            dve.wait_ge(tables_in, 48)
            dve.wait_ge(normed, 1)

            def split(n, c, pair):
                s, who = c % 2, 1 if c < CT else 0
                dve.wait_ge(x_in[s], pair * 16 + 16)
                for k in range(KD):
                    last = nc.vector.tensor_scalar(xt[s][:, k], xt[s][:, k], g.mods[:, 8 + k, who:who + 1],
                                                   g.mods[:, k, who:who + 1], ALU.mult, ALU.add)
                last.then_inc(modulated, 1)

            def work(n, c, is_x):
                at, seen = before(n, STEPS_C, STEPS_X), [0]

                def link(ins):
                    seen[0] += 1
                    ins.then_inc(step, 1)
                    dve.wait_ge(step, at + seen[0])
                hs, heads = h[c % 2], 8 if is_x else HKV
                by_head = lambda t: t.rearrange("p (h d) -> p h d", d=DH)
                dve.wait_ge(squared, n + 1)
                link(nc.vector.reduce_sum(ss[:, 0:1], sq[:, 0:KVR], AX.X))
                link(nc.vector.reduce_sum(ss[:, 1:1 + heads], by_head(sq[:, KVR:KVR + heads * DH]), AX.X))
                if is_x:
                    link(nc.vector.reduce_sum(ss[:, 9:10], sq[:, NORM - QR:NORM], AX.X))
                link(nc.vector.tensor_tensor(tmp[:, :], ss[:, :], inv_n[:, :], ALU.mult))
                nc.vector.tensor_scalar(var[:, :], tmp[:, :], EPS, None, ALU.add).then_inc(var_set, 1)
                dve.wait_ge(std_set, n + 1)
                link(nc.vector.reciprocal(rstd[:, :], rstd[:, :]))
                link(nc.vector.tensor_tensor(tmp[:, :], rstd[:, :], rstd[:, :], ALU.mult))
                link(nc.vector.tensor_tensor(tmp[:, :], tmp[:, :], var[:, :], ALU.mult))
                link(nc.vector.tensor_scalar(tmp[:, :], tmp[:, :], -0.5, 1.5, ALU.mult, ALU.add))
                link(nc.vector.tensor_tensor(rstd[:, :], rstd[:, :], tmp[:, :], ALU.mult))
                ghs = hs[:, O_GK:O_GK + heads * DH]
                link(nc.vector.tensor_tensor(by_head(ghs), by_head(ghs), rstd[:, 1:1 + heads, None].to_broadcast([P, heads, DH]), ALU.mult))
                ckv, cq = hs[:, O_CKV:O_CKV + KVR], hs[:, O_CQ:O_CQ + QR]
                nc.vector.tensor_scalar(ckv, ckv, rstd[:, 0:1], None, ALU.mult)
                need(dve, turned, n)
                if not is_x:
                    nc.vector.tensor_tensor(rot[:, 0:heads * DH], ghs, g_row[:, 0:heads * DH], ALU.mult).then_inc(rotated, 1)
                    assert seen[0] == STEPS_C
                    return
                nc.vector.tensor_scalar(cq, cq, rstd[:, 9:10], None, ALU.mult)
                nc.vector.tensor_tensor(ghs, ghs, g_row[:, :], ALU.mult).then_inc(normed, 1)
                dve.wait_ge(normed, n - CT + 2)
                pairs = ghs.rearrange("p (h f two) -> p h f two", h=8, two=2)
                cos = cs[:, bass.ds(n - CT, 1), 0:32].to_broadcast([P, 8, 32])
                sin = cs[:, bass.ds(n - CT, 1), 32:64].to_broadcast([P, 8, 32])
                part = lambda q: rt[:, q].rearrange("p (h f) -> p h f", h=8)
                nc.vector.tensor_tensor(part(0), pairs[:, :, :, 0], cos, ALU.mult)
                link(nc.vector.tensor_tensor(part(1), pairs[:, :, :, 1], sin, ALU.mult))
                turned_pairs = rot[:, :].rearrange("p (h f two) -> p h f two", h=8, two=2)
                nc.vector.tensor_tensor(turned_pairs[:, :, :, 0], part(0), part(1), ALU.subtract).then_inc(rotated, 1)
                assert seen[0] == STEPS_X

            def out(n, c, is_x):
                dve.wait_ge(hi_out, n + 1)
                for q in range(3 if is_x else 1):
                    nc.vector.scalar_tensor_tensor(out=a_lo[:, q], in0=tr_a[:, q * P:(q + 1) * P], scalar=g.gcol[:, q:q + 1],
                                                   in1=a_hi[:, q], op0=ALU.mult, op1=ALU.subtract)
                nb = 4 if is_x else 1
                nc.vector.tensor_tensor(b_lo[:, 0:nb], tr_b[:, 0:nb * P].rearrange("p (c t) -> p c t", t=P), b_hi[:, 0:nb], ALU.subtract)
                nc.vector.tensor_tensor(k_lo[:, :], tr_k[0:ROPE, 0:P], k_hi[:, :], ALU.subtract).then_inc(lo_out, 1)
            schedule(dve, split, work, out)

        @block.gpsimd
        def _(pool):
            pool.wait_ge(tables_in, 48)

            def split(n, c, pair):
                pool.wait_ge(uhi_set, n + 1)
                nc.gpsimd.tensor_tensor(u_lo[c % 2][:, :, :], xt[c % 2][:, :, :], u_hi[c % 2][:, :, :], ALU.subtract).then_inc(ulo_set, 1)

            def work(n, c, is_x):
                hs = h[c % 2]
                pool.wait_ge(squared, n + 1)
                need(pool, turned, n)
                key = hs[:, O_KPE:O_KPE + ROPE].rearrange("p (f two) -> p f two", two=2)
                if not is_x:
                    nc.gpsimd.tensor_copy(kper[:, 0:16], key[:, :, 0])
                    nc.gpsimd.tensor_copy(kper[:, 16:32], key[:, :, 1]).then_inc(pool_done, 1)
                    return
                nc.gpsimd.tensor_tensor(conv_p[:, :], hs[:, O_CC:O_CC + CW], hs[:, O_CH:O_CH + CW], ALU.mult)
                kcos, ksin = (cs[:, bass.ds(n - CT, 1), f:f + 16].rearrange("p o f -> p (o f)") for f in (64, 80))
                nc.gpsimd.tensor_tensor(kpt[:, 0], key[:, :, 0], kcos, ALU.mult)
                nc.gpsimd.tensor_tensor(kpt[:, 1], key[:, :, 1], ksin, ALU.mult)
                nc.gpsimd.tensor_tensor(kpt[:, 2], key[:, :, 0], ksin, ALU.mult)
                nc.gpsimd.tensor_tensor(kpt[:, 3], key[:, :, 1], kcos, ALU.mult).then_inc(pool_step, 1)
                pool.wait_ge(pool_step, (n - CT) * 2 + 1)
                nc.gpsimd.tensor_tensor(kper[:, 0:16], kpt[:, 0], kpt[:, 1], ALU.subtract)
                nc.gpsimd.tensor_tensor(kper[:, 16:32], kpt[:, 2], kpt[:, 3], ALU.add)
                pool.wait_ge(normed, n - CT + 2)
                pairs = hs[:, O_GK:O_GK + 8 * DH].rearrange("p (h f two) -> p h f two", h=8, two=2)
                cos = cs[:, bass.ds(n - CT, 1), 0:32].to_broadcast([P, 8, 32])
                sin = cs[:, bass.ds(n - CT, 1), 32:64].to_broadcast([P, 8, 32])
                part = lambda q: rt[:, q].rearrange("p (h f) -> p h f", h=8)
                nc.gpsimd.tensor_tensor(part(2), pairs[:, :, :, 0], sin, ALU.mult)
                nc.gpsimd.tensor_tensor(part(3), pairs[:, :, :, 1], cos, ALU.mult).then_inc(pool_step, 1)
                pool.wait_ge(pool_step, (n - CT) * 2 + 2)
                turned_pairs = rot[:, :].rearrange("p (h f two) -> p h f two", h=8, two=2)
                nc.gpsimd.tensor_tensor(turned_pairs[:, :, :, 1], part(2), part(3), ALU.add).then_inc(pool_done, 1)

            def out(n, c, is_x):
                pool.wait_ge(v_hi_set, n + 1)
                nc.gpsimd.tensor_tensor(v_st[:, 1, :], h[c % 2][:, O_GV:O_GV + P], v_st[:, 0, :], ALU.subtract).then_inc(v_lo_set, 1)
            schedule(pool, split, work, out)

        @block.tensor
        def _(pe):
            pe.wait_ge(w_hi_set, KD)
            pe.wait_ge(w_lo_set, KD)

            def split(n, c, pair):
                pass

            def work(n, c, is_x):
                s = c % 2
                pe.wait_ge(uhi_set, n + 1)
                pe.wait_ge(ulo_set, n + 1)
                for b, (c0, cn) in enumerate(BANKS if is_x else BANKS[:1]):
                    if c > CT:
                        pe.wait_ge(bank_out, banks_before(n - 1) + (b + 1))
                    elif b == 0:
                        need(pe, bank_out, c)
                    for k in range(KD):
                        for lhs, rhs in ((u_hi, w_hi), (u_hi, w_lo), (u_lo, w_hi)):
                            mm = nc.tensor.matmul(main[:, b, 0:cn], lhs[s][:, k], rhs[:, k, c0:c0 + cn],
                                                  start=(k == 0 and rhs is w_hi and lhs is u_hi),
                                                  stop=(k == KD - 1 and lhs is u_lo))
                    mm.then_inc(bank_done, 1)

            def out(n, c, is_x):
                hs = h[c % 2]
                pe.wait_ge(rotated, n + 1)
                pe.wait_ge(pool_done, n + 1)
                need(pe, hi_out, n)
                need(pe, lo_out, n)
                turn = lambda ps_, src, m=P: nc.tensor.transpose(ps_, src, g.ident[:, :])
                turn(tr_a[:, 0:P], hs[:, O_CKV:O_CKV + P])
                turn(tr_b[:, 0:P], rot[:, 0:P])
                if is_x:
                    for q in range(2):
                        turn(tr_a[:, (1 + q) * P:(2 + q) * P], hs[:, O_CQ + q * P:O_CQ + (q + 1) * P])
                        turn(tr_c[:, q * P:(q + 1) * P], conv_p[:, q * P:(q + 1) * P])
                        turn(tr_c[:, (2 + q) * P:(3 + q) * P], hs[:, O_CB + q * P:O_CB + (q + 1) * P])
                    for q in range(1, 4):
                        turn(tr_b[:, q * P:(q + 1) * P], rot[:, q * P:(q + 1) * P])
                turn(tr_k[0:ROPE, 0:P], kper[:, :]).then_inc(turned, 1)
            schedule(pe, split, work, out)


def stage_expand(nc, g, a):
    with ExitStack() as ctx:
        sb = lambda n, s, d=F32: ctx.enter_context(nc.sbuf_tensor("e_" + n, s, d))
        ps = lambda n, s: ctx.enter_context(nc.psum_tensor("e_" + n, s, F32))
        sem = lambda n: ctx.enter_context(nc.semaphore("e_" + n))
        UQ, UKV = 640, 768
        ckv_hi, ckv_lo = sb("ckv_hi", [P, KEYS], F32R), sb("ckv_lo", [P, KEYS], F32R)
        cq_hi = [sb(f"cq_hi{i}", [P, 2, QB], F32R) for i in range(2)]
        cq_lo = [sb(f"cq_lo{i}", [P, 2, QB], F32R) for i in range(2)]
        raw_q, raw_kv = sb("raw_q", [P, 2, UQ]), sb("raw_kv", [P, UKV])
        uq_hi, uq_lo = sb("uq_hi", [P, 2, UQ], F32R), sb("uq_lo", [P, 2, UQ], F32R)
        ukv_hi, ukv_lo = sb("ukv_hi", [P, UKV], F32R), sb("ukv_lo", [P, UKV], F32R)
        st_hi, st_lo = sb("st_hi", [P, 3, QB], F32R), sb("st_lo", [P, 3, QB], F32R)
        cs = [sb(f"cs{i}", [6 * 16, 2, QB]) for i in range(2)]
        rt, ro = sb("rt", [6 * 16, 4, QB]), sb("ro", [6 * 16, 2, QB])
        ro_hi, ro_lo = sb("ro_hi", [6 * 16, 2, QB], F32R), sb("ro_lo", [6 * 16, 2, QB], F32R)
        VG = 6
        v_hi, v_lo = sb("v_hi", [P, 2, HM, VG, DH], F32R), sb("v_lo", [P, 2, HM, VG, DH], F32R)
        cp, cb, cy = sb("cp", [P, T + 2]), sb("cb", [P, T]), sb("cy", [P, T])
        c_hi = sb("c_hi", [P, T], F32R)
        SLOTS, M0, M1 = 4, 16, 48
        wa = sb("wa", [P, SLOTS, KD, P])
        ring, rope_ps, v_ps, ada_ps = ps("ring", [P, 3, QB]), ps("rope", [P, 2, QB]), ps("v", [P, 2, QB]), ps("ada", [P, QB])

        w_in, ckv_in, cp_in = sem("w_in"), sem("ckv_in"), sem("cp_in")
        blk_in = [sem(f"blk_in{i}") for i in range(2)]
        wa_in = [sem(f"wa_in{i}") for i in range(SLOTS)]
        w_hi_set, w_lo_set = sem("w_hi_set"), sem("w_lo_set")
        tile_done, hi_set, lo_set = sem("tile_done"), sem("hi_set"), sem("lo_set")
        st_stored = [sem(f"st_stored{i}") for i in range(3)]
        rope_done, rope_mults, rope_set, rope_hi, rope_lo, rope_stored = (sem(n) for n in (
            "rope_done", "rope_mults", "rope_set", "rope_hi", "rope_lo", "rope_stored"))
        v_done, v_hi_set, v_lo_set = sem("v_done"), sem("v_hi_set"), sem("v_lo_set")
        v_stored = [sem(f"v_stored{i}") for i in range(2)]
        edges, conv_step, conv_done, conv_hi, conv_lo, conv_stored = (sem(n) for n in (
            "edges", "conv_step", "conv_done", "conv_hi", "conv_lo", "conv_stored"))
        wa_used, ada_set = sem("wa_used"), sem("ada_set")
        block = ctx.enter_context(nc.Block())
        raw = lambda t: t.bitcast(F32)
        ITEMS = 6
        items_before = lambda b: b * ITEMS + 3

        @block.sync
        def _(sp):
            sp.dma_start(raw_kv[:, :], a["w_ukv"]).then_inc(w_in, 16)
            sp.dma_start(raw_q[:, :, :], a["w_uq"].rearrange("(k p) c -> p k c", p=P)).then_inc(w_in, 16)
            sp.dma_start(raw(ckv_hi[:, :]), g.ckv[0]).then_inc(ckv_in, 16)
            sp.dma_start(raw(ckv_lo[:, :]), g.ckv[1]).then_inc(ckv_in, 16)

            def load(b, s):
                sp.dma_start(raw(cq_hi[s][:, :, :]), g.cq[0][:, :, bass.ds(b * QB, QB)].rearrange("c p t -> p c t")).then_inc(blk_in[s], 16)
                sp.dma_start(raw(cq_lo[s][:, :, :]), g.cq[1][:, :, bass.ds(b * QB, QB)].rearrange("c p t -> p c t")).then_inc(blk_in[s], 16)
                sp.dma_start(cs[s][:, :, :], a["cs_rope"][:, :, bass.ds(b * QB, QB)]).then_inc(blk_in[s], 16)
            load(0, 0)
            load(1, 1)
            sp.dma_start(cp[:, 1:T + 1], g.conv_p[0]).then_inc(cp_in, 16)
            sp.dma_start(cb[:, :], g.conv_b[0]).then_inc(cp_in, 16)

            def store_item(n, r, dst):
                sp.wait_ge(lo_set, n + 1)
                width = dst[0].shape[-1]
                for part, t in enumerate((st_hi, st_lo)):
                    sp.dma_start(dst[part], raw(t[:, r, 0:width])).then_inc(st_stored[r], 16)
            for c in range(3):
                store_item(c, c, [g.kn[part][c * P:(c + 1) * P, 0:CTX] for part in range(2)])

            def stores(b):
                for c in range(3):
                    store_item(items_before(b) + c, c, [g.qn[part][c * P:(c + 1) * P, bass.ds(b * QB, QB)] for part in range(2)])
                for c in range(3):
                    store_item(items_before(b) + 3 + c, c, [g.kn[part][c * P:(c + 1) * P, bass.ds(b * QB + CTX, QB)] for part in range(2)])
                sp.wait_ge(rope_lo, b + 1)
                for part, t in enumerate((ro_hi, ro_lo)):
                    sp.dma_start(g.qr[part][:, :, bass.ds(b * QB, QB)].rearrange("s p t -> p s t"), raw(t[:, :, :])).then_inc(rope_stored, 16)
            for b in range(NQB):
                stores(b)
                if b < 2:
                    sp.wait_ge(conv_lo, b + 1)
                    sp.dma_start(g.co[0][b], raw(c_hi[:, :])).then_inc(conv_stored, 16)
                    sp.dma_start(g.co[1][b], cy[:, :]).then_inc(conv_stored, 16)
                if b + 2 < NQB:
                    load(b + 2, b % 2)
                if b == 0:
                    sp.wait_ge(conv_done, 1)
                    sp.dma_start(cp[:, 1:T + 1], g.conv_p[1]).then_inc(cp_in, 16)
                    sp.dma_start(cb[:, :], g.conv_b[1]).then_inc(cp_in, 16)
            for q in range(KT // VG):
                sp.wait_ge(v_lo_set, VG * (q + 1))
                for part, t in enumerate((v_hi, v_lo)):
                    sp.dma_start(g.vm[part][:, :, q * VG:(q + 1) * VG, :].rearrange("h p t v -> p h (t v)"),
                                 raw(t[:, q % 2]).rearrange("p h t v -> p h (t v)")).then_inc(v_stored[q % 2], 16)
            for r in range(3):
                sp.wait_ge(st_stored[r], 32 * (1 + 2 * NQB))
            sp.wait_ge(rope_stored, 32 * NQB)
            sp.wait_ge(v_stored[0], 64)
            sp.wait_ge(v_stored[1], 32)
            sp.wait_ge(conv_stored, 64)

        @block.gpsimd
        def _(pool):
            nc.gpsimd.memset(cp[:, 0:1], 0.0)
            nc.gpsimd.memset(cp[:, T + 1:T + 2], 0.0).then_inc(edges, 1)
            with pool.Fori(0, (M1 - M0) // SLOTS) as i:
                for s in range(SLOTS):
                    pool.wait_ge(wa_used, i * SLOTS + s + 1)
                    pool.dma_start(wa[:, s], a["w_ada"][:, bass.ds(i * (SLOTS * P) + (M0 + s) * P, P)].rearrange("(k p) c -> p k c", p=P)).then_inc(wa_in[s], 16)

        @block.scalar
        def _(act):
            act.wait_ge(w_in, 32)
            nc.scalar.activation(ukv_hi[:, :], raw_kv[:, :], ACT.Copy).then_inc(w_hi_set, 1)
            nc.scalar.activation(uq_hi[:, :, :], raw_q[:, :, :], ACT.Copy).then_inc(w_hi_set, 1)

            def item(n, r, former, width=QB):
                act.wait_ge(tile_done, n + 1)
                need(act, st_stored[r], former)
                nc.scalar.activation(st_hi[:, r, 0:width], ring[:, r, 0:width], ACT.Copy).then_inc(hi_set, 1)
            for c in range(3):
                item(c, c, 0, CTX)

            def blk(b):
                for c in range(6):
                    item(items_before(b) + c, c % 3, b * 64 + 32 * (1 + c // 3))
                act.wait_ge(rope_set, b + 1)
                need(act, rope_stored, b * 32)
                nc.scalar.activation(ro_hi[:, :, :], ro[:, :, :], ACT.Copy).then_inc(rope_hi, 1)
            for b in range(NQB):
                blk(b)
                if b < 2:
                    act.wait_ge(conv_done, b + 1)
                    need(act, conv_stored, 32 * b)
                    nc.scalar.activation(c_hi[:, :], cy[:, :], ACT.Copy).then_inc(conv_hi, 1)
            for t in range(KT):
                act.wait_ge(v_done, t + 1)
                q = t // VG
                if q >= 2:
                    act.wait_ge(v_stored[q % 2], 32 * (q // 2))
                nc.scalar.activation(v_hi[:, q % 2, :, t % VG, :], v_ps[:, t % 2, 0:HM * DH].rearrange("p (h v) -> p h v", v=DH), ACT.Copy).then_inc(v_hi_set, 1)

        @block.vector
        def _(dve):
            dve.wait_ge(w_hi_set, 2)
            nc.vector.tensor_tensor(ukv_lo[:, :], raw_kv[:, :], ukv_hi[:, :], ALU.subtract).then_inc(w_lo_set, 1)
            nc.vector.tensor_tensor(uq_lo[:, :, :], raw_q[:, :, :], uq_hi[:, :, :], ALU.subtract).then_inc(w_lo_set, 1)

            def item(n, r, width=QB):
                dve.wait_ge(hi_set, n + 1)
                nc.vector.tensor_tensor(st_lo[:, r, 0:width], ring[:, r, 0:width], st_hi[:, r, 0:width], ALU.subtract).then_inc(lo_set, 1)
            for c in range(3):
                item(c, c, CTX)

            def blk(b, s):
                for c in range(6):
                    item(items_before(b) + c, c % 3)
                dve.wait_ge(rope_done, b + 1)
                ev, od = rope_ps[0:96, 0, :], rope_ps[0:96, 1, :]
                cos, sin = cs[s][:, 0, :], cs[s][:, 1, :]
                need(dve, rope_lo, b)
                nc.vector.tensor_tensor(rt[:, 0], ev, cos, ALU.mult)
                nc.vector.tensor_tensor(rt[:, 1], od, sin, ALU.mult)
                nc.vector.tensor_tensor(rt[:, 2], ev, sin, ALU.mult)
                nc.vector.tensor_tensor(rt[:, 3], od, cos, ALU.mult).then_inc(rope_mults, 1)
                dve.wait_ge(rope_mults, b + 1)
                nc.vector.tensor_tensor(ro[:, 0], rt[:, 0], rt[:, 1], ALU.subtract)
                nc.vector.tensor_tensor(ro[:, 1], rt[:, 2], rt[:, 3], ALU.add).then_inc(rope_set, 1)
                dve.wait_ge(rope_hi, b + 1)
                nc.vector.tensor_tensor(ro_lo[:, :, :], ro[:, :, :], ro_hi[:, :, :], ALU.subtract).then_inc(rope_lo, 1)
            for b in range(NQB):
                blk(b, b % 2)
                if b < 2:
                    c = b
                    dve.wait_ge(cp_in, 32 * (c + 1))
                    dve.wait_ge(edges, 1)
                    need(dve, conv_stored, 32 * c)
                    tap = lambda q: g.gcol[:, 3 + 3 * c + q:4 + 3 * c + q]
                    nc.vector.tensor_scalar(cy[:, :], cp[:, 0:T], tap(0), None, ALU.mult).then_inc(conv_step, 1)
                    dve.wait_ge(conv_step, 3 * c + 1)
                    nc.vector.scalar_tensor_tensor(out=cy[:, :], in0=cp[:, 1:T + 1], scalar=tap(1), in1=cy[:, :], op0=ALU.mult, op1=ALU.add).then_inc(conv_step, 1)
                    dve.wait_ge(conv_step, 3 * c + 2)
                    nc.vector.scalar_tensor_tensor(out=cy[:, :], in0=cp[:, 2:T + 2], scalar=tap(2), in1=cy[:, :], op0=ALU.mult, op1=ALU.add).then_inc(conv_step, 1)
                    dve.wait_ge(conv_step, 3 * c + 3)
                    nc.vector.tensor_tensor(cy[:, :], cy[:, :], cb[:, :], ALU.mult).then_inc(conv_done, 1)
                    dve.wait_ge(conv_hi, c + 1)
                    nc.vector.tensor_tensor(cy[:, :], cy[:, :], c_hi[:, :], ALU.subtract).then_inc(conv_lo, 1)
            for t in range(KT):
                dve.wait_ge(v_hi_set, t + 1)
                q = t // VG
                nc.vector.tensor_tensor(v_lo[:, q % 2, :, t % VG, :], v_ps[:, t % 2, 0:HM * DH].rearrange("p (h v) -> p h v", v=DH),
                                        v_hi[:, q % 2, :, t % VG, :], ALU.subtract).then_inc(v_lo_set, 1)
            n = M1 - M0
            dve.wait_ge(wa_used, n + SLOTS)
            nc.vector.tensor_tensor(g.mods[:, M0:M1, :], ada_ps[:, 0:2 * n].rearrange("p (m c) -> p m c", c=2),
                                    g.b_ada[:, M0:M1, None].to_broadcast([P, n, 2]), ALU.add).then_inc(ada_set, 1)
            dve.wait_ge(ada_set, 1)
            nc.vector.tensor_scalar(g.mods[:, 32:40, :], g.mods[:, 32:40, :], 1.0, None, ALU.add).then_inc(ada_set, 1)

        @block.tensor
        def _(pe):
            pe.sem_inc(wa_used, SLOTS)
            pe.wait_ge(w_lo_set, 2)
            pe.wait_ge(ckv_in, 32)

            def products(out, parts):
                for q, (sh, sl, mh, ml) in enumerate(parts):
                    for m, (x, y) in enumerate(((sh, mh), (sh, ml), (sl, mh))):
                        mm = nc.tensor.matmul(out, x, y, start=(q == 0 and m == 0), stop=(q == len(parts) - 1 and m == 2))
                return mm

            def k_tile(n, c, col, width):
                need(pe, lo_set, n - 2)
                w = slice(c * P, (c + 1) * P)
                products(ring[:, c, 0:width], [(ukv_hi[:, w], ukv_lo[:, w], ckv_hi[:, bass.ds(col, width)], ckv_lo[:, bass.ds(col, width)])]).then_inc(tile_done, 1)
            for c in range(3):
                k_tile(c, c, 0, CTX)

            def q_parts(s, c0):
                return [(uq_hi[:, k, c0:c0 + P], uq_lo[:, k, c0:c0 + P], cq_hi[s][:, k], cq_lo[s][:, k]) for k in range(2)]

            for b in range(NQB):
                s = b % 2
                pe.wait_ge(blk_in[s], 48 * (b // 2 + 1))
                for c in range(3):
                    pe.wait_ge(lo_set, items_before(b) + c - 2)
                    products(ring[:, c, :], q_parts(s, c * P)).then_inc(tile_done, 1)
                for c in range(3):
                    k_tile(items_before(b) + 3 + c, c, CTX + b * QB, QB)
                need(pe, rope_mults, b)
                products(rope_ps[:, 0, :], q_parts(s, 384))
                products(rope_ps[:, 1, :], q_parts(s, 512)).then_inc(rope_done, 1)
            for t in range(KT):
                need(pe, v_lo_set, t - 1)
                k = slice(t * P, (t + 1) * P)
                products(v_ps[:, t % 2, 0:HM * DH], [(ckv_hi[:, k], ckv_lo[:, k], ukv_hi[:, 384:], ukv_lo[:, 384:])]).then_inc(v_done, 1)
            with pe.Fori(0, (M1 - M0) // SLOTS) as i:
                for s in range(SLOTS):
                    pe.wait_ge(wa_in[s], i * 16 + 16)
                    for k in range(KD):
                        mm = nc.tensor.matmul(ada_ps[:, bass.ds(i * (2 * SLOTS) + 2 * s, 2)], wa[:, s, k], g.cond[:, 2 * k:2 * k + 2],
                                              start=(k == 0), stop=(k == KD - 1))
                    mm.then_inc(wa_used, 1)


def stage_attend(nc, g, a):
    with ExitStack() as ctx:
        sb = lambda n, s, d=F32: ctx.enter_context(nc.sbuf_tensor("a_" + n, s, d))
        ps = lambda n, s: ctx.enter_context(nc.psum_tensor("a_" + n, s, F32))
        sem = lambda n: ctx.enter_context(nc.semaphore("a_" + n))
        STEPS = KT // 2
        HEAD = STEPS * NQB
        BODY = 2 * HEAD
        NB = 2 * NQB
        HEADS = HM
        mk_hi, mk_lo = sb("mk_hi", [QK + 1, KEYS], F32R), sb("mk_lo", [QK, KEYS], F32R)
        mq_hi, mq_lo = sb("mq_hi", [QK + 1, T], F32R), sb("mq_lo", [QK, T], F32R)
        gk_hh, gk_lo = sb("gk_hh", [P, KEYS], F32R), sb("gk_lo", [DH + 1, KEYS], F32R)
        gq_hl, gq_hm = sb("gq_hl", [P, T], F32R), sb("gq_hm", [DH + 1, T], F32R)
        v1 = [sb(f"v1_{i}", [P, KT, P], F32R) for i in range(2)]
        v0 = [sb(f"v0_{i}", [P, KT, P], F32R) for i in range(2)]
        pf = [sb(f"pf{i}", [P, 2 * QB]) for i in range(2)]
        p_hi = [sb(f"p_hi{i}", [P, 2 * QB], F32R) for i in range(3)]
        p_lo = [sb(f"p_lo{i}", [P, 2 * QB], F32R) for i in range(3)]
        o_sb = sb("o_sb", [P, QB])
        o_out = sb("o_out", [P, 4, DH])
        rden = sb("rden", [P, 4])
        mpart, mneg = sb("mpart", [P, 4, 5]), sb("mneg", [P, 4])
        mcol = [sb("mcol_m", [P, 4, P], F32R), sb("mcol_g", [P, 4, P], F32R)]
        sc = [ps(f"sc{i}", [P, 2 * QB]) for i in range(2)]
        mx = [ps(f"mx{i}", [P, QB]) for i in range(2)]
        o_ps, t_ps = ps("o", [P, QB]), ps("t", [P, QB])
        CHUNKS = [(k, min(QB, KEYS - k)) for k in range(0, KEYS, QB)]
        ITEMS = [(s, k) for s in range(4) for k in range(len(CHUNKS))]
        NI = len(ITEMS) + 1
        assert NI % 2 == 1 and BODY % 6 == 0

        consts, zeroed = sem("consts"), sem("zeroed")
        in_m, in_g, kpe_in = sem("in_m"), sem("in_g"), sem("kpe_in")
        scored, exped, hi_set, lo_set, pv_done = sem("scored"), sem("exped"), sem("hi_set"), sem("lo_set"), sem("pv_done")
        mx_done, mx_read, max_set, neg_set, col_set, row_set = (sem(n) for n in ("mx_done", "mx_read", "max_set", "neg_set", "col_set", "row_set"))
        o_copied, o_turned, den_set, o_set, o_stored = (sem(n) for n in ("o_copied", "o_turned", "den_set", "o_set", "o_stored"))
        block = ctx.enter_context(nc.Block())
        raw = lambda t: t.bitcast(F32)
        SCALES = (float(QK) ** -0.5, float(DH) ** -0.5)
        LOADS_M, LOADS_G = 10, 8

        @block.sync
        def _(sp):
            sp.dma_start(raw(mk_hi[NOPE:QK, :]), g.kpe[0]).then_inc(kpe_in, 16)
            sp.dma_start(raw(mk_lo[NOPE:QK, :]), g.kpe[1]).then_inc(kpe_in, 16)

            def load_m(h):
                rows = slice(h * NOPE, (h + 1) * NOPE)
                for part, (k, q, v) in enumerate(((mk_hi, mq_hi, v1[0]), (mk_lo, mq_lo, v0[0]))):
                    sp.dma_start(raw(k[0:NOPE, :]), g.kn[part][rows]).then_inc(in_m, 16)
                    sp.dma_start(raw(q[0:NOPE, :]), g.qn[part][rows]).then_inc(in_m, 16)
                    for r in range(2):
                        sp.dma_start(raw(q[NOPE + 16 * r:NOPE + 16 * (r + 1), :]), g.qr[part][r][h * 16:(h + 1) * 16]).then_inc(in_m, 16)
                    sp.dma_start(raw(v[:, :, 0:DH]), g.vm[part][h]).then_inc(in_m, 16)

            def load_g(h):
                kv = h // (HG // HKV)
                rows, krows = slice(h * DH, (h + 1) * DH), slice(kv * DH, (kv + 1) * DH)
                sp.dma_start(raw(gk_hh[0:DH, :]), g.kg[0][krows]).then_inc(in_g, 16)
                sp.dma_start(raw(gk_hh[DH:P, :]), g.kg[0][krows]).then_inc(in_g, 16)
                sp.dma_start(raw(gk_lo[0:DH, :]), g.kg[1][krows]).then_inc(in_g, 16)
                sp.dma_start(raw(gq_hl[0:DH, :]), g.qg[0][rows]).then_inc(in_g, 16)
                sp.dma_start(raw(gq_hl[DH:P, :]), g.qg[1][rows]).then_inc(in_g, 16)
                sp.dma_start(raw(gq_hm[0:DH, :]), g.qg[0][rows]).then_inc(in_g, 16)
                for part, v in enumerate((v1[1], v0[1])):
                    sp.dma_start(raw(v[:, :, 0:DH]), g.vg[:, :, part, krows]).then_inc(in_g, 16)

            def store(i, nb):
                sp.wait_ge(o_set, i * NB + nb + 1)
                col = (i if nb < NQB else HM + i) * DH
                row = (nb % NQB) * QB
                sp.dma_start(g.mix[row:row + QB, col:col + DH].rearrange("(s p) v -> p s v", p=P), o_out[:, :, :]).then_inc(o_stored, 16)
            sp.sem_inc(o_stored, 16)
            load_m(0)
            load_g(0)
            for i in range(HEADS):
                for nb in range(NQB):
                    store(i, nb)
                sp.wait_ge(pv_done, i * BODY + HEAD)
                load_m((i + 1) % HEADS)
                for nb in range(NQB, NB):
                    store(i, nb)
                if i + 1 < HEADS:
                    load_g(i + 1)
            sp.wait_ge(o_stored, 16 * HEADS * NB + 16)
            sp.wait_ge(in_m, 16 * LOADS_M * (HEADS + 1))

        @block.gpsimd
        def _(pool):
            for i in range(2):
                nc.gpsimd.memset(raw(v1[i][:, :, DH:P]), 1.0)
                nc.gpsimd.memset(raw(v0[i][:, :, DH:P]), 0.0)
                nc.gpsimd.memset(raw(mcol[i][:, :, :]), 0.0).then_inc(zeroed, 1)

        def each_turn(eng, body):
            with eng.Fori(0, HEADS) as i:
                body(i)

        item_no = lambda i, nb, c: i * (NI * NB) + (NI * (nb + 1) + c)
        reads_no = lambda i, nb, c: i * ((NI - 1) * NB) + ((NI - 1) * (nb + 1) + c)
        ITEM_STEPS = [range(3 * t, min(3 * t + 3, NI - 1)) for t in range(7)]
        is_mla = lambda nb: nb % NB < NQB

        @block.scalar
        def _(act):
            def row(i, nb):
                n = item_no(i, nb, NI - 1)
                act.wait_ge(mx_done, n + 1)
                q = slice(((nb + 1) % NQB) * QB, ((nb + 1) % NQB + 1) * QB)
                bank = mx[(NI * (nb + 1) + NI - 1) % 2]
                if is_mla(nb + 1):
                    nc.scalar.activation(mq_hi[QK:QK + 1, q], bank[QK:QK + 1, :], ACT.Copy).then_inc(row_set, 1)
                else:
                    nc.scalar.activation(gq_hm[DH:DH + 1, q], bank[DH:DH + 1, :], ACT.Copy).then_inc(row_set, 1)
            row(0, -1)

            def copy_o(i, nb):
                act.wait_ge(pv_done, i * BODY + STEPS * (nb + 1))
                if nb:
                    act.wait_ge(o_turned, i * NB + nb)
                nc.scalar.activation(o_sb[:, :], o_ps[:, :], ACT.Copy).then_inc(o_copied, 1)

            def body(i):
                for st in range(BODY):
                    nb, kp = divmod(st, STEPS)
                    n = i * BODY + st
                    if kp == 2 and nb:
                        copy_o(i, nb - 1)
                    if kp == 8:
                        row(i, nb)
                    act.wait_ge(scored, n + 1)
                    if st >= 2:
                        act.wait_ge(lo_set, n - 1)
                    nc.scalar.activation(pf[st % 2][:, :], sc[st % 2][:, :], ACT.Exp, scale=SCALES[nb // NQB]).then_inc(exped, 1)
                    act.wait_ge(exped, n + 1)
                    if st >= 3:
                        act.wait_ge(pv_done, n - 2)
                    nc.scalar.activation(p_hi[st % 3][:, :], pf[st % 2][:, :], ACT.Copy).then_inc(hi_set, 1)
                copy_o(i, NB - 1)
            each_turn(act, body)

        @block.vector
        def _(dve):
            nc.vector.memset(raw(mk_hi[QK:QK + 1, :]), 1.0)
            nc.vector.memset(raw(gk_lo[DH:DH + 1, :]), 1.0).then_inc(consts, 1)
            dve.wait_ge(zeroed, 2)
            def read_max(i, nb, c):
                s, k = ITEMS[c]
                dve.wait_ge(mx_done, item_no(i, nb, c) + 1)
                width = CHUNKS[k][1]
                ins = nc.vector.reduce_max(mpart[:, s, k:k + 1], mx[(NI * (nb + 1) + c) % 2][:, 0:width], AX.X)
                ins.then_inc(mx_read, 1)

            def columns(i, nb):
                b = i * NB + nb
                dve.wait_ge(mx_read, reads_no(i, nb, NI - 1))
                nc.vector.reduce_max(mneg[:, :], mpart[:, :, :], AX.X).then_inc(max_set, 1)
                dve.wait_ge(max_set, b + 2)
                col = QK if is_mla(nb + 1) else DH
                nc.vector.tensor_scalar(mcol[0 if is_mla(nb + 1) else 1][:, :, col], mneg[:, :], -1.0, None, ALU.mult).then_inc(col_set, 1)
            for c in range(NI - 1):
                read_max(0, -1, c)
            columns(0, -1)

            def low(i, st):
                n = i * BODY + st
                dve.wait_ge(hi_set, n + 1)
                nc.vector.tensor_tensor(p_lo[st % 3][:, :], pf[st % 2][:, :], p_hi[st % 3][:, :], ALU.subtract).then_inc(lo_set, 1)

            def norm_o(i, nb):
                b = i * NB + nb
                dve.wait_ge(o_turned, b + 1)
                t = t_ps[:, :].rearrange("p (s v) -> p s v", s=4)
                nc.vector.reciprocal(rden[:, :], t[:, :, DH]).then_inc(den_set, 1)
                dve.wait_ge(den_set, b + 1)
                dve.wait_ge(o_stored, b * 16 + 16)
                nc.vector.tensor_tensor(o_out[:, :, :], t[:, :, 0:DH], rden[:, :, None].to_broadcast([P, 4, DH]), ALU.mult).then_inc(o_set, 1)

            def body(i):
                for st in range(BODY):
                    nb, kp = divmod(st, STEPS)
                    its = list(ITEM_STEPS[kp]) if kp < 7 else []
                    for c in its[:2]:
                        read_max(i, nb, c)
                    if st:
                        low(i, st - 1)
                    for c in its[2:]:
                        read_max(i, nb, c)
                    if kp == 6:
                        columns(i, nb)
                    if kp == 4 and nb:
                        norm_o(i, nb - 1)
                low(i, BODY - 1)
                norm_o(i, NB - 1)
            each_turn(dve, body)

        @block.tensor
        def _(pe):
            pe.wait_ge(consts, 1)
            pe.wait_ge(zeroed, 2)
            pe.wait_ge(kpe_in, 32)

            def items(i, nb, cs_):
                q0 = ((nb + 1) % NQB) * QB
                for c in cs_:
                    s, k = ITEMS[c]
                    k0, width = CHUNKS[k]
                    if c >= 2:
                        pe.wait_ge(mx_read, reads_no(i, nb, c - 1))
                    elif c == 0:
                        need(pe, mx_read, reads_no(i, nb, 0) if nb >= 0 else 0)
                    elif nb >= 0:
                        pe.wait_ge(row_set, i * NB + nb + 1)
                    queries = slice(q0 + s * P, q0 + (s + 1) * P)
                    lhs, rhs = (mq_hi[0:QK, queries], mk_hi[0:QK, k0:k0 + width]) if is_mla(nb + 1) else (gq_hl[:, queries], gk_hh[:, k0:k0 + width])
                    nc.tensor.matmul(mx[(NI * (nb + 1) + c) % 2][:, 0:width], lhs, rhs, start=True, stop=True).then_inc(mx_done, 1)

            def lay_row(i, nb):
                pe.wait_ge(mx_read, reads_no(i, nb, NI - 2))
                pe.wait_ge(col_set, i * NB + nb + 2)
                for s in range(4):
                    mm = nc.tensor.matmul(mx[(NI * (nb + 1) + NI - 1) % 2][:, s * P:(s + 1) * P], mcol[0 if is_mla(nb + 1) else 1][:, s], g.ident_r[:, :],
                                          start=True, stop=True)
                mm.then_inc(mx_done, 1)

            def scores(i, st, half):
                nb, kp = divmod(st, STEPS)
                n = i * BODY + st
                if st >= 2 and half == 0:
                    pe.wait_ge(exped, n - 1)
                if kp == 0 and half == 0:
                    pe.wait_ge(row_set, i * NB + nb + 1)
                q = slice((nb % NQB) * QB, (nb % NQB + 1) * QB)
                k = slice((2 * kp + half) * P, (2 * kp + half + 1) * P)
                out = sc[st % 2][:, half * QB:(half + 1) * QB]
                if nb < NQB:
                    ops = ((mk_hi[:, k], mq_hi[:, q]), (mk_hi[0:QK, k], mq_lo[:, q]), (mk_lo[:, k], mq_hi[0:QK, q]))
                else:
                    ops = ((gk_hh[:, k], gq_hl[:, q]), (gk_lo[:, k], gq_hm[:, q]))
                for m, (x, y) in enumerate(ops):
                    mm = nc.tensor.matmul(out, x, y, start=(m == 0), stop=(m == len(ops) - 1))
                if half == 1:
                    mm.then_inc(scored, 1)

            def values(i, st, half):
                nb, kp = divmod(st, STEPS)
                n = i * BODY + st
                if half == 0:
                    pe.wait_ge(lo_set, n + 1)
                if kp == 0 and nb and half == 0:
                    pe.wait_ge(o_copied, i * NB + nb)
                kind = nb // NQB
                kt, cols = 2 * kp + half, slice(half * QB, (half + 1) * QB)
                ops = ((v1[kind][:, kt], p_hi[st % 3][:, cols]), (v1[kind][:, kt], p_lo[st % 3][:, cols]), (v0[kind][:, kt], p_hi[st % 3][:, cols]))
                for m, (x, y) in enumerate(ops):
                    mm = nc.tensor.matmul(o_ps[:, :], x, y, start=(kt == 0 and m == 0), stop=(kt == KT - 1 and m == 2))
                if half == 1:
                    mm.then_inc(pv_done, 1)

            def turn_o(i, nb):
                b = i * NB + nb
                pe.wait_ge(o_copied, b + 1)
                if nb:
                    pe.wait_ge(o_set, b)
                for s in range(4):
                    mm = nc.tensor.transpose(t_ps[:, s * P:(s + 1) * P], o_sb[:, s * P:(s + 1) * P], g.ident[:, :])
                mm.then_inc(o_turned, 1)

            pe.wait_ge(in_m, 16 * LOADS_M)
            items(0, -1, range(NI - 1))
            lay_row(0, -1)

            def body(i):
                for st in range(BODY):
                    nb, kp = divmod(st, STEPS)
                    its = list(ITEM_STEPS[kp]) if kp < 7 else []
                    scores(i, st, 0)
                    if kp == 0 and nb == NQB - 1:
                        pe.wait_ge(in_g, i * (16 * LOADS_G) + 16 * LOADS_G)
                    if kp == 0 and nb == NB - 1:
                        pe.wait_ge(in_m, i * (16 * LOADS_M) + 32 * LOADS_M)
                    items(i, nb, its[:1])
                    scores(i, st, 1)
                    items(i, nb, its[1:2])
                    if kp == 3 and nb:
                        turn_o(i, nb - 1)
                    if st >= 2:
                        values(i, st - 2, 0)
                    items(i, nb, its[2:3])
                    if st >= 2:
                        values(i, st - 2, 1)
                    if kp == 7:
                        lay_row(i, nb)
                for st in (BODY - 2, BODY - 1):
                    for half in range(2):
                        values(i, st, half)
                turn_o(i, NB - 1)
            each_turn(pe, body)


def gate_row(nc, pe, g, ps_pair, m0):
    for k in range(KD):
        mm = nc.tensor.matmul(ps_pair[:, k * P:(k + 1) * P], g.mods[:, m0 + k, 0:1].to_broadcast([P, P]), g.ident[:, :],
                              start=True, stop=True)
    return mm


def stage_mix(nc, g, a):
    with ExitStack() as ctx:
        sb = lambda n, s, d=F32: ctx.enter_context(nc.sbuf_tensor("o_" + n, s, d))
        ps = lambda n, s: ctx.enter_context(nc.psum_tensor("o_" + n, s, F32))
        sem = lambda n: ctx.enter_context(nc.semaphore("o_" + n))
        KO = 2 * HM * DH // P
        wo_hi, wo_lo = sb("wo_hi", [P, KD, D], F32R), sb("wo_lo", [P, KD, D], F32R)
        stage = [sb(f"stage{i}", [P, D]) for i in range(2)]
        mix = [sb(f"mix{i}", [P, KO * P]) for i in range(2)]
        m_hi = [sb(f"m_hi{i}", [P, KD, P], F32R) for i in range(2)]
        m_lo = [sb(f"m_lo{i}", [P, KD, P], F32R) for i in range(2)]
        x = [sb(f"x{i}", [P, D]) for i in range(2)]
        gate, ln_g, ln_b = sb("gate", [P, D]), sb("ln_g", [P, D]), sb("ln_b", [P, D])
        r = [sb(f"r{i}", [P, D]) for i in range(2)]
        x1 = [sb(f"x1{i}", [P, D]) for i in range(2)]
        u = sb("u", [P, KD, P])
        u_hi, u_lo = sb("u_hi", [P, KD, P], F32R), sb("u_lo", [P, KD, P], F32R)
        stats, mv, var, rstd, tmp = sb("stats", [P, 2, 6]), sb("mv", [P, 2]), sb("var", [P, 1]), sb("rstd", [P, 1]), sb("tmp", [P, 1])
        t_mix, y, t_x = ps("t_mix", [P, 2, 512]), ps("y", [P, 2, 512]), ps("t_x", [P, 2, 512])

        rows_in, gate_done, gate_set = sem("rows_in"), sem("gate_done"), sem("gate_set")
        w_in = [sem(f"w_in{i}") for i in range(2)]
        w_hi_set, w_lo_set = sem("w_hi_set"), sem("w_lo_set")
        mix_in = [sem(f"mix_in{i}") for i in range(2)]
        x_in = [sem(f"x_in{i}") for i in range(2)]
        turned, m_hi_set, m_lo_set, y_done, y_read = sem("turned"), sem("m_hi_set"), sem("m_lo_set"), sem("y_done"), sem("y_read")
        step, var_set, std_set, normed, scaled, x1_set = sem("step"), sem("var_set"), sem("std_set"), sem("normed"), sem("scaled"), sem("x1_set")
        x_turned, u_set, u_hi_set, u_lo_set = sem("x_turned"), sem("u_set"), sem("u_hi_set"), sem("u_lo_set")
        x1_stored = [sem(f"x1_stored{i}") for i in range(2)]
        u_stored = sem("u_stored")
        block = ctx.enter_context(nc.Block())
        raw = lambda t: t.bitcast(F32)
        STEPS = 9

        def schedule(eng, first, work, out):
            def step_(i, c):
                t = i * 2 + c
                if c + 1 < TT:
                    first(t + 1, (c + 1) % 2, i + (c + 1) // 2)
                work(t, c % 2, i + c // 2)
                if c > 0:
                    out(t - 1, (c - 1) % 2, i + (c - 1) // 2)
            first(0, 0, 0)
            step_(0, 0)
            with eng.Fori(0, (TT - 2) // 2) as i:
                step_(i, 1)
                step_(i, 2)
            step_(0, TT - 1)
            out(TT - 1, 1, (TT - 1) // 2)

        @block.sync
        def _(sp):
            for row, name in ((ln_g, "ln1_g"), (ln_b, "ln1_b")):
                sp.dma_start(row[:, :], a[name]).then_inc(rows_in, 16)
            for k in range(KD):
                if k >= 2:
                    sp.wait_ge(w_lo_set, k - 1)
                sp.dma_start(stage[k % 2][:, :], a["w_o"][k * P:(k + 1) * P, :]).then_inc(w_in[k % 2], 16)

            def load(t, s, pair):
                if not isinstance(t, int) or t >= 2:
                    sp.wait_ge(y_done, t - 1)
                    sp.wait_ge(y_read, t - 1)
                tok = bass.ds(t * P, P)
                sp.dma_start(mix[s][:, :], g.mix[tok, :]).then_inc(mix_in[s], 16)
                sp.dma_start(x[s][:, :], a["x"][tok, :]).then_inc(x_in[s], 16)
                for part, m in enumerate((m_hi, m_lo)):
                    sp.dma_start(raw(m[s][:, KO:KD]), g.co[part][:, :, tok].rearrange("c p t -> p c t")).then_inc(x_in[s], 16)

            def store(t, s, pair):
                tok = bass.ds(t * P, P)
                sp.wait_ge(u_lo_set, t + 1)
                sp.wait_ge(rows_in, 32)
                sp.dma_start(g.x1[tok, :], x1[s][:, :]).then_inc(x1_stored[s], 16)
                for part, t_ in enumerate((u_hi, u_lo)):
                    sp.dma_start(g.u2[part][:, :, tok].rearrange("k p t -> p k t"), raw(t_[:, :, :])).then_inc(u_stored, 16)
            schedule(sp, load, lambda *_: None, store)
            sp.wait_ge(u_stored, 32 * TT)
            for s in range(2):
                sp.wait_ge(x1_stored[s], 16 * (TT // 2))

        @block.scalar
        def _(act):
            for k in range(KD):
                act.wait_ge(w_in[k % 2], 16 * (k // 2 + 1))
                nc.scalar.activation(wo_hi[:, k], stage[k % 2][:, :], ACT.Copy).then_inc(w_hi_set, 1)

            def first(t, s, pair):
                act.wait_ge(turned, t + 1)
                if not isinstance(t, int) or t >= 2:
                    act.wait_ge(y_done, t - 1)
                nc.scalar.activation(m_hi[s][:, 0:4], t_mix[:, 0, :].rearrange("p (k t) -> p k t", t=P), ACT.Copy)
                nc.scalar.activation(m_hi[s][:, 4:KO], t_mix[:, 1, 0:2 * P].rearrange("p (k t) -> p k t", t=P), ACT.Copy).then_inc(m_hi_set, 1)

            def work(t, s, pair):
                act.wait_ge(var_set, t + 1)
                nc.scalar.activation(rstd[:, :], var[:, :], ACT.Sqrt).then_inc(std_set, 1)

            def out(t, s, pair):
                act.wait_ge(x_turned, t + 1)
                need(act, u_lo_set, t)
                for k in range(KD):
                    last = nc.scalar.activation(u[:, k], t_x[:, k // 4, (k % 4) * P:(k % 4 + 1) * P], ACT.Identity,
                                                scale=g.mods[:, 32 + k, 0:1], bias=g.mods[:, 24 + k, 0:1])
                last.then_inc(u_set, 1)
                act.wait_ge(u_set, t + 1)
                need(act, u_stored, t * 32)
                nc.scalar.activation(u_hi[:, :, :], u[:, :, :], ACT.Copy).then_inc(u_hi_set, 1)
            schedule(act, first, work, out)

        @block.vector
        def _(dve):
            for k in range(KD):
                dve.wait_ge(w_hi_set, k + 1)
                nc.vector.tensor_tensor(wo_lo[:, k], stage[k % 2][:, :], wo_hi[:, k], ALU.subtract).then_inc(w_lo_set, 1)
            dve.wait_ge(gate_done, 1)
            nc.vector.tensor_copy(gate[:, :], t_x[:, :, :].rearrange("p b n -> p (b n)")).then_inc(gate_set, 1)
            dve.wait_ge(gate_set, 1)

            def first(t, s, pair):
                dve.wait_ge(m_hi_set, t + 1)
                nc.vector.tensor_tensor(m_lo[s][:, 0:4], t_mix[:, 0, :].rearrange("p (k t) -> p k t", t=P), m_hi[s][:, 0:4], ALU.subtract)
                nc.vector.tensor_tensor(m_lo[s][:, 4:KO], t_mix[:, 1, 0:2 * P].rearrange("p (k t) -> p k t", t=P), m_hi[s][:, 4:KO],
                                        ALU.subtract).then_inc(m_lo_set, 1)

            def work(t, s, pair):
                seen = [0]

                def link(ins):
                    seen[0] += 1
                    ins.then_inc(step, 1)
                    dve.wait_ge(step, t * STEPS + seen[0])
                dve.wait_ge(y_done, t + 1)
                dve.wait_ge(x_in[s], pair * 48 + 48)
                if not isinstance(t, int) or t >= 2:
                    dve.wait_ge(x1_set, t - 1)
                link(nc.vector.tensor_tensor(r[s][:, :], y[:, :, :].rearrange("p b n -> p (b n)"), gate[:, :], ALU.mult))
                nc.vector.scalar_tensor_tensor(out=r[s][:, :], in0=x[s][:, :], scalar=ALPHA, in1=r[s][:, :], op0=ALU.mult, op1=ALU.add).then_inc(y_read, 1)
                dve.wait_ge(y_read, t + 1)
                for b in range(2):
                    ins = nc.vector.bn_stats(stats[:, b, :], r[s][:, b * 512:(b + 1) * 512])
                link(ins)
                nc.vector.memset(tmp[:, :], 0.0)
                link(nc.vector.bn_aggr(mv[:, :], stats[:, :, :]))
                nc.vector.tensor_scalar(var[:, :], mv[:, 1:2], EPS, None, ALU.add).then_inc(var_set, 1)
                dve.wait_ge(std_set, t + 1)
                link(nc.vector.reciprocal(rstd[:, :], rstd[:, :]))
                link(nc.vector.tensor_tensor(tmp[:, :], rstd[:, :], rstd[:, :], ALU.mult))
                link(nc.vector.tensor_tensor(tmp[:, :], tmp[:, :], var[:, :], ALU.mult))
                link(nc.vector.tensor_scalar(tmp[:, :], tmp[:, :], -0.5, 1.5, ALU.mult, ALU.add))
                link(nc.vector.tensor_tensor(rstd[:, :], rstd[:, :], tmp[:, :], ALU.mult))
                link(nc.vector.tensor_scalar(r[s][:, :], r[s][:, :], mv[:, 0:1], rstd[:, 0:1], ALU.subtract, ALU.mult))
                dve.wait_ge(rows_in, 32)
                if not isinstance(t, int) or t >= 2:
                    dve.wait_ge(x1_stored[s], pair * 16)
                    dve.wait_ge(x_turned, t - 1)
                nc.vector.tensor_tensor(x1[s][:, :], r[s][:, :], ln_g[:, :], ALU.mult).then_inc(normed, 1)
                assert seen[0] == STEPS, seen

            def out(t, s, pair):
                dve.wait_ge(u_hi_set, t + 1)
                nc.vector.tensor_tensor(u_lo[:, :, :], u[:, :, :], u_hi[:, :, :], ALU.subtract).then_inc(u_lo_set, 1)
            schedule(dve, first, work, out)

        @block.gpsimd
        def _(pool):
            pool.wait_ge(rows_in, 32)

            def work(t, s, pair):
                pool.wait_ge(normed, t + 1)
                nc.gpsimd.tensor_tensor(x1[s][:, :], x1[s][:, :], ln_b[:, :], ALU.add).then_inc(x1_set, 1)
            schedule(pool, lambda *_: None, work, lambda *_: None)

        @block.tensor
        def _(pe):
            gate_row(nc, pe, g, t_x[:, :, :].rearrange("p b n -> p (b n)"), 16).then_inc(gate_done, 1)

            def first(t, s, pair):
                pe.wait_ge(mix_in[s], pair * 16 + 16)
                need(pe, m_lo_set, t)
                for k in range(KO):
                    mm = nc.tensor.transpose(t_mix[:, k // 4, (k % 4) * P:(k % 4 + 1) * P], mix[s][:, k * P:(k + 1) * P], g.ident[:, :])
                mm.then_inc(turned, 1)

            def work(t, s, pair):
                pe.wait_ge(w_hi_set, KD)
                pe.wait_ge(w_lo_set, KD)
                pe.wait_ge(m_lo_set, t + 1)
                pe.wait_ge(x_in[s], pair * 48 + 48)
                need(pe, y_read, t)
                for k in range(KD):
                    for n, (x_, w_) in enumerate(((m_hi, wo_hi), (m_hi, wo_lo), (m_lo, wo_hi))):
                        for half in range(2):
                            mm = nc.tensor.matmul(y[:, half, :], x_[s][:, k], w_[:, k, half * 512:(half + 1) * 512],
                                                  start=(k == 0 and n == 0), stop=(k == KD - 1 and n == 2))
                mm.then_inc(y_done, 1)

            def out(t, s, pair):
                pe.wait_ge(x1_set, t + 1)
                pe.wait_ge(gate_set, 1)
                need(pe, u_set, t)
                for k in range(KD):
                    mm = nc.tensor.transpose(t_x[:, k // 4, (k % 4) * P:(k % 4 + 1) * P], x1[s][:, k * P:(k + 1) * P], g.ident[:, :])
                mm.then_inc(x_turned, 1)
            schedule(pe, first, work, out)


def stage_mlp(nc, g, a):
    with ExitStack() as ctx:
        sb = lambda n, s, d=F32: ctx.enter_context(nc.sbuf_tensor("f_" + n, s, d))
        ps = lambda n, s: ctx.enter_context(nc.psum_tensor("f_" + n, s, F32))
        sem = lambda n: ctx.enter_context(nc.semaphore("f_" + n))
        HALF = T // 2
        GF = 512
        NG = FF // GF
        NF = GF // P
        TB = HALF // 512
        YT = HALF // P
        u_hi, u_lo = sb("u_hi", [P, KD, HALF], F32R), sb("u_lo", [P, KD, HALF], F32R)
        yacc = sb("yacc", [P, YT, D])
        w1_hi, w1_lo = sb("w1_hi", [P, KD, GF], F32R), sb("w1_lo", [P, KD, GF], F32R)
        w2_hi, w2_lo = sb("w2_hi", [P, NF, D], F32R), sb("w2_lo", [P, NF, D], F32R)
        h_hi, h_lo = sb("h_hi", [P, NF, HALF], F32R), sb("h_lo", [P, NF, HALF], F32R)
        stage = [sb(f"stage{i}", [P, D]) for i in range(2)]
        rl = [sb(f"relu{i}", [P, 512]) for i in range(2)]
        one = [ps(f"one{i}", [P, 512]) for i in range(4)]
        two = [ps(f"two{i}", [P, 512]) for i in range(4)]

        u_in = sem("u_in")
        st_in = [sem(f"st_in{i}") for i in range(2)]
        w_hi_set, w_lo_set = sem("w_hi_set"), sem("w_lo_set")
        one_done, relu_set, sq_set, h_hi_set, h_lo_set = sem("one_done"), sem("relu_set"), sem("sq_set"), sem("h_hi_set"), sem("h_lo_set")
        two_done, two_read, zeroed, y_stored = sem("two_done"), sem("two_read"), sem("zeroed"), sem("y_stored")
        block = ctx.enter_context(nc.Block())
        raw = lambda t: t.bitcast(F32)
        W1S, W2S = 4, NF
        SL = W1S + W2S
        ONES, TWOS = TB * NF, YT * 2

        def halves(eng, start, w1_of, group, end):
            for hf in range(2):
                start(hf)
                w1_of(hf, 0)
                with eng.Fori(0, NG - 1) as q:
                    group(hf, q, True)
                group(hf, NG - 1, False)
                end(hf)

        no = lambda hf, q: q + hf * NG

        @block.sync
        def _(sp):
            def slice_in(n, s, src):
                sp.wait_ge(w_lo_set, n - 1) if not isinstance(n, int) or n >= 2 else None
                sp.dma_start(stage[s][:, :] if src.shape[0] == P and len(src.shape) == 2 else stage[s][:, :].rearrange("p (k c) -> p k c", k=2), src).then_inc(st_in[s], 16)

            def w1_of(hf, q):
                for j in range(W1S):
                    src = a["w1"][j * 2 * P:(j + 1) * 2 * P, bass.ds(q * GF, GF)].rearrange("(k p) c -> p k c", p=P)
                    slice_in(no(hf, q) * SL + j, j % 2, src)

            def start(hf):
                if hf:
                    sp.wait_ge(one_done, hf * NG * ONES)
                for part, t in enumerate((u_hi, u_lo)):
                    for tb in range(TB):
                        sp.dma_start(raw(t[:, :, tb * 512:(tb + 1) * 512]),
                                     g.u2[part][:, :, hf * HALF + tb * 512:hf * HALF + (tb + 1) * 512].rearrange("k p t -> p k t")).then_inc(u_in, 16)

            def group(hf, q, more):
                for j in range(W2S):
                    slice_in(no(hf, q) * SL + (W1S + j), j % 2, a["w2"][bass.ds(q * GF + j * P, P), :])
                if more:
                    w1_of(hf, q + 1)

            def end(hf):
                sp.wait_ge(two_read, (hf + 1) * NG * TWOS)
                sp.dma_start(g.y[hf * HALF:(hf + 1) * HALF, :].rearrange("(t p) d -> p t d", p=P), yacc[:, :, :]).then_inc(y_stored, 16)
            halves(sp, start, w1_of, group, end)
            sp.wait_ge(y_stored, 32)

        @block.scalar
        def _(act):
            def slice_hi(n, s, pair, dst):
                act.wait_ge(st_in[s], pair * 16 + 16)
                nc.scalar.activation(dst, stage[s][:, :], ACT.Copy).then_inc(w_hi_set, 1)

            def w1_of(hf, q):
                if hf or not isinstance(q, int) or q:
                    act.wait_ge(one_done, no(hf, q) * ONES)
                for j in range(W1S):
                    slice_hi(no(hf, q) * SL + j, j % 2, no(hf, q) * (SL // 2) + j // 2, w1_hi[:, 2 * j:2 * j + 2].rearrange("p k c -> p (k c)"))

            def group(hf, q, more):
                gn = no(hf, q)
                for j in range(W2S):
                    if j == 0:
                        act.wait_ge(one_done, gn * ONES + 1)
                    slice_hi(gn * SL + (W1S + j), j % 2, gn * (SL // 2) + (W1S // 2 + j // 2), w2_hi[:, j])
                    for o in (2 * j, 2 * j + 1):
                        hidden(gn, o)
                if more:
                    w1_of(hf, q + 1)

            def hidden(gn, o):
                tb, f = divmod(o, NF)
                n = gn * ONES + o
                act.wait_ge(one_done, n + 1)
                nc.scalar.activation(rl[o % 2][:, :], one[o % 4][:, :], ACT.Relu).then_inc(relu_set, 1)
                act.wait_ge(sq_set, n + 1)
                nc.scalar.activation(h_hi[:, f, tb * 512:(tb + 1) * 512], rl[o % 2][:, :], ACT.Copy).then_inc(h_hi_set, 1)
            halves(act, lambda hf: None, w1_of, group, lambda hf: None)

        @block.gpsimd
        def _(pool):
            def slice_lo(n, s, hi, lo):
                pool.wait_ge(w_hi_set, n + 1)
                nc.gpsimd.tensor_tensor(lo, stage[s][:, :], hi, ALU.subtract).then_inc(w_lo_set, 1)

            def w1_of(hf, q):
                for j in range(W1S):
                    t = [w[:, 2 * j:2 * j + 2].rearrange("p k c -> p (k c)") for w in (w1_hi, w1_lo)]
                    slice_lo(no(hf, q) * SL + j, j % 2, *t)

            def group(hf, q, more):
                for j in range(W2S):
                    slice_lo(no(hf, q) * SL + (W1S + j), j % 2, w2_hi[:, j], w2_lo[:, j])
                if more:
                    w1_of(hf, q + 1)
            halves(pool, lambda hf: None, w1_of, group, lambda hf: None)

        @block.vector
        def _(dve):
            def start(hf):
                need(dve, y_stored, 16 * hf)
                nc.vector.memset(yacc[:, :, :], 0.0).then_inc(zeroed, 1)
                dve.wait_ge(zeroed, hf + 1)

            def group(hf, q, more):
                gn = no(hf, q)
                for o in range(ONES):
                    tb, f = divmod(o, NF)
                    n = gn * ONES + o
                    dve.wait_ge(relu_set, n + 1)
                    nc.vector.tensor_tensor(rl[o % 2][:, :], rl[o % 2][:, :], rl[o % 2][:, :], ALU.mult).then_inc(sq_set, 1)
                    dve.wait_ge(h_hi_set, n + 1)
                    cols = slice(tb * 512, (tb + 1) * 512)
                    nc.vector.tensor_tensor(h_lo[:, f, cols], rl[o % 2][:, :], h_hi[:, f, cols], ALU.subtract).then_inc(h_lo_set, 1)
                for o in range(TWOS):
                    t, half = divmod(o, 2)
                    dve.wait_ge(two_done, gn * TWOS + (o + 1))
                    acc = yacc[:, t, half * 512:(half + 1) * 512]
                    nc.vector.tensor_tensor(acc, two[o % 4][:, :], acc, ALU.add).then_inc(two_read, 1)
            halves(dve, start, lambda *_: None, group, lambda hf: None)

        @block.tensor
        def _(pe):
            def group(hf, q, more):
                gn = no(hf, q)
                pe.wait_ge(u_in, 64 * (hf + 1))
                pe.wait_ge(w_lo_set, gn * SL + W1S)
                for o in range(ONES):
                    tb, f = divmod(o, NF)
                    cols = slice(tb * 512, (tb + 1) * 512)
                    if o >= 4:
                        pe.wait_ge(relu_set, gn * ONES + (o - 3))
                    for k in range(KD):
                        w = slice(f * P, (f + 1) * P)
                        for n, (x, y) in enumerate(((w1_hi, u_hi), (w1_hi, u_lo), (w1_lo, u_hi))):
                            mm = nc.tensor.matmul(one[o % 4][:, :], x[:, k, w], y[:, k, cols], start=(k == 0 and n == 0), stop=(k == KD - 1 and n == 2))
                    mm.then_inc(one_done, 1)
                pe.wait_ge(w_lo_set, gn * SL + SL)
                for o in range(TWOS):
                    t, half = divmod(o, 2)
                    if t % 4 == 0 and half == 0:
                        pe.wait_ge(h_lo_set, gn * ONES + NF * (t // 4 + 1))
                    if o >= 4:
                        pe.wait_ge(two_read, gn * TWOS + (o - 3))
                    for f in range(NF):
                        tok, cols = slice(t * P, (t + 1) * P), slice(half * 512, (half + 1) * 512)
                        for n, (x, y) in enumerate(((h_hi, w2_hi), (h_hi, w2_lo), (h_lo, w2_hi))):
                            mm = nc.tensor.matmul(two[o % 4][:, :], x[:, f, tok], y[:, f, cols], start=(f == 0 and n == 0), stop=(f == NF - 1 and n == 2))
                    mm.then_inc(two_done, 1)
            halves(pe, lambda hf: None, lambda *_: None, group, lambda hf: None)


def stage_finish(nc, g, a):
    with ExitStack() as ctx:
        sb = lambda n, s, d=F32: ctx.enter_context(nc.sbuf_tensor("z_" + n, s, d))
        sem = lambda n: ctx.enter_context(nc.semaphore("z_" + n))
        N = 4
        y, x = [sb(f"y{i}", [P, D]) for i in range(N)], [sb(f"x{i}", [P, D]) for i in range(N)]
        gate, ln_g, ln_b = sb("gate", [P, D]), sb("ln_g", [P, D]), sb("ln_b", [P, D])
        stats, mv, var, rstd, tmp = sb("stats", [P, 2, 6]), sb("mv", [P, 2]), sb("var", [P, 1]), sb("rstd", [P, 1]), sb("tmp", [P, 1])
        gate_ps = ctx.enter_context(nc.psum_tensor("z_gate_ps", [P, D], F32))
        rows_in, gate_done, gate_set = sem("rows_in"), sem("gate_done"), sem("gate_set")
        tile_in = [sem(f"tile_in{i}") for i in range(N)]
        stored = [sem(f"stored{i}") for i in range(N)]
        step, var_set, std_set, normed, out_set = sem("step"), sem("var_set"), sem("std_set"), sem("normed"), sem("out_set")
        block = ctx.enter_context(nc.Block())
        STEPS = 10

        @block.sync
        def _(sp):
            for row, name in ((ln_g, "ln2_g"), (ln_b, "ln2_b")):
                sp.dma_start(row[:, :], a[name]).then_inc(rows_in, 16)

            def load(t):
                s = t % N
                if t >= N:
                    sp.wait_ge(stored[s], 16 * (t // N))
                sp.dma_start(y[s][:, :], g.y[t * P:(t + 1) * P, :]).then_inc(tile_in[s], 16)
                sp.dma_start(x[s][:, :], g.x1[t * P:(t + 1) * P, :]).then_inc(tile_in[s], 16)
            for t in range(2):
                load(t)
            for t in range(TT):
                if t + 2 < TT:
                    load(t + 2)
                sp.wait_ge(out_set, t + 1)
                sp.dma_start(a["out"][0, t * P:(t + 1) * P, :], y[t % N][:, :]).then_inc(stored[t % N], 16)
            for s in range(N):
                sp.wait_ge(stored[s], 16 * (TT // N))

        @block.tensor
        def _(pe):
            gate_row(nc, pe, g, gate_ps, 40).then_inc(gate_done, 1)

        @block.scalar
        def _(act):
            act.wait_ge(gate_done, 1)
            nc.scalar.activation(gate[:, :], gate_ps[:, :], ACT.Copy).then_inc(gate_set, 1)
            with act.Fori(0, TT) as t:
                act.wait_ge(var_set, t + 1)
                nc.scalar.activation(rstd[:, :], var[:, :], ACT.Sqrt).then_inc(std_set, 1)

        @block.gpsimd
        def _(pool):
            for t in range(TT):
                pool.wait_ge(normed, t + 1)
                nc.gpsimd.tensor_tensor(y[t % N][:, :], y[t % N][:, :], ln_b[:, :], ALU.add).then_inc(out_set, 1)

        @block.vector
        def _(dve):
            dve.wait_ge(gate_set, 1)
            dve.wait_ge(rows_in, 32)

            def tile(i, s):
                t, seen = i * N + s, [0]

                def link(ins):
                    seen[0] += 1
                    ins.then_inc(step, 1)
                    dve.wait_ge(step, t * STEPS + seen[0])
                r = y[s]
                dve.wait_ge(tile_in[s], i * 32 + 32)
                link(nc.vector.tensor_tensor(r[:, :], r[:, :], gate[:, :], ALU.mult))
                link(nc.vector.scalar_tensor_tensor(out=r[:, :], in0=x[s][:, :], scalar=ALPHA, in1=r[:, :], op0=ALU.mult, op1=ALU.add))
                nc.vector.bn_stats(stats[:, 0, :], r[:, 0:512])
                link(nc.vector.bn_stats(stats[:, 1, :], r[:, 512:]))
                nc.vector.memset(tmp[:, :], 0.0)
                link(nc.vector.bn_aggr(mv[:, :], stats[:, :, :]))
                nc.vector.tensor_scalar(var[:, :], mv[:, 1:2], EPS, None, ALU.add).then_inc(var_set, 1)
                dve.wait_ge(std_set, t + 1)
                link(nc.vector.reciprocal(rstd[:, :], rstd[:, :]))
                link(nc.vector.tensor_tensor(tmp[:, :], rstd[:, :], rstd[:, :], ALU.mult))
                link(nc.vector.tensor_tensor(tmp[:, :], tmp[:, :], var[:, :], ALU.mult))
                link(nc.vector.tensor_scalar(tmp[:, :], tmp[:, :], -0.5, 1.5, ALU.mult, ALU.add))
                link(nc.vector.tensor_tensor(rstd[:, :], rstd[:, :], tmp[:, :], ALU.mult))
                link(nc.vector.tensor_scalar(r[:, :], r[:, :], mv[:, 0:1], rstd[:, 0:1], ALU.subtract, ALU.mult))
                nc.vector.tensor_tensor(r[:, :], r[:, :], ln_g[:, :], ALU.mult).then_inc(normed, 1)
                assert seen[0] == STEPS, seen
            with dve.Fori(0, TT // N) as i:
                for s in range(N):
                    tile(i, s)


def make_shared(nc, ctx, a):
    g = Shared()
    sb = lambda n, s, d=F32: ctx.enter_context(nc.sbuf_tensor(n, s, d))
    g.ident, g.ident_r = sb("ident", [P, P]), sb("ident_r", [P, P], F32R)
    g.ones = sb("ones_f", [P, P])
    g.cond = sb("cond_silu", [P, KD * 2])
    g.b_ada = sb("b_ada_c", [P, 48])
    g.mods = sb("mods", [P, 48, 2])
    g.gcol = sb("gcol", [P, 9])
    dram = lambda n, s: nc.dram_tensor(n, s, F32, kind="Internal").ap()
    g.ckv = dram("s_ckv", [2, P, KEYS])
    g.cq = dram("s_cq", [2, 2, P, T])
    g.kg = dram("s_kg", [2, HKV * DH, KEYS])
    g.kpe = dram("s_kpe", [2, ROPE, KEYS])
    g.vg = dram("s_vg", [P, KT, 2, HKV * DH])
    g.qg = dram("s_qg", [2, HG * DH, T])
    g.conv_p, g.conv_b = dram("s_conv_p", [2, P, T]), dram("s_conv_b", [2, P, T])
    g.qn, g.qr = dram("s_qn", [2, HM * NOPE, T]), dram("s_qr", [2, 2, HM * 16, T])
    g.kn = dram("s_kn", [2, HM * NOPE, KEYS])
    g.vm = dram("s_vm", [2, HM, P, KT, DH])
    g.co = dram("s_co", [2, 2, P, T])
    g.mix = dram("s_mix", [T, 2 * HM * DH])
    g.x1, g.u2, g.y = dram("s_x1", [T, D]), dram("s_u2", [2, KD, P, T]), dram("s_y", [T, D])
    return g


STAGES = [stage_modulate, stage_project, stage_expand, stage_attend, stage_mix, stage_mlp, stage_finish]


def build(nc, a, stages=None):
    with ExitStack() as ctx:
        g = make_shared(nc, ctx, a)
        for stage in stages or STAGES:
            stage(nc, g, a)


def rope_tables():
    t = np.arange(T)
    row, col = (t // 64).astype(np.float32), (t % 64).astype(np.float32)
    out = []
    for dim in (DH, ROPE):
        n = dim // 4
        inv = (np.float32(10000.0) ** (-np.arange(n, dtype=np.float32) / np.float32(n))).astype(np.float32)
        ang = np.concatenate([row[:, None] * inv, col[:, None] * inv], axis=-1)
        out += [np.cos(ang).astype(np.float32), np.sin(ang).astype(np.float32)]
    return out


def lay_out(x, c, ctx, c_ctx, w_ada, b_ada, w_in, g_cq, w_uq, g_ckv, w_ukv, g_qn, g_kn,
            w_conv, w_o, ln1_g, ln1_b, w_mlp1, w_mlp2, ln2_g, ln2_b):
    f = lambda t: np.ascontiguousarray(t)
    tiles = lambda t: f(t.reshape(-1, P, KD, P).transpose(0, 3, 2, 1))
    rep = lambda row: f(np.broadcast_to(row, (P, row.size)))
    cg, sg, cr, sr = rope_tables()
    w = w_in[0]
    kv, q = 416, 640
    cols = [w[:, 128:160], w[:, 288:416], w[:, 0:128], w[:, 160:288], w[:, kv + 256:kv + q], w[:, kv:kv + 256], w[:, kv + q:]]
    uq, ukv, pad = w_uq[0].reshape(QR, HM, QK), w_ukv[0].reshape(KVR, HM, 2 * DH), np.zeros((QR, 32), np.float32)
    out = {
        "x_t": tiles(x[0]), "ctx_t": tiles(ctx[0]),
        "cond": f(np.stack([c[0].reshape(KD, P).T, c_ctx.reshape(KD, P).T], axis=2).reshape(P, 2 * KD)),
        "w_ada": f(w_ada[0]), "b_ada": f(b_ada[0].reshape(48, P).T),
        "w_in": f(np.concatenate(cols, axis=1)),
        "gcol": f(np.concatenate([g_ckv[0][:, None], g_cq[0].reshape(2, P).T, w_conv[0].reshape(3, 2, P).transpose(2, 1, 0).reshape(P, 6)], axis=1)),
        "g_heads": rep(np.concatenate([g_kn[0]] * HKV + [g_qn[0]] * HG)),
        "inv_n": rep(np.array([1 / KVR] + [1 / DH] * 8 + [1 / QR], np.float32)),
        "cs_tok": f(np.concatenate([cg, sg, cr, sr], axis=1).reshape(TT, P, 96).transpose(1, 0, 2)),
        "w_uq": f(np.concatenate([uq[:, :, :NOPE].reshape(QR, -1), uq[:, :, NOPE::2].reshape(QR, -1), pad,
                                  uq[:, :, NOPE + 1::2].reshape(QR, -1), pad], axis=1)),
        "w_ukv": f(np.concatenate([ukv[:, :, :NOPE].reshape(KVR, -1), ukv[:, :, NOPE:].reshape(KVR, -1)], axis=1)),
        "x": f(x[0]), "w_o": f(w_o[0]), "w1": f(w_mlp1[0]), "w2": f(w_mlp2[0]),
        "ln1_g": rep(ln1_g[0]), "ln1_b": rep(ln1_b[0]), "ln2_g": rep(ln2_g[0]), "ln2_b": rep(ln2_b[0]),
        "cs_rope": f(np.stack([np.tile(cr.T, (HM, 1)), np.tile(sr.T, (HM, 1))], axis=1)),
    }
    return out


def kernel(**inputs):
    import concourse.bacc as bacc
    from concourse.bass_utils import run_bass_kernel_spmd

    arrays = {f"in_{n}": v for n, v in lay_out(**{k: np.asarray(v) for k, v in inputs.items()}).items()}
    nc = bacc.Bacc("TRN2", target_bir_lowering=False, num_devices=1)
    a = {n[3:]: nc.dram_tensor(n, v.shape, mybir.dt.from_np(v.dtype), kind="ExternalInput").ap() for n, v in arrays.items()}
    a["out"] = nc.dram_tensor("out_0", (1, T, D), F32, kind="ExternalOutput").ap()
    build(nc, a)
    r = run_bass_kernel_spmd(nc, [arrays], core_ids=[0])
    return r.results[0]["out_0"]
```

```python
from contextlib import ExitStack

import numpy as np
import concourse.bass as bass
from concourse import mybir

F32 = mybir.dt.float32
F32R = mybir.dt.float32r
ACT = mybir.ActivationFunctionType
ALU = mybir.AluOpType
AX = mybir.AxisListType

P = 128
D = 1024
T = 2048
CTX = 256
KEYS = CTX + T
KD = D // P
TT = T // P
CT = CTX // P
KT = KEYS // P
HM = 6
HG = 6
HKV = 2
DH = 64
NOPE, ROPE = 64, 32
QK = NOPE + ROPE
QR, KVR = 256, 128
CW = 256
FF = 4 * D
EPS = 1e-6
ALPHA = 2.0 ** 0.25
O_KPE, O_GV, O_CKV, O_GK, O_GQ, O_CQ, O_CH, O_CB, O_CC = 0, 32, 160, 288, 416, 800, 1056, 1312, 1568
NCOL = O_CC + CW
BANKS = [(0, 416), (416, 384), (800, 512), (1312, 512)]
NORM = NCOL - 3 * CW - O_CKV
QB = 512
NQB = T // QB


class Shared:
    pass


def need(eng, sem, value):
    if not isinstance(value, int) or value > 0:
        eng.wait_ge(sem, value)


def stage_modulate(nc, g, a):
    with ExitStack() as ctx:
        sb = lambda n, s, d=F32: ctx.enter_context(nc.sbuf_tensor(n, s, d))
        sem = lambda n: ctx.enter_context(nc.semaphore(n))
        SLOTS = 4
        w = sb("ada_w", [P, SLOTS, KD, 2 * P])
        cond = sb("cond", [P, KD * 2])
        en = sb("cond_e", [P, KD * 2])
        ps = ctx.enter_context(nc.psum_tensor("ada_ps", [P, 512], F32))
        cond_in, const_in, e_done, silu_step = sem("m_cond_in"), sem("m_const_in"), sem("m_e"), sem("m_silu_step")
        w_in = [sem(f"m_w_in{s}") for s in range(SLOTS)]
        w_used, biased = sem("m_w_used"), sem("m_biased")
        ident_set = sem("m_ident")
        block = ctx.enter_context(nc.Block())

        @block.sync
        def _(sp):
            sp.dma_start(cond[:, :], a["cond"]).then_inc(cond_in, 16)
            sp.dma_start(g.b_ada[:, :], a["b_ada"]).then_inc(const_in, 16)
            sp.dma_start(g.gcol[:, :], a["gcol"]).then_inc(const_in, 16)
            for m in range(2 * SLOTS):
                s = m % SLOTS
                if m >= SLOTS:
                    sp.wait_ge(w_used, m - SLOTS + 1)
                sp.dma_start(w[:, s], a["w_ada"][:, 2 * m * P:2 * (m + 1) * P].rearrange("(k p) c -> p k c", p=P)).then_inc(w_in[s], 16)
            sp.wait_ge(const_in, 32)

        @block.gpsimd
        def _(pool):
            nc.gpsimd.memset(g.ident[:, :], 0.0).then_inc(ident_set, 1)
            nc.gpsimd.memset(g.ones[:, :], 1.0).then_inc(ident_set, 1)
            pool.wait_ge(ident_set, 2)
            nc.gpsimd.affine_select(out=g.ident[:, :], in_=g.ident[:, :], compare_op=ALU.not_equal, fill=1.0,
                                    base=0, pattern=[[-1, P]], channel_multiplier=1).then_inc(ident_set, 1)

        @block.scalar
        def _(act):
            act.wait_ge(cond_in, 16)
            nc.scalar.activation(en[:, :], cond[:, :], ACT.Exp, scale=-1.0).then_inc(e_done, 1)
            act.wait_ge(ident_set, 3)
            nc.scalar.activation(g.ident_r[:, :], g.ident[:, :], ACT.Copy).then_inc(e_done, 1)

        @block.vector
        def _(dve):
            dve.wait_ge(e_done, 1)
            nc.vector.tensor_scalar(en[:, :], en[:, :], 1.0, None, ALU.add).then_inc(silu_step, 1)
            dve.wait_ge(silu_step, 1)
            nc.vector.reciprocal(en[:, :], en[:, :]).then_inc(silu_step, 1)
            dve.wait_ge(silu_step, 2)
            nc.vector.tensor_tensor(g.cond[:, :], cond[:, :], en[:, :], ALU.mult).then_inc(silu_step, 1)
            dve.wait_ge(const_in, 32)
            dve.wait_ge(w_used, 2 * SLOTS)
            nc.vector.tensor_tensor(g.mods[:, 0:16, :], ps[:, 0:32].rearrange("p (m c) -> p m c", c=2),
                                    g.b_ada[:, 0:16, None].to_broadcast([P, 16, 2]), ALU.add).then_inc(biased, 1)
            dve.wait_ge(biased, 1)
            nc.vector.tensor_scalar(g.mods[:, 8:16, :], g.mods[:, 8:16, :], 1.0, None, ALU.add).then_inc(biased, 1)

        @block.tensor
        def _(pe):
            pe.wait_ge(silu_step, 3)
            for m in range(2 * SLOTS):
                pe.wait_ge(w_in[m % SLOTS], 16 * (m // SLOTS + 1))
                for c in range(2):
                    for k in range(KD):
                        mm = nc.tensor.matmul(ps[:, 4 * m + 2 * c:4 * m + 2 * c + 2], w[:, m % SLOTS, k, c * P:(c + 1) * P], g.cond[:, 2 * k:2 * k + 2],
                                              start=(k == 0), stop=(k == KD - 1))
                mm.then_inc(w_used, 1)



def stage_project(nc, g, a):
    with ExitStack() as ctx:
        sb = lambda n, s, d=F32: ctx.enter_context(nc.sbuf_tensor(n, s, d))
        ps = lambda n, s: ctx.enter_context(nc.psum_tensor(n, s, F32))
        sem = lambda n: ctx.enter_context(nc.semaphore("p_" + n))
        w_hi, w_lo = sb("win_hi", [P, KD, NCOL], F32R), sb("win_lo", [P, KD, NCOL], F32R)
        xt = [sb(f"xt{i}", [P, KD, P]) for i in range(2)]
        u_hi = [sb(f"u_hi{i}", [P, KD, P], F32R) for i in range(2)]
        u_lo = [sb(f"u_lo{i}", [P, KD, P], F32R) for i in range(2)]
        h = [sb(f"h{i}", [P, NCOL]) for i in range(2)]
        sq = sb("sq", [P, NORM])
        g_row = sb("g_row", [P, 8 * DH])
        cs = sb("cs", [P, TT, 96])
        rt = sb("rope_t", [P, 4, 256])
        kpt = sb("kpe_t", [P, 4, 16])
        rot = sb("rot", [P, 8 * DH])
        kper = sb("kper", [P, ROPE])
        conv_p = sb("conv_p", [P, CW])
        ss, var, rstd, tmp = (sb(n, [P, 10]) for n in ("ss", "var", "rstd", "ntmp"))
        inv_n = sb("inv_n", [P, 10])
        a_hi, a_lo = sb("a_hi", [P, 3, P], F32R), sb("a_lo", [P, 3, P], F32R)
        b_hi, b_lo = sb("b_hi", [P, 4, P], F32R), sb("b_lo", [P, 4, P], F32R)
        c_st = sb("c_st", [P, 4, P])
        k_hi, k_lo = sb("k_hi", [ROPE, P], F32R), sb("k_lo", [ROPE, P], F32R)
        v_st = sb("v_st", [P, 2, P], F32R)
        main = ps("p_main", [P, 4, 512])
        tr_a, tr_b, tr_c, tr_k = (ps(n, [P, 512]) for n in ("tr_a", "tr_b", "tr_c", "tr_k"))

        wraw_in = [sem(f"wraw_in{s}") for s in range(2)]
        w_hi_set, w_lo_set, tables_in = sem("w_hi"), sem("w_lo"), sem("tables_in")
        x_in = [sem(f"x_in{s}") for s in range(2)]
        modulated, uhi_set, ulo_set = sem("modulated"), sem("uhi"), sem("ulo")
        bank_done, bank_out = sem("bank_done"), sem("bank_out")
        squared, var_set, std_set, step = sem("squared"), sem("var_set"), sem("std_set"), sem("dve_step")
        normed, rotated, pool_step, pool_done = sem("normed"), sem("rotated"), sem("pool_step"), sem("pool_done")
        turned, hi_out, lo_out, stored = sem("turned"), sem("hi_out"), sem("lo_out"), sem("stored")
        v_hi_set, v_lo_set = sem("v_hi"), sem("v_lo")
        block = ctx.enter_context(nc.Block())

        STORES_C, STORES_X = 7, 13
        STEPS_C, STEPS_X = 9, 11

        def before(n, per_ctx, per_x):
            if isinstance(n, int) and n < CT:
                return per_ctx * n
            return (n - CT) * per_x + per_ctx * CT

        banks_before = lambda n: before(n, 1, len(BANKS))
        stores_before = lambda n: before(n, 16 * STORES_C, 16 * STORES_X)

        def schedule(eng, split, work, out):
            for n in range(CT):
                split(n, n, n // 2)
                work(n, n, False)
                out(n, n, False)
            split(CT, CT, CT // 2)

            def step(i, c):
                n = i * 2 + c
                if c < CT + TT - 1:
                    split(n + 1, c + 1, i + (c + 1) // 2)
                work(n, c, True)
                if c > CT:
                    out(n - 1, c - 1, True)
            step(0, CT)
            with eng.Fori(0, (TT - 2) // 2) as i:
                step(i, CT + 1)
                step(i, CT + 2)
            step(0, CT + TT - 1)
            out(CT + TT - 1, CT + TT - 1, True)

        @block.sync
        def _(sp):
            sp.dma_start(g_row[:, :], a["g_heads"]).then_inc(tables_in, 16)
            sp.dma_start(inv_n[:, :], a["inv_n"]).then_inc(tables_in, 16)
            sp.dma_start(cs[:, :, :], a["cs_tok"]).then_inc(tables_in, 16)
            for n in range(CT):
                sp.dma_start(xt[n][:, :, :], a["ctx_t"][n]).then_inc(x_in[n], 16)
            for k in range(KD):
                need(sp, w_lo_set, k - 1)
                sp.dma_start(h[k % 2][:, :], a["w_in"][k * P:(k + 1) * P, :]).then_inc(wraw_in[k % 2], 16)

            def load(n, c):
                sp.wait_ge(ulo_set, n - 1)
                s = c % 2
                sp.dma_start(xt[s][:, :, :], a["x_t"][bass.ds(n - CT, 1)].rearrange("o p k t -> p (o k) t")).then_inc(x_in[s], 16)

            def store(n, is_x):
                sp.wait_ge(hi_out, n + 1)
                sp.wait_ge(lo_out, n + 1)
                sp.wait_ge(v_lo_set, n + 1)
                raw = lambda t: t.bitcast(F32)
                tok = bass.ds(n * P, P)
                for part, (ta, tb, tk) in enumerate(((a_hi, b_hi, k_hi), (a_lo, b_lo, k_lo))):
                    sp.dma_start(g.ckv[part][:, tok], raw(ta[:, 0])).then_inc(stored, 16)
                    sp.dma_start(g.kg[part][:, tok], raw(tb[:, 0])).then_inc(stored, 16)
                    sp.dma_start(g.kpe[part][:, tok], raw(tk[:, :])).then_inc(stored, 16)
                sp.dma_start(g.vg[:, bass.ds(n, 1)].rearrange("p o a c -> p (o a) c"), raw(v_st[:, :, :])).then_inc(stored, 16)
                if is_x:
                    q = bass.ds((n - CT) * P, P)
                    for part, (ta, tb) in enumerate(((a_hi, b_hi), (a_lo, b_lo))):
                        sp.dma_start(g.cq[part][:, :, q].rearrange("c p t -> p c t"), raw(ta[:, 1:3])).then_inc(stored, 16)
                        sp.dma_start(g.qg[part][:, q].rearrange("(c p) t -> p c t", p=P), raw(tb[:, 1:4])).then_inc(stored, 16)
                    sp.dma_start(g.conv_p[:, :, q].rearrange("c p t -> p c t"), c_st[:, 0:2]).then_inc(stored, 16)
                    sp.dma_start(g.conv_b[:, :, q].rearrange("c p t -> p c t"), c_st[:, 2:4]).then_inc(stored, 16)

            for n in range(CT):
                store(n, False)
                load(n + CT, n + CT)

            def step(i, c):
                n = i * 2 + c
                if c < CT + TT - 2:
                    load(n + 2, c)
                if c > CT:
                    store(n - 1, True)
            step(0, CT)
            with sp.Fori(0, (TT - 4) // 2) as i:
                step(i, CT + 1)
                step(i, CT + 2)
            for c in range(CT + TT - 3, CT + TT):
                step(0, c)
            store(CT + TT - 1, True)
            sp.wait_ge(stored, stores_before(CT + TT))

        @block.scalar
        def _(act):
            for k in range(KD):
                act.wait_ge(wraw_in[k % 2], 16 * (k // 2 + 1))
                nc.scalar.activation(w_hi[:, k], h[k % 2][:, :], ACT.Copy).then_inc(w_hi_set, 1)
            act.wait_ge(w_lo_set, KD)

            def split(n, c, pair):
                act.wait_ge(modulated, n + 1)
                need(act, bank_done, banks_before(n - 1))
                nc.scalar.activation(u_hi[c % 2][:, :, :], xt[c % 2][:, :, :], ACT.Copy).then_inc(uhi_set, 1)

            def work(n, c, is_x):
                at, hs = banks_before(n), h[c % 2]
                banks = len(BANKS) if is_x else 1
                need(act, turned, n - 1)
                need(act, v_lo_set, n - 1)
                for b in range(banks):
                    act.wait_ge(bank_done, at + (b + 1))
                    c0, cn = BANKS[b]
                    nc.scalar.activation(hs[:, c0:c0 + cn], main[:, b, 0:cn], ACT.Copy).then_inc(bank_out, 1)
                act.wait_ge(bank_out, at + banks)
                need(act, var_set, n)
                width = NORM if is_x else KVR + HKV * DH
                nc.scalar.activation(sq[:, 0:width], hs[:, O_CKV:O_CKV + width], ACT.Square).then_inc(squared, 1)
                act.wait_ge(var_set, n + 1)
                nc.scalar.activation(rstd[:, :], var[:, :], ACT.Sqrt).then_inc(std_set, 1)

            def out(n, c, is_x):
                act.wait_ge(turned, n + 1)
                need(act, stored, stores_before(n))
                for q in range(3 if is_x else 1):
                    nc.scalar.activation(a_hi[:, q], tr_a[:, q * P:(q + 1) * P], ACT.Copy, scale=g.gcol[:, q:q + 1])
                nb = 4 if is_x else 1
                nc.scalar.activation(b_hi[:, 0:nb], tr_b[:, 0:nb * P].rearrange("p (c t) -> p c t", t=P), ACT.Copy)
                if is_x:
                    nc.scalar.activation(c_st[:, :], tr_c[:, :].rearrange("p (c t) -> p c t", t=P), ACT.Copy)
                nc.scalar.activation(k_hi[:, :], tr_k[0:ROPE, 0:P], ACT.Copy).then_inc(hi_out, 1)
                nc.scalar.activation(v_st[:, 0, :], h[c % 2][:, O_GV:O_GV + P], ACT.Copy).then_inc(v_hi_set, 1)
            schedule(act, split, work, out)

        @block.vector
        def _(dve):
            for k in range(KD):
                dve.wait_ge(w_hi_set, k + 1)
                nc.vector.tensor_tensor(w_lo[:, k], h[k % 2][:, :], w_hi[:, k], ALU.subtract).then_inc(w_lo_set, 1)
            nc.vector.memset(ss[:, :], 1.0).then_inc(normed, 1)
            dve.wait_ge(tables_in, 48)
            dve.wait_ge(normed, 1)

            def split(n, c, pair):
                s, who = c % 2, 1 if c < CT else 0
                dve.wait_ge(x_in[s], pair * 16 + 16)
                for k in range(KD):
                    last = nc.vector.tensor_scalar(xt[s][:, k], xt[s][:, k], g.mods[:, 8 + k, who:who + 1],
                                                   g.mods[:, k, who:who + 1], ALU.mult, ALU.add)
                last.then_inc(modulated, 1)

            def work(n, c, is_x):
                at, seen = before(n, STEPS_C, STEPS_X), [0]

                def link(ins):
                    seen[0] += 1
                    ins.then_inc(step, 1)
                    dve.wait_ge(step, at + seen[0])
                hs, heads = h[c % 2], 8 if is_x else HKV
                by_head = lambda t: t.rearrange("p (h d) -> p h d", d=DH)
                dve.wait_ge(squared, n + 1)
                link(nc.vector.reduce_sum(ss[:, 0:1], sq[:, 0:KVR], AX.X))
                link(nc.vector.reduce_sum(ss[:, 1:1 + heads], by_head(sq[:, KVR:KVR + heads * DH]), AX.X))
                if is_x:
                    link(nc.vector.reduce_sum(ss[:, 9:10], sq[:, NORM - QR:NORM], AX.X))
                link(nc.vector.tensor_tensor(tmp[:, :], ss[:, :], inv_n[:, :], ALU.mult))
                nc.vector.tensor_scalar(var[:, :], tmp[:, :], EPS, None, ALU.add).then_inc(var_set, 1)
                dve.wait_ge(std_set, n + 1)
                link(nc.vector.reciprocal(rstd[:, :], rstd[:, :]))
                link(nc.vector.tensor_tensor(tmp[:, :], rstd[:, :], rstd[:, :], ALU.mult))
                link(nc.vector.tensor_tensor(tmp[:, :], tmp[:, :], var[:, :], ALU.mult))
                link(nc.vector.tensor_scalar(tmp[:, :], tmp[:, :], -0.5, 1.5, ALU.mult, ALU.add))
                link(nc.vector.tensor_tensor(rstd[:, :], rstd[:, :], tmp[:, :], ALU.mult))
                ghs = hs[:, O_GK:O_GK + heads * DH]
                link(nc.vector.tensor_tensor(by_head(ghs), by_head(ghs), rstd[:, 1:1 + heads, None].to_broadcast([P, heads, DH]), ALU.mult))
                ckv, cq = hs[:, O_CKV:O_CKV + KVR], hs[:, O_CQ:O_CQ + QR]
                nc.vector.tensor_scalar(ckv, ckv, rstd[:, 0:1], None, ALU.mult)
                need(dve, turned, n)
                if not is_x:
                    nc.vector.tensor_tensor(rot[:, 0:heads * DH], ghs, g_row[:, 0:heads * DH], ALU.mult).then_inc(rotated, 1)
                    assert seen[0] == STEPS_C
                    return
                nc.vector.tensor_scalar(cq, cq, rstd[:, 9:10], None, ALU.mult)
                nc.vector.tensor_tensor(ghs, ghs, g_row[:, :], ALU.mult).then_inc(normed, 1)
                dve.wait_ge(normed, n - CT + 2)
                pairs = ghs.rearrange("p (h f two) -> p h f two", h=8, two=2)
                cos = cs[:, bass.ds(n - CT, 1), 0:32].to_broadcast([P, 8, 32])
                sin = cs[:, bass.ds(n - CT, 1), 32:64].to_broadcast([P, 8, 32])
                part = lambda q: rt[:, q].rearrange("p (h f) -> p h f", h=8)
                nc.vector.tensor_tensor(part(0), pairs[:, :, :, 0], cos, ALU.mult)
                link(nc.vector.tensor_tensor(part(1), pairs[:, :, :, 1], sin, ALU.mult))
                turned_pairs = rot[:, :].rearrange("p (h f two) -> p h f two", h=8, two=2)
                nc.vector.tensor_tensor(turned_pairs[:, :, :, 0], part(0), part(1), ALU.subtract).then_inc(rotated, 1)
                assert seen[0] == STEPS_X

            def out(n, c, is_x):
                dve.wait_ge(hi_out, n + 1)
                for q in range(3 if is_x else 1):
                    nc.vector.scalar_tensor_tensor(out=a_lo[:, q], in0=tr_a[:, q * P:(q + 1) * P], scalar=g.gcol[:, q:q + 1],
                                                   in1=a_hi[:, q], op0=ALU.mult, op1=ALU.subtract)
                nb = 4 if is_x else 1
                nc.vector.tensor_tensor(b_lo[:, 0:nb], tr_b[:, 0:nb * P].rearrange("p (c t) -> p c t", t=P), b_hi[:, 0:nb], ALU.subtract)
                nc.vector.tensor_tensor(k_lo[:, :], tr_k[0:ROPE, 0:P], k_hi[:, :], ALU.subtract).then_inc(lo_out, 1)
            schedule(dve, split, work, out)

        @block.gpsimd
        def _(pool):
            pool.wait_ge(tables_in, 48)

            def split(n, c, pair):
                pool.wait_ge(uhi_set, n + 1)
                nc.gpsimd.tensor_tensor(u_lo[c % 2][:, :, :], xt[c % 2][:, :, :], u_hi[c % 2][:, :, :], ALU.subtract).then_inc(ulo_set, 1)

            def work(n, c, is_x):
                hs = h[c % 2]
                pool.wait_ge(squared, n + 1)
                need(pool, turned, n)
                key = hs[:, O_KPE:O_KPE + ROPE].rearrange("p (f two) -> p f two", two=2)
                if not is_x:
                    nc.gpsimd.tensor_copy(kper[:, 0:16], key[:, :, 0])
                    nc.gpsimd.tensor_copy(kper[:, 16:32], key[:, :, 1]).then_inc(pool_done, 1)
                    return
                nc.gpsimd.tensor_tensor(conv_p[:, :], hs[:, O_CC:O_CC + CW], hs[:, O_CH:O_CH + CW], ALU.mult)
                kcos, ksin = (cs[:, bass.ds(n - CT, 1), f:f + 16].rearrange("p o f -> p (o f)") for f in (64, 80))
                nc.gpsimd.tensor_tensor(kpt[:, 0], key[:, :, 0], kcos, ALU.mult)
                nc.gpsimd.tensor_tensor(kpt[:, 1], key[:, :, 1], ksin, ALU.mult)
                nc.gpsimd.tensor_tensor(kpt[:, 2], key[:, :, 0], ksin, ALU.mult)
                nc.gpsimd.tensor_tensor(kpt[:, 3], key[:, :, 1], kcos, ALU.mult).then_inc(pool_step, 1)
                pool.wait_ge(pool_step, (n - CT) * 2 + 1)
                nc.gpsimd.tensor_tensor(kper[:, 0:16], kpt[:, 0], kpt[:, 1], ALU.subtract)
                nc.gpsimd.tensor_tensor(kper[:, 16:32], kpt[:, 2], kpt[:, 3], ALU.add)
                pool.wait_ge(normed, n - CT + 2)
                pairs = hs[:, O_GK:O_GK + 8 * DH].rearrange("p (h f two) -> p h f two", h=8, two=2)
                cos = cs[:, bass.ds(n - CT, 1), 0:32].to_broadcast([P, 8, 32])
                sin = cs[:, bass.ds(n - CT, 1), 32:64].to_broadcast([P, 8, 32])
                part = lambda q: rt[:, q].rearrange("p (h f) -> p h f", h=8)
                nc.gpsimd.tensor_tensor(part(2), pairs[:, :, :, 0], sin, ALU.mult)
                nc.gpsimd.tensor_tensor(part(3), pairs[:, :, :, 1], cos, ALU.mult).then_inc(pool_step, 1)
                pool.wait_ge(pool_step, (n - CT) * 2 + 2)
                turned_pairs = rot[:, :].rearrange("p (h f two) -> p h f two", h=8, two=2)
                nc.gpsimd.tensor_tensor(turned_pairs[:, :, :, 1], part(2), part(3), ALU.add).then_inc(pool_done, 1)

            def out(n, c, is_x):
                pool.wait_ge(v_hi_set, n + 1)
                nc.gpsimd.tensor_tensor(v_st[:, 1, :], h[c % 2][:, O_GV:O_GV + P], v_st[:, 0, :], ALU.subtract).then_inc(v_lo_set, 1)
            schedule(pool, split, work, out)

        @block.tensor
        def _(pe):
            pe.wait_ge(w_hi_set, KD)
            pe.wait_ge(w_lo_set, KD)

            def split(n, c, pair):
                pass

            def work(n, c, is_x):
                s = c % 2
                pe.wait_ge(uhi_set, n + 1)
                pe.wait_ge(ulo_set, n + 1)
                for b, (c0, cn) in enumerate(BANKS if is_x else BANKS[:1]):
                    if c > CT:
                        pe.wait_ge(bank_out, banks_before(n - 1) + (b + 1))
                    elif b == 0:
                        need(pe, bank_out, c)
                    for k in range(KD):
                        for lhs, rhs in ((u_hi, w_hi), (u_hi, w_lo), (u_lo, w_hi)):
                            mm = nc.tensor.matmul(main[:, b, 0:cn], lhs[s][:, k], rhs[:, k, c0:c0 + cn],
                                                  start=(k == 0 and rhs is w_hi and lhs is u_hi),
                                                  stop=(k == KD - 1 and lhs is u_lo))
                    mm.then_inc(bank_done, 1)

            def out(n, c, is_x):
                hs = h[c % 2]
                pe.wait_ge(rotated, n + 1)
                pe.wait_ge(pool_done, n + 1)
                need(pe, hi_out, n)
                need(pe, lo_out, n)
                turn = lambda ps_, src, m=P: nc.tensor.transpose(ps_, src, g.ident[:, :])
                turn(tr_a[:, 0:P], hs[:, O_CKV:O_CKV + P])
                turn(tr_b[:, 0:P], rot[:, 0:P])
                if is_x:
                    for q in range(2):
                        turn(tr_a[:, (1 + q) * P:(2 + q) * P], hs[:, O_CQ + q * P:O_CQ + (q + 1) * P])
                        turn(tr_c[:, q * P:(q + 1) * P], conv_p[:, q * P:(q + 1) * P])
                        turn(tr_c[:, (2 + q) * P:(3 + q) * P], hs[:, O_CB + q * P:O_CB + (q + 1) * P])
                    for q in range(1, 4):
                        turn(tr_b[:, q * P:(q + 1) * P], rot[:, q * P:(q + 1) * P])
                turn(tr_k[0:ROPE, 0:P], kper[:, :]).then_inc(turned, 1)
            schedule(pe, split, work, out)


def stage_expand(nc, g, a):
    with ExitStack() as ctx:
        sb = lambda n, s, d=F32: ctx.enter_context(nc.sbuf_tensor("e_" + n, s, d))
        ps = lambda n, s: ctx.enter_context(nc.psum_tensor("e_" + n, s, F32))
        sem = lambda n: ctx.enter_context(nc.semaphore("e_" + n))
        UQ, UKV = 640, 768
        ckv_hi, ckv_lo = sb("ckv_hi", [P, KEYS], F32R), sb("ckv_lo", [P, KEYS], F32R)
        cq_hi = [sb(f"cq_hi{i}", [P, 2, QB], F32R) for i in range(2)]
        cq_lo = [sb(f"cq_lo{i}", [P, 2, QB], F32R) for i in range(2)]
        raw_q, raw_kv = sb("raw_q", [P, 2, UQ]), sb("raw_kv", [P, UKV])
        uq_hi, uq_lo = sb("uq_hi", [P, 2, UQ], F32R), sb("uq_lo", [P, 2, UQ], F32R)
        ukv_hi, ukv_lo = sb("ukv_hi", [P, UKV], F32R), sb("ukv_lo", [P, UKV], F32R)
        st_hi, st_lo = sb("st_hi", [P, 3, QB], F32R), sb("st_lo", [P, 3, QB], F32R)
        cs = [sb(f"cs{i}", [6 * 16, 2, QB]) for i in range(2)]
        rt, ro = sb("rt", [6 * 16, 4, QB]), sb("ro", [6 * 16, 2, QB])
        ro_hi, ro_lo = sb("ro_hi", [6 * 16, 2, QB], F32R), sb("ro_lo", [6 * 16, 2, QB], F32R)
        VG = 6
        v_hi, v_lo = sb("v_hi", [P, 2, HM, VG, DH], F32R), sb("v_lo", [P, 2, HM, VG, DH], F32R)
        cp, cb, cy = sb("cp", [P, T + 2]), sb("cb", [P, T]), sb("cy", [P, T])
        c_hi = sb("c_hi", [P, T], F32R)
        M0, M1 = 40, 48
        HALVES = 2
        MH = (M1 - M0) // HALVES
        wa = sb("wa", [P, KD, MH * P])
        ring, rope_ps, v_ps, ada_ps = ps("ring", [P, 3, QB]), ps("rope", [P, 2, QB]), ps("v", [P, 2, QB]), ps("ada", [P, QB])

        w_in, ckv_in, cp_in = sem("w_in"), sem("ckv_in"), sem("cp_in")
        blk_in = [sem(f"blk_in{i}") for i in range(2)]
        wa_in = sem("wa_in")
        w_hi_set, w_lo_set = sem("w_hi_set"), sem("w_lo_set")
        tile_done, hi_set, lo_set = sem("tile_done"), sem("hi_set"), sem("lo_set")
        st_stored = [sem(f"st_stored{i}") for i in range(3)]
        rope_done, rope_mults, rope_set, rope_hi, rope_lo, rope_stored = (sem(n) for n in (
            "rope_done", "rope_mults", "rope_set", "rope_hi", "rope_lo", "rope_stored"))
        v_done, v_hi_set, v_lo_set = sem("v_done"), sem("v_hi_set"), sem("v_lo_set")
        v_stored = [sem(f"v_stored{i}") for i in range(2)]
        conv_step, conv_done, conv_hi, conv_lo, conv_stored = (sem(n) for n in (
            "conv_step", "conv_done", "conv_hi", "conv_lo", "conv_stored"))
        wa_used, ada_set = sem("wa_used"), sem("ada_set")
        block = ctx.enter_context(nc.Block())
        raw = lambda t: t.bitcast(F32)
        ITEMS = 6
        items_before = lambda b: b * ITEMS + 3

        @block.sync
        def _(sp):
            sp.dma_start(raw_kv[:, :], a["w_ukv"]).then_inc(w_in, 16)
            sp.dma_start(raw_q[:, :, :], a["w_uq"].rearrange("(k p) c -> p k c", p=P)).then_inc(w_in, 16)
            sp.dma_start(raw(ckv_hi[:, :]), g.ckv[0]).then_inc(ckv_in, 16)
            sp.dma_start(raw(ckv_lo[:, :]), g.ckv[1]).then_inc(ckv_in, 16)

            def load(b, s):
                sp.dma_start(raw(cq_hi[s][:, :, :]), g.cq[0][:, :, bass.ds(b * QB, QB)].rearrange("c p t -> p c t")).then_inc(blk_in[s], 16)
                sp.dma_start(raw(cq_lo[s][:, :, :]), g.cq[1][:, :, bass.ds(b * QB, QB)].rearrange("c p t -> p c t")).then_inc(blk_in[s], 16)
                sp.dma_start(cs[s][:, :, :], a["cs_rope"][:, :, bass.ds(b * QB, QB)]).then_inc(blk_in[s], 16)
            load(0, 0)
            load(1, 1)
            sp.dma_start(cp[:, 1:T + 1], g.conv_p[0]).then_inc(cp_in, 16)
            sp.dma_start(cb[:, :], g.conv_b[0]).then_inc(cp_in, 16)

            def store_item(n, r, dst):
                sp.wait_ge(lo_set, n + 1)
                width = dst[0].shape[-1]
                for part, t in enumerate((st_hi, st_lo)):
                    sp.dma_start(dst[part], raw(t[:, r, 0:width])).then_inc(st_stored[r], 16)
            for c in range(3):
                store_item(c, c, [g.kn[part][c * P:(c + 1) * P, 0:CTX] for part in range(2)])

            def stores(b):
                for c in range(3):
                    store_item(items_before(b) + c, c, [g.qn[part][c * P:(c + 1) * P, bass.ds(b * QB, QB)] for part in range(2)])
                for c in range(3):
                    store_item(items_before(b) + 3 + c, c, [g.kn[part][c * P:(c + 1) * P, bass.ds(b * QB + CTX, QB)] for part in range(2)])
                sp.wait_ge(rope_lo, b + 1)
                for part, t in enumerate((ro_hi, ro_lo)):
                    sp.dma_start(g.qr[part][:, :, bass.ds(b * QB, QB)].rearrange("s p t -> p s t"), raw(t[:, :, :])).then_inc(rope_stored, 16)
            for b in range(NQB):
                if b < HALVES:
                    need(sp, wa_used, b)
                    sp.dma_start(wa[:, :, :], a["w_ada"][:, (M0 + b * MH) * P:(M0 + (b + 1) * MH) * P].rearrange("(k p) c -> p k c", p=P)).then_inc(wa_in, 16)
                stores(b)
                if b < 2:
                    sp.wait_ge(conv_lo, b + 1)
                    sp.dma_start(g.co[0][b], raw(c_hi[:, :])).then_inc(conv_stored, 16)
                    sp.dma_start(g.co[1][b], cy[:, :]).then_inc(conv_stored, 16)
                if b + 2 < NQB:
                    load(b + 2, b % 2)
                if b == 0:
                    sp.wait_ge(conv_done, 1)
                    sp.dma_start(cp[:, 1:T + 1], g.conv_p[1]).then_inc(cp_in, 16)
                    sp.dma_start(cb[:, :], g.conv_b[1]).then_inc(cp_in, 16)
            for q in range(KT // VG):
                sp.wait_ge(v_lo_set, VG * (q + 1))
                for part, t in enumerate((v_hi, v_lo)):
                    sp.dma_start(g.vm[part][:, :, q * VG:(q + 1) * VG, :].rearrange("h p t v -> p h (t v)"),
                                 raw(t[:, q % 2]).rearrange("p h t v -> p h (t v)")).then_inc(v_stored[q % 2], 16)
            for r in range(3):
                sp.wait_ge(st_stored[r], 32 * (1 + 2 * NQB))
            sp.wait_ge(rope_stored, 32 * NQB)
            sp.wait_ge(v_stored[0], 64)
            sp.wait_ge(v_stored[1], 32)
            sp.wait_ge(conv_stored, 64)

        @block.scalar
        def _(act):
            act.wait_ge(w_in, 32)
            nc.scalar.activation(ukv_hi[:, :], raw_kv[:, :], ACT.Copy).then_inc(w_hi_set, 1)
            nc.scalar.activation(uq_hi[:, :, :], raw_q[:, :, :], ACT.Copy).then_inc(w_hi_set, 1)

            def item(n, r, former, width=QB):
                act.wait_ge(tile_done, n + 1)
                need(act, st_stored[r], former)
                nc.scalar.activation(st_hi[:, r, 0:width], ring[:, r, 0:width], ACT.Copy).then_inc(hi_set, 1)
            for c in range(3):
                item(c, c, 0, CTX)

            def blk(b):
                for c in range(6):
                    item(items_before(b) + c, c % 3, b * 64 + 32 * (1 + c // 3))
                act.wait_ge(rope_set, b + 1)
                need(act, rope_stored, b * 32)
                nc.scalar.activation(ro_hi[:, :, :], ro[:, :, :], ACT.Copy).then_inc(rope_hi, 1)
            for b in range(NQB):
                blk(b)
                if b < 2:
                    act.wait_ge(conv_done, b + 1)
                    need(act, conv_stored, 32 * b)
                    nc.scalar.activation(c_hi[:, :], cy[:, :], ACT.Copy).then_inc(conv_hi, 1)
            for t in range(KT):
                act.wait_ge(v_done, t + 1)
                q = t // VG
                if q >= 2:
                    act.wait_ge(v_stored[q % 2], 32 * (q // 2))
                nc.scalar.activation(v_hi[:, q % 2, :, t % VG, :], v_ps[:, t % 2, 0:HM * DH].rearrange("p (h v) -> p h v", v=DH), ACT.Copy).then_inc(v_hi_set, 1)

        @block.vector
        def _(dve):
            nc.vector.memset(cp[:, 0:1], 0.0)
            nc.vector.memset(cp[:, T + 1:T + 2], 0.0).then_inc(conv_step, 1)
            dve.wait_ge(w_hi_set, 2)
            nc.vector.tensor_tensor(ukv_lo[:, :], raw_kv[:, :], ukv_hi[:, :], ALU.subtract).then_inc(w_lo_set, 1)
            nc.vector.tensor_tensor(uq_lo[:, :, :], raw_q[:, :, :], uq_hi[:, :, :], ALU.subtract).then_inc(w_lo_set, 1)

            def item(n, r, width=QB):
                dve.wait_ge(hi_set, n + 1)
                nc.vector.tensor_tensor(st_lo[:, r, 0:width], ring[:, r, 0:width], st_hi[:, r, 0:width], ALU.subtract).then_inc(lo_set, 1)
            for c in range(3):
                item(c, c, CTX)

            def blk(b, s):
                for c in range(6):
                    item(items_before(b) + c, c % 3)
                dve.wait_ge(rope_done, b + 1)
                ev, od = rope_ps[0:96, 0, :], rope_ps[0:96, 1, :]
                cos, sin = cs[s][:, 0, :], cs[s][:, 1, :]
                need(dve, rope_lo, b)
                nc.vector.tensor_tensor(rt[:, 0], ev, cos, ALU.mult)
                nc.vector.tensor_tensor(rt[:, 1], od, sin, ALU.mult)
                nc.vector.tensor_tensor(rt[:, 2], ev, sin, ALU.mult)
                nc.vector.tensor_tensor(rt[:, 3], od, cos, ALU.mult).then_inc(rope_mults, 1)
                dve.wait_ge(rope_mults, b + 1)
                nc.vector.tensor_tensor(ro[:, 0], rt[:, 0], rt[:, 1], ALU.subtract)
                nc.vector.tensor_tensor(ro[:, 1], rt[:, 2], rt[:, 3], ALU.add).then_inc(rope_set, 1)
                dve.wait_ge(rope_hi, b + 1)
                nc.vector.tensor_tensor(ro_lo[:, :, :], ro[:, :, :], ro_hi[:, :, :], ALU.subtract).then_inc(rope_lo, 1)
            for b in range(NQB):
                blk(b, b % 2)
                if b < 2:
                    c = b
                    dve.wait_ge(cp_in, 32 * (c + 1))
                    dve.wait_ge(conv_step, 1 + 3 * c)
                    need(dve, conv_stored, 32 * c)
                    tap = lambda q: g.gcol[:, 3 + 3 * c + q:4 + 3 * c + q]
                    nc.vector.tensor_scalar(cy[:, :], cp[:, 0:T], tap(0), None, ALU.mult).then_inc(conv_step, 1)
                    dve.wait_ge(conv_step, 3 * c + 2)
                    nc.vector.scalar_tensor_tensor(out=cy[:, :], in0=cp[:, 1:T + 1], scalar=tap(1), in1=cy[:, :], op0=ALU.mult, op1=ALU.add).then_inc(conv_step, 1)
                    dve.wait_ge(conv_step, 3 * c + 3)
                    nc.vector.scalar_tensor_tensor(out=cy[:, :], in0=cp[:, 2:T + 2], scalar=tap(2), in1=cy[:, :], op0=ALU.mult, op1=ALU.add).then_inc(conv_step, 1)
                    dve.wait_ge(conv_step, 3 * c + 4)
                    nc.vector.tensor_tensor(cy[:, :], cy[:, :], cb[:, :], ALU.mult).then_inc(conv_done, 1)
                    dve.wait_ge(conv_hi, c + 1)
                    nc.vector.tensor_tensor(cy[:, :], cy[:, :], c_hi[:, :], ALU.subtract).then_inc(conv_lo, 1)
            for t in range(KT):
                dve.wait_ge(v_hi_set, t + 1)
                q = t // VG
                nc.vector.tensor_tensor(v_lo[:, q % 2, :, t % VG, :], v_ps[:, t % 2, 0:HM * DH].rearrange("p (h v) -> p h v", v=DH),
                                        v_hi[:, q % 2, :, t % VG, :], ALU.subtract).then_inc(v_lo_set, 1)
            n = M1 - M0
            dve.wait_ge(wa_used, HALVES)
            nc.vector.tensor_tensor(g.mods[:, M0:M1, :], ada_ps[:, 0:2 * n].rearrange("p (m c) -> p m c", c=2),
                                    g.b_ada[:, M0:M1, None].to_broadcast([P, n, 2]), ALU.add).then_inc(ada_set, 1)

        @block.tensor
        def _(pe):
            pe.wait_ge(w_lo_set, 2)
            pe.wait_ge(ckv_in, 32)

            def products(out, parts):
                for q, (sh, sl, mh, ml) in enumerate(parts):
                    for m, (x, y) in enumerate(((sh, mh), (sh, ml), (sl, mh))):
                        mm = nc.tensor.matmul(out, x, y, start=(q == 0 and m == 0), stop=(q == len(parts) - 1 and m == 2))
                return mm

            def k_tile(n, c, col, width):
                need(pe, lo_set, n - 2)
                w = slice(c * P, (c + 1) * P)
                products(ring[:, c, 0:width], [(ukv_hi[:, w], ukv_lo[:, w], ckv_hi[:, bass.ds(col, width)], ckv_lo[:, bass.ds(col, width)])]).then_inc(tile_done, 1)
            for c in range(3):
                k_tile(c, c, 0, CTX)

            def q_parts(s, c0):
                return [(uq_hi[:, k, c0:c0 + P], uq_lo[:, k, c0:c0 + P], cq_hi[s][:, k], cq_lo[s][:, k]) for k in range(2)]

            def modulations(half):
                pe.wait_ge(wa_in, 16 * (half + 1))
                for c in range(MH):
                    for k in range(KD):
                        col = 2 * (half * MH + c)
                        mm = nc.tensor.matmul(ada_ps[:, col:col + 2], wa[:, k, c * P:(c + 1) * P], g.cond[:, 2 * k:2 * k + 2],
                                              start=(k == 0), stop=(k == KD - 1))
                mm.then_inc(wa_used, 1)

            for b in range(NQB):
                s = b % 2
                pe.wait_ge(blk_in[s], 48 * (b // 2 + 1))
                for c in range(3):
                    pe.wait_ge(lo_set, items_before(b) + c - 2)
                    products(ring[:, c, :], q_parts(s, c * P)).then_inc(tile_done, 1)
                for c in range(3):
                    k_tile(items_before(b) + 3 + c, c, CTX + b * QB, QB)
                need(pe, rope_mults, b)
                products(rope_ps[:, 0, :], q_parts(s, 384))
                products(rope_ps[:, 1, :], q_parts(s, 512)).then_inc(rope_done, 1)
                if b < HALVES:
                    modulations(b)
            for t in range(KT):
                need(pe, v_lo_set, t - 1)
                k = slice(t * P, (t + 1) * P)
                products(v_ps[:, t % 2, 0:HM * DH], [(ckv_hi[:, k], ckv_lo[:, k], ukv_hi[:, 384:], ukv_lo[:, 384:])]).then_inc(v_done, 1)


def stage_attend(nc, g, a):
    with ExitStack() as ctx:
        sb = lambda n, s, d=F32: ctx.enter_context(nc.sbuf_tensor("a_" + n, s, d))
        ps = lambda n, s: ctx.enter_context(nc.psum_tensor("a_" + n, s, F32))
        sem = lambda n: ctx.enter_context(nc.semaphore("a_" + n))
        STEPS = KT // 2
        HEAD = STEPS * NQB
        BODY = 2 * HEAD
        NB = 2 * NQB
        HEADS = HM
        mk_hi, mk_lo = sb("mk_hi", [QK + 1, KEYS], F32R), sb("mk_lo", [QK, KEYS], F32R)
        mq_hi, mq_lo = sb("mq_hi", [QK + 1, T], F32R), sb("mq_lo", [QK, T], F32R)
        gk_hh, gk_lo = sb("gk_hh", [P, KEYS], F32R), sb("gk_lo", [DH + 1, KEYS], F32R)
        gq_hl, gq_hm = sb("gq_hl", [P, T], F32R), sb("gq_hm", [DH + 1, T], F32R)
        v1 = [sb(f"v1_{i}", [P, KT, P], F32R) for i in range(2)]
        v0 = [sb(f"v0_{i}", [P, KT, P], F32R) for i in range(2)]
        pf = [sb(f"pf{i}", [P, 2 * QB]) for i in range(2)]
        p_hi = [sb(f"p_hi{i}", [P, 2 * QB], F32R) for i in range(3)]
        p_lo = [sb(f"p_lo{i}", [P, 2 * QB], F32R) for i in range(3)]
        o_sb = sb("o_sb", [P, QB])
        o_out = sb("o_out", [P, 4, DH])
        rden = sb("rden", [P, 4])
        mpart, mneg = sb("mpart", [P, 4, 5]), sb("mneg", [P, 4])
        mcol = [sb("mcol_m", [P, 4, P], F32R), sb("mcol_g", [P, 4, P], F32R)]
        M0, MT = 16, 4
        wa = sb("wa", [P, 2, KD, 2 * P])
        sc = [ps(f"sc{i}", [P, 2 * QB]) for i in range(2)]
        mx = [ps(f"mx{i}", [P, QB]) for i in range(2)]
        o_ps, t_ps = ps("o", [P, QB]), ps("t", [P, QB])
        CHUNKS = [(k, min(QB, KEYS - k)) for k in range(0, KEYS, QB)]
        ITEMS = [(s, k) for s in range(4) for k in range(len(CHUNKS))]
        NI = len(ITEMS) + 1
        assert NI % 2 == 1 and BODY % 6 == 0

        consts = sem("consts")
        in_m, in_g, kpe_in = sem("in_m"), sem("in_g"), sem("kpe_in")
        scored, exped, hi_set, lo_set, pv_done = sem("scored"), sem("exped"), sem("hi_set"), sem("lo_set"), sem("pv_done")
        mx_done, mx_read, max_set, col_set, row_set = (sem(n) for n in ("mx_done", "mx_read", "max_set", "col_set", "row_set"))
        o_copied, o_turned, den_set, o_set, o_stored = (sem(n) for n in ("o_copied", "o_turned", "den_set", "o_set", "o_stored"))
        wa_in = [sem(f"wa_in{i}") for i in range(2)]
        ada_done, ada_set = sem("ada_done"), sem("ada_set")
        block = ctx.enter_context(nc.Block())
        raw = lambda t: t.bitcast(F32)
        SCALES = (float(QK) ** -0.5, float(DH) ** -0.5)
        LOADS_M, LOADS_G = 10, 8

        @block.sync
        def _(sp):
            sp.dma_start(raw(mk_hi[NOPE:QK, :]), g.kpe[0]).then_inc(kpe_in, 16)
            sp.dma_start(raw(mk_lo[NOPE:QK, :]), g.kpe[1]).then_inc(kpe_in, 16)

            def load_m(h):
                rows = slice(h * NOPE, (h + 1) * NOPE)
                for part, (k, q, v) in enumerate(((mk_hi, mq_hi, v1[0]), (mk_lo, mq_lo, v0[0]))):
                    sp.dma_start(raw(k[0:NOPE, :]), g.kn[part][rows]).then_inc(in_m, 16)
                    sp.dma_start(raw(q[0:NOPE, :]), g.qn[part][rows]).then_inc(in_m, 16)
                    for r in range(2):
                        sp.dma_start(raw(q[NOPE + 16 * r:NOPE + 16 * (r + 1), :]), g.qr[part][r][h * 16:(h + 1) * 16]).then_inc(in_m, 16)
                    sp.dma_start(raw(v[:, :, 0:DH]), g.vm[part][h]).then_inc(in_m, 16)

            def load_g(h):
                kv = h // (HG // HKV)
                rows, krows = slice(h * DH, (h + 1) * DH), slice(kv * DH, (kv + 1) * DH)
                sp.dma_start(raw(gk_hh[0:DH, :]), g.kg[0][krows]).then_inc(in_g, 16)
                sp.dma_start(raw(gk_hh[DH:P, :]), g.kg[0][krows]).then_inc(in_g, 16)
                sp.dma_start(raw(gk_lo[0:DH, :]), g.kg[1][krows]).then_inc(in_g, 16)
                sp.dma_start(raw(gq_hl[0:DH, :]), g.qg[0][rows]).then_inc(in_g, 16)
                sp.dma_start(raw(gq_hl[DH:P, :]), g.qg[1][rows]).then_inc(in_g, 16)
                sp.dma_start(raw(gq_hm[0:DH, :]), g.qg[0][rows]).then_inc(in_g, 16)
                for part, v in enumerate((v1[1], v0[1])):
                    sp.dma_start(raw(v[:, :, 0:DH]), g.vg[:, :, part, krows]).then_inc(in_g, 16)

            def store(i, nb):
                sp.wait_ge(o_set, i * NB + nb + 1)
                col = (i if nb < NQB else HM + i) * DH
                row = (nb % NQB) * QB
                sp.dma_start(g.mix[row:row + QB, col:col + DH].rearrange("(s p) v -> p s v", p=P), o_out[:, :, :]).then_inc(o_stored, 16)
            def load_wa(i, s):
                col = (M0 + MT * i + 2 * s) * P
                sp.dma_start(wa[:, s], a["w_ada"][:, col:col + 2 * P].rearrange("(k p) c -> p k c", p=P)).then_inc(wa_in[s], 16)
            sp.sem_inc(o_stored, 16)
            load_m(0)
            load_g(0)
            load_wa(0, 0)
            load_wa(0, 1)
            for i in range(HEADS):
                for nb in range(NQB):
                    store(i, nb)
                if i + 1 < HEADS:
                    sp.wait_ge(ada_done, 2 * i + 1)
                    load_wa(i + 1, 0)
                sp.wait_ge(pv_done, i * BODY + HEAD)
                load_m((i + 1) % HEADS)
                for nb in range(NQB, NB):
                    store(i, nb)
                if i + 1 < HEADS:
                    sp.wait_ge(ada_done, 2 * i + 2)
                    load_wa(i + 1, 1)
                    load_g(i + 1)
            sp.wait_ge(o_stored, 16 * HEADS * NB + 16)
            sp.wait_ge(in_m, 16 * LOADS_M * (HEADS + 1))

        @block.gpsimd
        def _(pool):
            for i in range(2):
                nc.gpsimd.memset(raw(v1[i][:, :, DH:P]), 1.0)
                nc.gpsimd.memset(raw(v0[i][:, :, DH:P]), 0.0)
                nc.gpsimd.memset(raw(mcol[i][:, :, :]), 0.0).then_inc(consts, 1)

        def each_turn(eng, body):
            with eng.Fori(0, HEADS) as i:
                body(i)

        item_no = lambda i, nb, c: i * (NI * NB) + (NI * (nb + 1) + c)
        reads_no = lambda i, nb, c: i * ((NI - 1) * NB) + ((NI - 1) * (nb + 1) + c)
        ITEM_STEPS = [range(3 * t, min(3 * t + 3, NI - 1)) for t in range(7)]
        ADA_AT = {2: 0, 6: 1}
        is_mla = lambda nb: nb % NB < NQB

        @block.scalar
        def _(act):
            def row(i, nb):
                n = item_no(i, nb, NI - 1)
                act.wait_ge(mx_done, n + 1)
                q = slice(((nb + 1) % NQB) * QB, ((nb + 1) % NQB + 1) * QB)
                bank = mx[(NI * (nb + 1) + NI - 1) % 2]
                if is_mla(nb + 1):
                    nc.scalar.activation(mq_hi[QK:QK + 1, q], bank[QK:QK + 1, :], ACT.Copy).then_inc(row_set, 1)
                else:
                    nc.scalar.activation(gq_hm[DH:DH + 1, q], bank[DH:DH + 1, :], ACT.Copy).then_inc(row_set, 1)
            row(0, -1)

            def copy_o(i, nb):
                act.wait_ge(pv_done, i * BODY + STEPS * (nb + 1))
                if nb:
                    act.wait_ge(o_turned, i * NB + nb)
                nc.scalar.activation(o_sb[:, :], o_ps[:, :], ACT.Copy).then_inc(o_copied, 1)

            def body(i):
                for st in range(BODY):
                    nb, kp = divmod(st, STEPS)
                    n = i * BODY + st
                    if kp == 2 and nb:
                        copy_o(i, nb - 1)
                    if kp == 8:
                        row(i, nb)
                    act.wait_ge(scored, n + 1)
                    if st >= 2:
                        act.wait_ge(lo_set, n - 1)
                    nc.scalar.activation(pf[st % 2][:, :], sc[st % 2][:, :], ACT.Exp, scale=SCALES[nb // NQB]).then_inc(exped, 1)
                    act.wait_ge(exped, n + 1)
                    if st >= 3:
                        act.wait_ge(pv_done, n - 2)
                    nc.scalar.activation(p_hi[st % 3][:, :], pf[st % 2][:, :], ACT.Copy).then_inc(hi_set, 1)
                copy_o(i, NB - 1)
            each_turn(act, body)

        @block.vector
        def _(dve):
            nc.vector.memset(raw(mk_hi[QK:QK + 1, :]), 1.0)
            nc.vector.memset(raw(gk_lo[DH:DH + 1, :]), 1.0).then_inc(consts, 1)
            dve.wait_ge(consts, 3)

            def read_max(i, nb, c):
                s, k = ITEMS[c]
                dve.wait_ge(mx_done, item_no(i, nb, c) + 1)
                width = CHUNKS[k][1]
                ins = nc.vector.reduce_max(mpart[:, s, k:k + 1], mx[(NI * (nb + 1) + c) % 2][:, 0:width], AX.X)
                ins.then_inc(mx_read, 1)

            def columns(i, nb):
                b = i * NB + nb
                dve.wait_ge(mx_read, reads_no(i, nb, NI - 1))
                nc.vector.reduce_max(mneg[:, :], mpart[:, :, :], AX.X).then_inc(max_set, 1)
                dve.wait_ge(max_set, b + 2)
                col = QK if is_mla(nb + 1) else DH
                nc.vector.tensor_scalar(mcol[0 if is_mla(nb + 1) else 1][:, :, col], mneg[:, :], -1.0, None, ALU.mult).then_inc(col_set, 1)
            for c in range(NI - 1):
                read_max(0, -1, c)
            columns(0, -1)

            def low(i, st):
                n = i * BODY + st
                dve.wait_ge(hi_set, n + 1)
                nc.vector.tensor_tensor(p_lo[st % 3][:, :], pf[st % 2][:, :], p_hi[st % 3][:, :], ALU.subtract).then_inc(lo_set, 1)

            def norm_o(i, nb):
                b = i * NB + nb
                dve.wait_ge(o_turned, b + 1)
                t = t_ps[:, :].rearrange("p (s v) -> p s v", s=4)
                nc.vector.reciprocal(rden[:, :], t[:, :, DH]).then_inc(den_set, 1)
                dve.wait_ge(den_set, b + 1)
                dve.wait_ge(o_stored, b * 16 + 16)
                nc.vector.tensor_tensor(o_out[:, :, :], t[:, :, 0:DH], rden[:, :, None].to_broadcast([P, 4, DH]), ALU.mult).then_inc(o_set, 1)

            def body(i):
                for st in range(BODY):
                    nb, kp = divmod(st, STEPS)
                    its = list(ITEM_STEPS[kp]) if kp < 7 else []
                    for c in its[:2]:
                        read_max(i, nb, c)
                    if st:
                        low(i, st - 1)
                    for c in its[2:]:
                        read_max(i, nb, c)
                    if kp == 6:
                        columns(i, nb)
                    if kp == 4 and nb:
                        norm_o(i, nb - 1)
                    if kp == 6 and nb in ADA_AT:
                        s = ADA_AT[nb]
                        dve.wait_ge(ada_done, i * 2 + (s + 1))
                        m = bass.ds(i * MT + (M0 + 2 * s), 2)
                        nc.vector.tensor_tensor(g.mods[:, m, :], t_ps[:, 0:4].rearrange("p (m c) -> p m c", c=2),
                                                g.b_ada[:, m, None].to_broadcast([P, 2, 2]), ALU.add).then_inc(ada_set, 1)
                low(i, BODY - 1)
                norm_o(i, NB - 1)
            each_turn(dve, body)
            dve.wait_ge(ada_set, 2 * HEADS)
            nc.vector.tensor_scalar(g.mods[:, 32:40, :], g.mods[:, 32:40, :], 1.0, None, ALU.add).then_inc(ada_set, 1)

        @block.tensor
        def _(pe):
            pe.wait_ge(consts, 3)
            pe.wait_ge(kpe_in, 32)

            def items(i, nb, cs_):
                q0 = ((nb + 1) % NQB) * QB
                for c in cs_:
                    s, k = ITEMS[c]
                    k0, width = CHUNKS[k]
                    if c >= 2:
                        pe.wait_ge(mx_read, reads_no(i, nb, c - 1))
                    elif c == 0:
                        need(pe, mx_read, reads_no(i, nb, 0) if nb >= 0 else 0)
                    elif nb >= 0:
                        pe.wait_ge(row_set, i * NB + nb + 1)
                    queries = slice(q0 + s * P, q0 + (s + 1) * P)
                    lhs, rhs = (mq_hi[0:QK, queries], mk_hi[0:QK, k0:k0 + width]) if is_mla(nb + 1) else (gq_hl[:, queries], gk_hh[:, k0:k0 + width])
                    nc.tensor.matmul(mx[(NI * (nb + 1) + c) % 2][:, 0:width], lhs, rhs, start=True, stop=True).then_inc(mx_done, 1)

            def lay_row(i, nb):
                pe.wait_ge(mx_read, reads_no(i, nb, NI - 2))
                pe.wait_ge(col_set, i * NB + nb + 2)
                for s in range(4):
                    mm = nc.tensor.matmul(mx[(NI * (nb + 1) + NI - 1) % 2][:, s * P:(s + 1) * P], mcol[0 if is_mla(nb + 1) else 1][:, s], g.ident_r[:, :],
                                          start=True, stop=True)
                mm.then_inc(mx_done, 1)

            def scores(i, st, half):
                nb, kp = divmod(st, STEPS)
                n = i * BODY + st
                if st >= 2 and half == 0:
                    pe.wait_ge(exped, n - 1)
                if kp == 0 and half == 0:
                    pe.wait_ge(row_set, i * NB + nb + 1)
                q = slice((nb % NQB) * QB, (nb % NQB + 1) * QB)
                k = slice((2 * kp + half) * P, (2 * kp + half + 1) * P)
                out = sc[st % 2][:, half * QB:(half + 1) * QB]
                if nb < NQB:
                    ops = ((mk_hi[:, k], mq_hi[:, q]), (mk_hi[0:QK, k], mq_lo[:, q]), (mk_lo[:, k], mq_hi[0:QK, q]))
                else:
                    ops = ((gk_hh[:, k], gq_hl[:, q]), (gk_lo[:, k], gq_hm[:, q]))
                for m, (x, y) in enumerate(ops):
                    mm = nc.tensor.matmul(out, x, y, start=(m == 0), stop=(m == len(ops) - 1))
                if half == 1:
                    mm.then_inc(scored, 1)

            def values(i, st, half):
                nb, kp = divmod(st, STEPS)
                n = i * BODY + st
                if half == 0:
                    pe.wait_ge(lo_set, n + 1)
                if kp == 0 and nb and half == 0:
                    pe.wait_ge(o_copied, i * NB + nb)
                kind = nb // NQB
                kt, cols = 2 * kp + half, slice(half * QB, (half + 1) * QB)
                ops = ((v1[kind][:, kt], p_hi[st % 3][:, cols]), (v1[kind][:, kt], p_lo[st % 3][:, cols]), (v0[kind][:, kt], p_hi[st % 3][:, cols]))
                for m, (x, y) in enumerate(ops):
                    mm = nc.tensor.matmul(o_ps[:, :], x, y, start=(kt == 0 and m == 0), stop=(kt == KT - 1 and m == 2))
                if half == 1:
                    mm.then_inc(pv_done, 1)

            def turn_o(i, nb):
                b = i * NB + nb
                pe.wait_ge(o_copied, b + 1)
                if nb:
                    pe.wait_ge(o_set, b)
                if nb - 1 in ADA_AT:
                    pe.wait_ge(ada_set, i * 2 + (ADA_AT[nb - 1] + 1))
                for s in range(4):
                    mm = nc.tensor.transpose(t_ps[:, s * P:(s + 1) * P], o_sb[:, s * P:(s + 1) * P], g.ident[:, :])
                mm.then_inc(o_turned, 1)

            def modulations(i, nb):
                s = ADA_AT[nb]
                pe.wait_ge(wa_in[s], i * 16 + 16)
                pe.wait_ge(o_set, i * NB + nb)
                for c in range(2):
                    for k in range(KD):
                        mm = nc.tensor.matmul(t_ps[:, 2 * c:2 * c + 2], wa[:, s, k, c * P:(c + 1) * P], g.cond[:, 2 * k:2 * k + 2],
                                              start=(k == 0), stop=(k == KD - 1))
                mm.then_inc(ada_done, 1)

            pe.wait_ge(in_m, 16 * LOADS_M)
            items(0, -1, range(NI - 1))
            lay_row(0, -1)

            def body(i):
                for st in range(BODY):
                    nb, kp = divmod(st, STEPS)
                    its = list(ITEM_STEPS[kp]) if kp < 7 else []
                    scores(i, st, 0)
                    if kp == 0 and nb == NQB - 1:
                        pe.wait_ge(in_g, i * (16 * LOADS_G) + 16 * LOADS_G)
                    if kp == 0 and nb == NB - 1:
                        pe.wait_ge(in_m, i * (16 * LOADS_M) + 32 * LOADS_M)
                    items(i, nb, its[:1])
                    scores(i, st, 1)
                    items(i, nb, its[1:2])
                    if kp == 3 and nb:
                        turn_o(i, nb - 1)
                    if st >= 2:
                        values(i, st - 2, 0)
                    items(i, nb, its[2:3])
                    if st >= 2:
                        values(i, st - 2, 1)
                    if kp == 5 and nb in ADA_AT:
                        modulations(i, nb)
                    if kp == 7:
                        lay_row(i, nb)
                for st in (BODY - 2, BODY - 1):
                    for half in range(2):
                        values(i, st, half)
                turn_o(i, NB - 1)
            each_turn(pe, body)


def gate_row(nc, pe, g, ps_pair, m0):
    for k in range(KD):
        mm = nc.tensor.matmul(ps_pair[:, k * P:(k + 1) * P], g.mods[:, m0 + k, 0:1].to_broadcast([P, P]), g.ident[:, :],
                              start=True, stop=True)
    return mm


def stage_mix(nc, g, a):
    with ExitStack() as ctx:
        sb = lambda n, s, d=F32: ctx.enter_context(nc.sbuf_tensor("o_" + n, s, d))
        ps = lambda n, s: ctx.enter_context(nc.psum_tensor("o_" + n, s, F32))
        sem = lambda n: ctx.enter_context(nc.semaphore("o_" + n))
        KO = 2 * HM * DH // P
        wo_hi, wo_lo = sb("wo_hi", [P, KD, D], F32R), sb("wo_lo", [P, KD, D], F32R)
        stage = [sb(f"stage{i}", [P, D]) for i in range(2)]
        mix = [sb(f"mix{i}", [P, KO * P]) for i in range(2)]
        m_hi = [sb(f"m_hi{i}", [P, KD, P], F32R) for i in range(2)]
        m_lo = [sb(f"m_lo{i}", [P, KD, P], F32R) for i in range(2)]
        x = [sb(f"x{i}", [P, D]) for i in range(2)]
        gate, ln_g, ln_b = sb("gate", [P, D]), sb("ln_g", [P, D]), sb("ln_b", [P, D])
        r = [sb(f"r{i}", [P, D]) for i in range(2)]
        x1 = [sb(f"x1{i}", [P, D]) for i in range(2)]
        u = sb("u", [P, KD, P])
        u_hi, u_lo = sb("u_hi", [P, KD, P], F32R), sb("u_lo", [P, KD, P], F32R)
        stats, mv, var, rstd, tmp = sb("stats", [P, 2, 6]), sb("mv", [P, 2]), sb("var", [P, 1]), sb("rstd", [P, 1]), sb("tmp", [P, 1])
        t_mix, y, t_x = ps("t_mix", [P, 2, 512]), ps("y", [P, 2, 512]), ps("t_x", [P, 2, 512])

        rows_in, gate_done, gate_set = sem("rows_in"), sem("gate_done"), sem("gate_set")
        w_in = [sem(f"w_in{i}") for i in range(2)]
        w_hi_set, w_lo_set = sem("w_hi_set"), sem("w_lo_set")
        mix_in = [sem(f"mix_in{i}") for i in range(2)]
        x_in = [sem(f"x_in{i}") for i in range(2)]
        turned, m_hi_set, m_lo_set, y_done, y_read = sem("turned"), sem("m_hi_set"), sem("m_lo_set"), sem("y_done"), sem("y_read")
        step, var_set, std_set, normed, x1_set = sem("step"), sem("var_set"), sem("std_set"), sem("normed"), sem("x1_set")
        x_turned, u_set, u_hi_set, u_lo_set = sem("x_turned"), sem("u_set"), sem("u_hi_set"), sem("u_lo_set")
        x1_stored = [sem(f"x1_stored{i}") for i in range(2)]
        u_stored, u0_in = sem("u_stored"), sem("u0_in")
        block = ctx.enter_context(nc.Block())
        raw = lambda t: t.bitcast(F32)
        STEPS = 9

        def schedule(eng, first, work, out):
            def step_(i, c):
                t = i * 2 + c
                if c + 1 < TT:
                    first(t + 1, (c + 1) % 2, i + (c + 1) // 2)
                work(t, c % 2, i + c // 2)
                if c > 0:
                    out(t - 1, (c - 1) % 2, i + (c - 1) // 2)
            first(0, 0, 0)
            step_(0, 0)
            with eng.Fori(0, (TT - 2) // 2) as i:
                step_(i, 1)
                step_(i, 2)
            step_(0, TT - 1)
            out(TT - 1, 1, (TT - 1) // 2)

        @block.sync
        def _(sp):
            for row, name in ((ln_g, "ln1_g"), (ln_b, "ln1_b")):
                sp.dma_start(row[:, :], a[name]).then_inc(rows_in, 16)
            for k in range(KD):
                if k >= 2:
                    sp.wait_ge(w_lo_set, k - 1)
                sp.dma_start(stage[k % 2][:, :], a["w_o"][k * P:(k + 1) * P, :]).then_inc(w_in[k % 2], 16)

            def load(t, s, pair):
                if not isinstance(t, int) or t >= 2:
                    sp.wait_ge(y_done, t - 1)
                    sp.wait_ge(y_read, t - 1)
                tok = bass.ds(t * P, P)
                sp.dma_start(mix[s][:, :], g.mix[tok, :]).then_inc(mix_in[s], 16)
                sp.dma_start(x[s][:, :], a["x"][tok, :]).then_inc(x_in[s], 16)
                for part, m in enumerate((m_hi, m_lo)):
                    sp.dma_start(raw(m[s][:, KO:KD]), g.co[part][:, :, tok].rearrange("c p t -> p c t")).then_inc(x_in[s], 16)

            def store(t, s, pair):
                tok = bass.ds(t * P, P)
                sp.wait_ge(u_lo_set, t + 1)
                sp.wait_ge(rows_in, 32)
                sp.dma_start(g.x1[tok, :], x1[s][:, :]).then_inc(x1_stored[s], 16)
                for part, t_ in enumerate((u_hi, u_lo)):
                    sp.dma_start(g.u2[part][:, :, tok].rearrange("k p t -> p k t"), raw(t_[:, :, :])).then_inc(u_stored, 16)
            schedule(sp, load, lambda *_: None, store)
            sp.wait_ge(u_stored, 32 * TT)
            for part in range(2):
                sp.dma_start(raw(g.u0[part][:, :, :]), g.u2[part][:, :, 0:512].rearrange("k p t -> p k t")).then_inc(u0_in, 16)
            sp.wait_ge(u0_in, 32)
            for s in range(2):
                sp.wait_ge(x1_stored[s], 16 * (TT // 2))

        @block.scalar
        def _(act):
            for k in range(KD):
                act.wait_ge(w_in[k % 2], 16 * (k // 2 + 1))
                nc.scalar.activation(wo_hi[:, k], stage[k % 2][:, :], ACT.Copy).then_inc(w_hi_set, 1)

            def first(t, s, pair):
                act.wait_ge(turned, t + 1)
                if not isinstance(t, int) or t >= 2:
                    act.wait_ge(y_done, t - 1)
                nc.scalar.activation(m_hi[s][:, 0:4], t_mix[:, 0, :].rearrange("p (k t) -> p k t", t=P), ACT.Copy)
                nc.scalar.activation(m_hi[s][:, 4:KO], t_mix[:, 1, 0:2 * P].rearrange("p (k t) -> p k t", t=P), ACT.Copy).then_inc(m_hi_set, 1)

            def work(t, s, pair):
                act.wait_ge(var_set, t + 1)
                nc.scalar.activation(rstd[:, :], var[:, :], ACT.Sqrt).then_inc(std_set, 1)

            def out(t, s, pair):
                act.wait_ge(x_turned, t + 1)
                need(act, u_lo_set, t)
                for k in range(KD):
                    last = nc.scalar.activation(u[:, k], t_x[:, k // 4, (k % 4) * P:(k % 4 + 1) * P], ACT.Identity,
                                                scale=g.mods[:, 32 + k, 0:1], bias=g.mods[:, 24 + k, 0:1])
                last.then_inc(u_set, 1)
                act.wait_ge(u_set, t + 1)
                need(act, u_stored, t * 32)
                nc.scalar.activation(u_hi[:, :, :], u[:, :, :], ACT.Copy).then_inc(u_hi_set, 1)
            schedule(act, first, work, out)

        @block.vector
        def _(dve):
            for k in range(KD):
                dve.wait_ge(w_hi_set, k + 1)
                nc.vector.tensor_tensor(wo_lo[:, k], stage[k % 2][:, :], wo_hi[:, k], ALU.subtract).then_inc(w_lo_set, 1)
            dve.wait_ge(gate_done, 1)
            nc.vector.tensor_copy(gate[:, :], t_x[:, :, :].rearrange("p b n -> p (b n)")).then_inc(gate_set, 1)
            dve.wait_ge(gate_set, 1)

            def first(t, s, pair):
                dve.wait_ge(m_hi_set, t + 1)
                nc.vector.tensor_tensor(m_lo[s][:, 0:4], t_mix[:, 0, :].rearrange("p (k t) -> p k t", t=P), m_hi[s][:, 0:4], ALU.subtract)
                nc.vector.tensor_tensor(m_lo[s][:, 4:KO], t_mix[:, 1, 0:2 * P].rearrange("p (k t) -> p k t", t=P), m_hi[s][:, 4:KO],
                                        ALU.subtract).then_inc(m_lo_set, 1)

            def work(t, s, pair):
                seen = [0]

                def link(ins):
                    seen[0] += 1
                    ins.then_inc(step, 1)
                    dve.wait_ge(step, t * STEPS + seen[0])
                dve.wait_ge(y_done, t + 1)
                dve.wait_ge(x_in[s], pair * 48 + 48)
                if not isinstance(t, int) or t >= 2:
                    dve.wait_ge(x1_set, t - 1)
                link(nc.vector.tensor_tensor(r[s][:, :], y[:, :, :].rearrange("p b n -> p (b n)"), gate[:, :], ALU.mult))
                nc.vector.scalar_tensor_tensor(out=r[s][:, :], in0=x[s][:, :], scalar=ALPHA, in1=r[s][:, :], op0=ALU.mult, op1=ALU.add).then_inc(y_read, 1)
                dve.wait_ge(y_read, t + 1)
                for b in range(2):
                    ins = nc.vector.bn_stats(stats[:, b, :], r[s][:, b * 512:(b + 1) * 512])
                link(ins)
                nc.vector.memset(tmp[:, :], 0.0)
                link(nc.vector.bn_aggr(mv[:, :], stats[:, :, :]))
                nc.vector.tensor_scalar(var[:, :], mv[:, 1:2], EPS, None, ALU.add).then_inc(var_set, 1)
                dve.wait_ge(std_set, t + 1)
                link(nc.vector.reciprocal(rstd[:, :], rstd[:, :]))
                link(nc.vector.tensor_tensor(tmp[:, :], rstd[:, :], rstd[:, :], ALU.mult))
                link(nc.vector.tensor_tensor(tmp[:, :], tmp[:, :], var[:, :], ALU.mult))
                link(nc.vector.tensor_scalar(tmp[:, :], tmp[:, :], -0.5, 1.5, ALU.mult, ALU.add))
                link(nc.vector.tensor_tensor(rstd[:, :], rstd[:, :], tmp[:, :], ALU.mult))
                link(nc.vector.tensor_scalar(r[s][:, :], r[s][:, :], mv[:, 0:1], rstd[:, 0:1], ALU.subtract, ALU.mult))
                dve.wait_ge(rows_in, 32)
                if not isinstance(t, int) or t >= 2:
                    dve.wait_ge(x1_stored[s], pair * 16)
                    dve.wait_ge(x_turned, t - 1)
                nc.vector.tensor_tensor(x1[s][:, :], r[s][:, :], ln_g[:, :], ALU.mult).then_inc(normed, 1)
                assert seen[0] == STEPS, seen

            def out(t, s, pair):
                dve.wait_ge(u_hi_set, t + 1)
                nc.vector.tensor_tensor(u_lo[:, :, :], u[:, :, :], u_hi[:, :, :], ALU.subtract).then_inc(u_lo_set, 1)
            schedule(dve, first, work, out)

        @block.gpsimd
        def _(pool):
            pool.wait_ge(rows_in, 32)

            def work(t, s, pair):
                pool.wait_ge(normed, t + 1)
                nc.gpsimd.tensor_tensor(x1[s][:, :], x1[s][:, :], ln_b[:, :], ALU.add).then_inc(x1_set, 1)
            schedule(pool, lambda *_: None, work, lambda *_: None)

        @block.tensor
        def _(pe):
            gate_row(nc, pe, g, t_x[:, :, :].rearrange("p b n -> p (b n)"), 16).then_inc(gate_done, 1)

            def first(t, s, pair):
                pe.wait_ge(mix_in[s], pair * 16 + 16)
                need(pe, m_lo_set, t)
                for k in range(KO):
                    mm = nc.tensor.transpose(t_mix[:, k // 4, (k % 4) * P:(k % 4 + 1) * P], mix[s][:, k * P:(k + 1) * P], g.ident[:, :])
                mm.then_inc(turned, 1)

            def work(t, s, pair):
                pe.wait_ge(w_hi_set, KD)
                pe.wait_ge(w_lo_set, KD)
                pe.wait_ge(m_lo_set, t + 1)
                pe.wait_ge(x_in[s], pair * 48 + 48)
                need(pe, y_read, t)
                for k in range(KD):
                    for n, (x_, w_) in enumerate(((m_hi, wo_hi), (m_hi, wo_lo), (m_lo, wo_hi))):
                        for half in range(2):
                            mm = nc.tensor.matmul(y[:, half, :], x_[s][:, k], w_[:, k, half * 512:(half + 1) * 512],
                                                  start=(k == 0 and n == 0), stop=(k == KD - 1 and n == 2))
                mm.then_inc(y_done, 1)

            def out(t, s, pair):
                pe.wait_ge(x1_set, t + 1)
                pe.wait_ge(gate_set, 1)
                need(pe, u_set, t)
                for k in range(KD):
                    mm = nc.tensor.transpose(t_x[:, k // 4, (k % 4) * P:(k % 4 + 1) * P], x1[s][:, k * P:(k + 1) * P], g.ident[:, :])
                mm.then_inc(x_turned, 1)
            schedule(pe, first, work, out)


def stage_mlp(nc, g, a):
    with ExitStack() as ctx:
        sb = lambda n, s, d=F32: ctx.enter_context(nc.sbuf_tensor("f_" + n, s, d))
        ps = lambda n, s: ctx.enter_context(nc.psum_tensor("f_" + n, s, F32))
        sem = lambda n: ctx.enter_context(nc.semaphore("f_" + n))
        HALF = T // 2
        GF = 256
        NG = FF // GF
        NF = GF // P
        TB = HALF // 512
        YT = HALF // P
        u_hi, u_lo = [g.u0[0], sb("u_hi1", [P, KD, 512], F32R)], [g.u0[1], sb("u_lo1", [P, KD, 512], F32R)]
        yacc = sb("yacc", [P, YT, D])
        w1_hi, w1_lo = sb("w1_hi", [P, KD, GF], F32R), sb("w1_lo", [P, KD, GF], F32R)
        w2_hi, w2_lo = sb("w2_hi", [P, NF, D], F32R), sb("w2_lo", [P, NF, D], F32R)
        h_hi, h_lo = sb("h_hi", [P, NF, HALF], F32R), sb("h_lo", [P, NF, HALF], F32R)
        W1S, W2S = KD * GF // D, NF
        SL = W1S + W2S
        stage = [sb(f"stage{i}", [P, D]) for i in range(SL)]
        rl = [sb(f"relu{i}", [P, 512]) for i in range(2)]
        gate, ln_g, ln_b = sb("gate", [P, D]), sb("ln_g", [P, D]), sb("ln_b", [P, D])
        r, x = sb("ln_r", [P, D]), sb("ln_x", [P, D])
        stats, mv, var, rstd, tmp = sb("stats", [P, 2, 6]), sb("mv", [P, 2]), sb("var", [P, 1]), sb("rstd", [P, 1]), sb("tmp", [P, 1])
        LB = 4
        mv_e, var_e, rstd_e, tmp_e, mean_e = sb("mv_e", [P, YT, 2]), sb("var_e", [P, YT]), sb("rstd_e", [P, YT]), sb("tmp_e", [P, YT]), sb("mean_e", [P, YT])
        one = [ps(f"one{i}", [P, 512]) for i in range(4)]
        two = ps("two", [P, 4, 512])

        u_in = [sem(f"u_in{i}") for i in range(TB)]
        st_in = [sem(f"st_in{i}") for i in range(SL)]
        w_hi_set, w_lo_set = sem("w_hi_set"), sem("w_lo_set")
        one_done, relu_set, sq_set, h_hi_set, h_lo_set = sem("one_done"), sem("relu_set"), sem("sq_set"), sem("h_hi_set"), sem("h_lo_set")
        two_done, two_read = sem("two_done"), sem("two_read")
        y_stored = [sem(f"y_stored{i}") for i in range(2)]
        rows_in, gate_done, gate_set = sem("rows_in"), sem("gate_done"), sem("gate_set")
        ln_in, step, var_set, std_set, normed, ln_out, ln_stored = (sem(n) for n in (
            "ln_in", "ln_step", "var_set", "std_set", "normed", "ln_out", "ln_stored"))
        x_in, gated, centred, scaled, out_even, out_odd, out_stored = (sem(n) for n in (
            "x_in", "gated", "centred", "scaled", "out_even", "out_odd", "out_stored"))
        block = ctx.enter_context(nc.Block())
        raw = lambda t: t.bitcast(F32)
        ONES, TWOS = TB * NF, YT * 2
        LN_STEPS = 10
        x_end = [raw(t[:, :, :]).rearrange("p k t -> p (k t)") for t in u_lo]

        def groups(eng, group):
            for hf in range(2):
                group(hf * NG, True, None, False)
                if hf == 0:
                    with eng.Fori(0, NG - 1) as q:
                        group(q + 1, False, None, False)
                else:
                    with eng.Fori(0, YT) as q:
                        group(q + (NG + 1), False, q, False)
                    with eng.Fori(0, NG - YT - 2) as q:
                        group(q + (NG + YT + 1), False, None, False)
            group(2 * NG - 1, False, None, True)

        @block.sync
        def _(sp):
            def weights(gn, q):
                for j in range(SL):
                    if not isinstance(gn, int) or gn:
                        sp.wait_ge(w_lo_set, gn * SL + (j - SL + 1))
                    if j < W1S:
                        n = KD // W1S
                        sp.dma_start(stage[j][:, :].rearrange("p (k c) -> p k c", k=n),
                                     a["w1"][j * n * P:(j + 1) * n * P, bass.ds(q * GF, GF)].rearrange("(k p) c -> p k c", p=P)).then_inc(st_in[j], 16)
                    else:
                        sp.dma_start(stage[j][:, :], a["w2"][bass.ds(q * GF + (j - W1S) * P, P), :]).then_inc(st_in[j], 16)

            def load_u(hf, tb):
                for part, t in enumerate((u_hi[tb], u_lo[tb])):
                    sp.dma_start(raw(t[:, :, :]), g.u2[part][:, :, hf * HALF + tb * 512:hf * HALF + (tb + 1) * 512].rearrange("k p t -> p k t")).then_inc(u_in[tb], 16)

            weights(0, 0)
            load_u(0, 1)
            for row, name in ((ln_g, "ln2_g"), (ln_b, "ln2_b")):
                sp.dma_start(row[:, :], a[name]).then_inc(rows_in, 16)
            with sp.Fori(0, NG - 1) as q:
                weights(q + 1, q + 1)
            sp.wait_ge(one_done, (NG - 1) * ONES + NF)
            load_u(1, 0)
            weights(NG, 0)
            sp.wait_ge(one_done, NG * ONES)
            load_u(1, 1)
            for part in range(2):
                n = YT // 2
                sp.wait_ge(two_read, (NG - 1) * TWOS + (part + 1) * 2 * n)
                sp.dma_start(g.y[part * n * P:(part + 1) * n * P, :].rearrange("(t p) d -> p t d", p=P), yacc[:, part * n:(part + 1) * n, :]).then_inc(y_stored[part], 16)
            for part in range(2):
                sp.wait_ge(y_stored[part], 16)

            def with_tile(t):
                weights(t + (NG + 1), t + 1)
                need(sp, ln_stored, t * 16)
                sp.dma_start(r[:, :], g.y[bass.ds(t * P, P), :]).then_inc(ln_in, 16)
                sp.dma_start(x[:, :], g.x1[bass.ds(t * P, P), :]).then_inc(ln_in, 16)
            with_tile(0)
            with sp.Fori(0, YT - 1) as t:
                with_tile(t + 1)
            with sp.Fori(0, NG - YT - 1) as q:
                weights(q + (NG + YT + 1), q + (YT + 1))
            sp.wait_ge(one_done, 2 * NG * ONES)
            for part in range(2):
                n = YT // 2
                sp.dma_start(x_end[part].rearrange("p (t d) -> p t d", t=n),
                             g.x1[HALF + part * n * P:HALF + (part + 1) * n * P, :].rearrange("(t p) d -> p t d", p=P)).then_inc(x_in, 16)
            for t in range(YT):
                sp.wait_ge(out_odd if t % 2 else out_even, t // 2 + 1)
                sp.dma_start(a["out"][0, HALF + t * P:HALF + (t + 1) * P, :], yacc[:, t, :]).then_inc(out_stored, 16)
            sp.wait_ge(out_stored, 16 * YT)
            sp.wait_ge(ln_stored, 16 * YT)

        @block.scalar
        def _(act):
            def slice_hi(gn, j, dst):
                act.wait_ge(st_in[j], gn * 16 + 16)
                nc.scalar.activation(dst, stage[j][:, :], ACT.Copy).then_inc(w_hi_set, 1)

            def w1_of(gn):
                for j in range(W1S):
                    n = KD // W1S
                    slice_hi(gn, j, w1_hi[:, n * j:n * (j + 1)].rearrange("p k c -> p (k c)"))

            def hidden(gn, o):
                tb, f = divmod(o, NF)
                n = gn * ONES + o
                act.wait_ge(one_done, n + 1)
                nc.scalar.activation(rl[o % 2][:, :], one[o % 4][:, :], ACT.Relu).then_inc(relu_set, 1)
                act.wait_ge(sq_set, n + 1)
                nc.scalar.activation(h_hi[:, f, tb * 512:(tb + 1) * 512], rl[o % 2][:, :], ACT.Copy).then_inc(h_hi_set, 1)

            def group(gn, first, ln, last):
                for o in range(ONES):
                    if o < W2S:
                        act.wait_ge(one_done, gn * ONES + 1)
                        slice_hi(gn, W1S + o, w2_hi[:, o])
                    hidden(gn, o)
                if not last:
                    act.wait_ge(one_done, gn * ONES + ONES)
                    w1_of(gn + 1)
                if ln is not None:
                    act.wait_ge(var_set, ln + 1)
                    nc.scalar.activation(rstd[:, :], var[:, :], ACT.Sqrt).then_inc(std_set, 1)
            w1_of(0)
            act.wait_ge(gate_done, 1)
            nc.scalar.activation(gate[:, :], two[:, 0:2, :].rearrange("p b n -> p (b n)"), ACT.Copy).then_inc(gate_set, 1)
            groups(act, group)
            for b in range(YT // LB):
                act.wait_ge(var_set, YT + 2 * (b + 1))
                nc.scalar.activation(rstd_e[:, b * LB:(b + 1) * LB], var_e[:, b * LB:(b + 1) * LB], ACT.Sqrt).then_inc(std_set, 1)
                for t in range(b * LB, (b + 1) * LB):
                    nc.scalar.activation(yacc[:, t, :], yacc[:, t, :], ACT.Identity, bias=mean_e[:, t:t + 1]).then_inc(centred, 1)

        @block.gpsimd
        def _(pool):
            def slice_lo(gn, j, hi, lo):
                pool.wait_ge(w_hi_set, gn * SL + (j + 1))
                nc.gpsimd.tensor_tensor(lo, stage[j][:, :], hi, ALU.subtract).then_inc(w_lo_set, 1)

            def w1_of(gn):
                for j in range(W1S):
                    n = KD // W1S
                    slice_lo(gn, j, *(w[:, n * j:n * (j + 1)].rearrange("p k c -> p (k c)") for w in (w1_hi, w1_lo)))

            def group(gn, first, ln, last):
                for j in range(W2S):
                    slice_lo(gn, W1S + j, w2_hi[:, j], w2_lo[:, j])
                if not last:
                    w1_of(gn + 1)
                if ln is not None:
                    pool.wait_ge(normed, ln + 1)
                    nc.gpsimd.tensor_tensor(r[:, :], r[:, :], ln_b[:, :], ALU.add).then_inc(ln_out, 1)
                    pool.wait_ge(ln_out, ln + 1)
                    pool.dma_start(a["out"][0, bass.ds(ln * P, P), :], r[:, :]).then_inc(ln_stored, 16)
            w1_of(0)
            pool.wait_ge(rows_in, 32)
            groups(pool, group)
            for t in range(YT):
                pool.wait_ge(two_read, (2 * NG - 1) * TWOS + 2 * t + 2)
                nc.gpsimd.tensor_tensor(yacc[:, t, :], yacc[:, t, :], gate[:, :], ALU.mult).then_inc(gated, 1)
            for t in range(0, YT, 2):
                pool.wait_ge(scaled, t + 1)
                nc.gpsimd.tensor_tensor(yacc[:, t, :], yacc[:, t, :], ln_b[:, :], ALU.add).then_inc(out_even, 1)

        @block.vector
        def _(dve):
            def newton(link, rstd, var, tmp):
                link(nc.vector.reciprocal(rstd, rstd))
                link(nc.vector.tensor_tensor(tmp, rstd, rstd, ALU.mult))
                link(nc.vector.tensor_tensor(tmp, tmp, var, ALU.mult))
                link(nc.vector.tensor_scalar(tmp, tmp, -0.5, 1.5, ALU.mult, ALU.add))
                link(nc.vector.tensor_tensor(rstd, rstd, tmp, ALU.mult))

            def layer_norm(t):
                seen = [0]

                def link(ins):
                    seen[0] += 1
                    ins.then_inc(step, 1)
                    dve.wait_ge(step, t * LN_STEPS + seen[0])
                dve.wait_ge(ln_in, t * 32 + 32)
                link(nc.vector.tensor_tensor(r[:, :], r[:, :], gate[:, :], ALU.mult))
                link(nc.vector.scalar_tensor_tensor(out=r[:, :], in0=x[:, :], scalar=ALPHA, in1=r[:, :], op0=ALU.mult, op1=ALU.add))
                nc.vector.bn_stats(stats[:, 0, :], r[:, 0:512])
                link(nc.vector.bn_stats(stats[:, 1, :], r[:, 512:]))
                nc.vector.memset(tmp[:, :], 0.0)
                link(nc.vector.bn_aggr(mv[:, :], stats[:, :, :]))
                nc.vector.tensor_scalar(var[:, :], mv[:, 1:2], EPS, None, ALU.add).then_inc(var_set, 1)
                dve.wait_ge(std_set, t + 1)
                newton(link, rstd[:, :], var[:, :], tmp[:, :])
                link(nc.vector.tensor_scalar(r[:, :], r[:, :], mv[:, 0:1], rstd[:, 0:1], ALU.subtract, ALU.mult))
                nc.vector.tensor_tensor(r[:, :], r[:, :], ln_g[:, :], ALU.mult).then_inc(normed, 1)
                assert seen[0] == LN_STEPS, seen

            def add_up(gn, o, first):
                t, half = divmod(o, 2)
                dve.wait_ge(two_done, gn * TWOS + (o + 1))
                acc = yacc[:, t, half * 512:(half + 1) * 512]
                if first:
                    if gn and half == 0 and t % (YT // 2) == 0:
                        dve.wait_ge(y_stored[t // (YT // 2)], 16)
                    nc.vector.tensor_copy(acc, two[:, o % 4, :]).then_inc(two_read, 1)
                else:
                    nc.vector.tensor_tensor(acc, two[:, o % 4, :], acc, ALU.add).then_inc(two_read, 1)

            def group(gn, first, ln, last):
                for o in range(ONES):
                    tb, f = divmod(o, NF)
                    n = gn * ONES + o
                    dve.wait_ge(relu_set, n + 1)
                    nc.vector.tensor_tensor(rl[o % 2][:, :], rl[o % 2][:, :], rl[o % 2][:, :], ALU.mult).then_inc(sq_set, 1)
                    dve.wait_ge(h_hi_set, n + 1)
                    cols = slice(tb * 512, (tb + 1) * 512)
                    nc.vector.tensor_tensor(h_lo[:, f, cols], rl[o % 2][:, :], h_hi[:, f, cols], ALU.subtract).then_inc(h_lo_set, 1)
                if last:
                    return
                for o in range(TWOS):
                    add_up(gn, o, first)
                if ln is not None:
                    layer_norm(ln)
            dve.wait_ge(gate_set, 1)
            dve.wait_ge(rows_in, 32)
            groups(dve, group)

            steps = [0]

            def link(ins):
                steps[0] += 1
                ins.then_inc(step, 1)
                dve.wait_ge(step, YT * LN_STEPS + steps[0])

            def residual(t):
                dve.wait_ge(gated, t + 1)
                dve.wait_ge(x_in, 32)
                n = YT // 2
                link(nc.vector.scalar_tensor_tensor(out=yacc[:, t, :], in0=x_end[t // n][:, (t % n) * D:(t % n + 1) * D], scalar=ALPHA,
                                                    in1=yacc[:, t, :], op0=ALU.mult, op1=ALU.add))
                nc.vector.bn_stats(stats[:, 0, :], yacc[:, t, 0:512])
                link(nc.vector.bn_stats(stats[:, 1, :], yacc[:, t, 512:]))
                link(nc.vector.bn_aggr(mv_e[:, t, :], stats[:, :, :]))

            def chain(b):
                c = slice(b * LB, (b + 1) * LB)
                nc.vector.tensor_scalar(var_e[:, c], mv_e[:, c, 1], EPS, None, ALU.add).then_inc(var_set, 1)
                nc.vector.tensor_scalar(mean_e[:, c], mv_e[:, c, 0], -1.0, None, ALU.mult).then_inc(var_set, 1)
                dve.wait_ge(std_set, YT + b + 1)
                newton(link, rstd_e[:, c], var_e[:, c], tmp_e[:, c])

            def finish(t):
                dve.wait_ge(centred, t + 1)
                ins = nc.vector.scalar_tensor_tensor(out=yacc[:, t, :], in0=yacc[:, t, :], scalar=rstd_e[:, t:t + 1], in1=ln_g[:, :], op0=ALU.mult, op1=ALU.mult)
                ins.then_inc(scaled, 1)
                if t % 2:
                    dve.wait_ge(scaled, t + 1)
                    nc.vector.tensor_tensor(yacc[:, t, :], yacc[:, t, :], ln_b[:, :], ALU.add).then_inc(out_odd, 1)
            for t in range(YT + 1):
                if t < YT:
                    add_up(2 * NG - 1, 2 * t, False)
                    add_up(2 * NG - 1, 2 * t + 1, False)
                if t:
                    residual(t - 1)
                if t > LB:
                    finish(t - 1 - LB)
                if t and t % LB == 0:
                    chain(t // LB - 1)
            for t in range(YT - LB, YT):
                finish(t)

        @block.tensor
        def _(pe):
            gate_row(nc, pe, g, two[:, 0:2, :].rearrange("p b n -> p (b n)"), 40).then_inc(gate_done, 1)

            def group(gn, first, ln, last):
                pe.wait_ge(w_lo_set, gn * SL + W1S)
                for o in range(ONES):
                    tb, f = divmod(o, NF)
                    if first and f == 0:
                        need(pe, u_in[tb], 32 * ((gn > 0) + tb))
                    if o >= 4:
                        pe.wait_ge(relu_set, gn * ONES + (o - 3))
                    for k in range(KD):
                        w = slice(f * P, (f + 1) * P)
                        for n, (x_, y_) in enumerate(((w1_hi, u_hi), (w1_hi, u_lo), (w1_lo, u_hi))):
                            mm = nc.tensor.matmul(one[o % 4][:, :], x_[:, k, w], y_[tb][:, k], start=(k == 0 and n == 0), stop=(k == KD - 1 and n == 2))
                    mm.then_inc(one_done, 1)
                pe.wait_ge(w_lo_set, gn * SL + SL)
                if first and gn == 0:
                    pe.wait_ge(gate_set, 1)
                for o in range(TWOS):
                    t, half = divmod(o, 2)
                    if t % 4 == 0 and half == 0:
                        pe.wait_ge(h_lo_set, gn * ONES + NF * (t // 4 + 1))
                    if o >= 4:
                        pe.wait_ge(two_read, gn * TWOS + (o - 3))
                    for f in range(NF):
                        tok, cols = slice(t * P, (t + 1) * P), slice(half * 512, (half + 1) * 512)
                        for n, (x_, y_) in enumerate(((h_hi, w2_hi), (h_hi, w2_lo), (h_lo, w2_hi))):
                            mm = nc.tensor.matmul(two[:, o % 4, :], x_[:, f, tok], y_[:, f, cols], start=(f == 0 and n == 0), stop=(f == NF - 1 and n == 2))
                    mm.then_inc(two_done, 1)
            groups(pe, group)


def make_shared(nc, ctx, a):
    g = Shared()
    sb = lambda n, s, d=F32: ctx.enter_context(nc.sbuf_tensor(n, s, d))
    g.ident, g.ident_r = sb("ident", [P, P]), sb("ident_r", [P, P], F32R)
    g.ones = sb("ones_f", [P, P])
    g.cond = sb("cond_silu", [P, KD * 2])
    g.b_ada = sb("b_ada_c", [P, 48])
    g.mods = sb("mods", [P, 48, 2])
    g.gcol = sb("gcol", [P, 9])
    dram = lambda n, s: nc.dram_tensor(n, s, F32, kind="Internal").ap()
    g.ckv = dram("s_ckv", [2, P, KEYS])
    g.cq = dram("s_cq", [2, 2, P, T])
    g.kg = dram("s_kg", [2, HKV * DH, KEYS])
    g.kpe = dram("s_kpe", [2, ROPE, KEYS])
    g.vg = dram("s_vg", [P, KT, 2, HKV * DH])
    g.qg = dram("s_qg", [2, HG * DH, T])
    g.conv_p, g.conv_b = dram("s_conv_p", [2, P, T]), dram("s_conv_b", [2, P, T])
    g.qn, g.qr = dram("s_qn", [2, HM * NOPE, T]), dram("s_qr", [2, 2, HM * 16, T])
    g.kn = dram("s_kn", [2, HM * NOPE, KEYS])
    g.vm = dram("s_vm", [2, HM, P, KT, DH])
    g.co = dram("s_co", [2, 2, P, T])
    g.mix = dram("s_mix", [T, 2 * HM * DH])
    g.x1, g.u2, g.y = dram("s_x1", [T, D]), dram("s_u2", [2, KD, P, T]), dram("s_y", [T, D])
    return g


STAGES = [stage_modulate, stage_project, stage_expand, stage_attend, stage_mix, stage_mlp]


def build(nc, a, stages=None):
    with ExitStack() as ctx:
        g = make_shared(nc, ctx, a)
        for stage in stages or STAGES:
            if stage is stage_mix:
                g.u0 = [ctx.enter_context(nc.sbuf_tensor(f"u0_{part}", [P, KD, 512], F32R)) for part in ("hi", "lo")]
            stage(nc, g, a)


def rope_tables():
    t = np.arange(T)
    row, col = (t // 64).astype(np.float32), (t % 64).astype(np.float32)
    out = []
    for dim in (DH, ROPE):
        n = dim // 4
        inv = (np.float32(10000.0) ** (-np.arange(n, dtype=np.float32) / np.float32(n))).astype(np.float32)
        ang = np.concatenate([row[:, None] * inv, col[:, None] * inv], axis=-1)
        out += [np.cos(ang).astype(np.float32), np.sin(ang).astype(np.float32)]
    return out


def lay_out(x, c, ctx, c_ctx, w_ada, b_ada, w_in, g_cq, w_uq, g_ckv, w_ukv, g_qn, g_kn,
            w_conv, w_o, ln1_g, ln1_b, w_mlp1, w_mlp2, ln2_g, ln2_b):
    f = lambda t: np.ascontiguousarray(t)
    tiles = lambda t: f(t.reshape(-1, P, KD, P).transpose(0, 3, 2, 1))
    rep = lambda row: f(np.broadcast_to(row, (P, row.size)))
    cg, sg, cr, sr = rope_tables()
    w = w_in[0]
    kv, q = 416, 640
    cols = [w[:, 128:160], w[:, 288:416], w[:, 0:128], w[:, 160:288], w[:, kv + 256:kv + q], w[:, kv:kv + 256], w[:, kv + q:]]
    uq, ukv, pad = w_uq[0].reshape(QR, HM, QK), w_ukv[0].reshape(KVR, HM, 2 * DH), np.zeros((QR, 32), np.float32)
    out = {
        "x_t": tiles(x[0]), "ctx_t": tiles(ctx[0]),
        "cond": f(np.stack([c[0].reshape(KD, P).T, c_ctx.reshape(KD, P).T], axis=2).reshape(P, 2 * KD)),
        "w_ada": f(w_ada[0]), "b_ada": f(b_ada[0].reshape(48, P).T),
        "w_in": f(np.concatenate(cols, axis=1)),
        "gcol": f(np.concatenate([g_ckv[0][:, None], g_cq[0].reshape(2, P).T, w_conv[0].reshape(3, 2, P).transpose(2, 1, 0).reshape(P, 6)], axis=1)),
        "g_heads": rep(np.concatenate([g_kn[0]] * HKV + [g_qn[0]] * HG)),
        "inv_n": rep(np.array([1 / KVR] + [1 / DH] * 8 + [1 / QR], np.float32)),
        "cs_tok": f(np.concatenate([cg, sg, cr, sr], axis=1).reshape(TT, P, 96).transpose(1, 0, 2)),
        "w_uq": f(np.concatenate([uq[:, :, :NOPE].reshape(QR, -1), uq[:, :, NOPE::2].reshape(QR, -1), pad,
                                  uq[:, :, NOPE + 1::2].reshape(QR, -1), pad], axis=1)),
        "w_ukv": f(np.concatenate([ukv[:, :, :NOPE].reshape(KVR, -1), ukv[:, :, NOPE:].reshape(KVR, -1)], axis=1)),
        "x": f(x[0]), "w_o": f(w_o[0]), "w1": f(w_mlp1[0]), "w2": f(w_mlp2[0]),
        "ln1_g": rep(ln1_g[0]), "ln1_b": rep(ln1_b[0]), "ln2_g": rep(ln2_g[0]), "ln2_b": rep(ln2_b[0]),
        "cs_rope": f(np.stack([np.tile(cr.T, (HM, 1)), np.tile(sr.T, (HM, 1))], axis=1)),
    }
    return out


def kernel(**inputs):
    import concourse.bacc as bacc
    from concourse.bass_utils import run_bass_kernel_spmd

    arrays = {f"in_{n}": v for n, v in lay_out(**{k: np.asarray(v) for k, v in inputs.items()}).items()}
    nc = bacc.Bacc("TRN2", target_bir_lowering=False, num_devices=1)
    a = {n[3:]: nc.dram_tensor(n, v.shape, mybir.dt.from_np(v.dtype), kind="ExternalInput").ap() for n, v in arrays.items()}
    a["out"] = nc.dram_tensor("out_0", (1, T, D), F32, kind="ExternalOutput").ap()
    build(nc, a)
    r = run_bass_kernel_spmd(nc, [arrays], core_ids=[0])
    return r.results[0]["out_0"]
```

```python
from contextlib import ExitStack

import numpy as np
import concourse.bass as bass
from concourse import mybir

F32 = mybir.dt.float32
F32R = mybir.dt.float32r
ACT = mybir.ActivationFunctionType
ALU = mybir.AluOpType
AX = mybir.AxisListType

P = 128
D = 1024
T = 2048
CTX = 256
KEYS = CTX + T
KD = D // P
TT = T // P
CT = CTX // P
KT = KEYS // P
HM = 6
HG = 6
HKV = 2
DH = 64
NOPE, ROPE = 64, 32
QK = NOPE + ROPE
QR, KVR = 256, 128
CW = 256
FF = 4 * D
EPS = 1e-6
ALPHA = 2.0 ** 0.25
O_KPE, O_GV, O_CKV, O_GK, O_GQ, O_CQ, O_CH, O_CB, O_CC = 0, 32, 160, 288, 416, 800, 1056, 1312, 1568
NCOL = O_CC + CW
BANKS = [(0, 416), (416, 384), (800, 512), (1312, 512)]
NORM = NCOL - 3 * CW - O_CKV
QB = 512
NQB = T // QB


class Shared:
    pass


def need(eng, sem, value):
    if not isinstance(value, int) or value > 0:
        eng.wait_ge(sem, value)


def stage_modulate(nc, g, a):
    with ExitStack() as ctx:
        sb = lambda n, s, d=F32: ctx.enter_context(nc.sbuf_tensor(n, s, d))
        sem = lambda n: ctx.enter_context(nc.semaphore(n))
        SLOTS = 4
        NM = 2 * D
        w = sb("ada_w", [P, SLOTS, NM])
        cond = sb("cond", [P, KD * 2])
        rows = [sb(f"w_in_rows{i}", [P, NCOL]) for i in range(2)]
        en = sb("cond_e", [P, KD * 2])
        row_sb = sb("ada_rows", [2, NM])
        row_ps = ctx.enter_context(nc.psum_tensor("ada_row_ps", [2, NM], F32))
        ps = ctx.enter_context(nc.psum_tensor("ada_ps", [P, 512], F32))
        const_in, e_done, silu_step = sem("m_const_in"), sem("m_e"), sem("m_silu_step")
        w_in = [sem(f"m_w_in{s}") for s in range(SLOTS)]
        w_used = sem("m_w_used")
        ident_set, turn_step = sem("m_ident"), sem("m_turn_step")
        rows_in = [sem(f"m_rows_in{s}") for s in range(2)]
        w_hi_set, w_lo_set, xt_in = sem("m_w_hi"), sem("m_w_lo"), sem("m_xt_in")
        block = ctx.enter_context(nc.Block())

        @block.sync
        def _(sp):
            sp.dma_start(cond[:, :], a["cond"]).then_inc(const_in, 16)
            sp.dma_start(g.b_ada[:, :], a["b_ada"]).then_inc(const_in, 16)
            sp.dma_start(g.gcol[:, :], a["gcol"]).then_inc(const_in, 16)
            def w_in_rows(k):
                need(sp, w_lo_set, k - 1)
                sp.dma_start(rows[k % 2][:, :], a["w_in"][k * P:(k + 1) * P, :]).then_inc(rows_in[k % 2], 16)
            for k in range(KD):
                s = k % SLOTS
                if k >= SLOTS:
                    sp.wait_ge(w_used, k - SLOTS + 1)
                sp.dma_start(w[:, s, :], a["w_ada"][k * P:(k + 1) * P, 0:NM]).then_inc(w_in[s], 16)
                if k >= 2:
                    w_in_rows(k - 2)
            for k in (KD - 2, KD - 1):
                w_in_rows(k)
            for n in range(CT):
                sp.dma_start(g.xt[n][:, :, :], a["ctx_t"][n]).then_inc(xt_in, 16)
            sp.wait_ge(xt_in, 16 * CT)
            sp.wait_ge(const_in, 48)

        @block.gpsimd
        def _(pool):
            nc.gpsimd.memset(g.ident[:, :], 0.0).then_inc(ident_set, 1)
            nc.gpsimd.memset(g.ones[:, :], 1.0).then_inc(ident_set, 1)
            pool.wait_ge(ident_set, 2)
            nc.gpsimd.affine_select(out=g.ident[:, :], in_=g.ident[:, :], compare_op=ALU.not_equal, fill=1.0,
                                    base=0, pattern=[[-1, P]], channel_multiplier=1).then_inc(ident_set, 1)

        @block.scalar
        def _(act):
            act.wait_ge(const_in, 48)
            nc.scalar.activation(en[:, :], cond[:, :], ACT.Exp, scale=-1.0).then_inc(e_done, 1)
            act.wait_ge(ident_set, 3)
            nc.scalar.activation(g.ident_r[:, :], g.ident[:, :], ACT.Copy).then_inc(e_done, 1)
            for k in range(KD):
                act.wait_ge(rows_in[k % 2], 16 * (k // 2 + 1))
                nc.scalar.activation(g.w_hi[:, k], rows[k % 2][:, :], ACT.Copy).then_inc(w_hi_set, 1)
                if k == KD - 3:
                    act.wait_ge(w_used, KD)
                    nc.scalar.activation(row_sb[:, :], row_ps[:, :], ACT.Copy).then_inc(turn_step, 1)

        @block.vector
        def _(dve):
            dve.wait_ge(e_done, 1)
            nc.vector.tensor_scalar(en[:, :], en[:, :], 1.0, None, ALU.add).then_inc(silu_step, 1)
            dve.wait_ge(silu_step, 1)
            nc.vector.reciprocal(en[:, :], en[:, :]).then_inc(silu_step, 1)
            dve.wait_ge(silu_step, 2)
            nc.vector.tensor_tensor(g.cond[:, :], cond[:, :], en[:, :], ALU.mult).then_inc(silu_step, 1)
            for k in range(KD):
                dve.wait_ge(w_hi_set, k + 1)
                nc.vector.tensor_tensor(g.w_lo[:, k], rows[k % 2][:, :], g.w_hi[:, k], ALU.subtract).then_inc(w_lo_set, 1)
            dve.wait_ge(const_in, 48)
            dve.wait_ge(turn_step, 2)
            nc.vector.tensor_tensor(g.mods[:, 0:16, :], ps[:, 0:32].rearrange("p (m c) -> p m c", c=2),
                                    g.b_ada[:, 0:16, None].to_broadcast([P, 16, 2]), ALU.add).then_inc(turn_step, 1)
            dve.wait_ge(turn_step, 3)
            nc.vector.tensor_scalar(g.mods[:, 8:16, :], g.mods[:, 8:16, :], 1.0, None, ALU.add).then_inc(turn_step, 1)

        @block.tensor
        def _(pe):
            pe.wait_ge(silu_step, 3)
            for k in range(KD):
                pe.wait_ge(w_in[k % SLOTS], 16 * (k // SLOTS + 1))
                for c in range(0, NM, 512):
                    mm = nc.tensor.matmul(row_ps[:, c:c + 512], g.cond[:, 2 * k:2 * k + 2], w[:, k % SLOTS, c:c + 512],
                                          start=(k == 0), stop=(k == KD - 1))
                mm.then_inc(w_used, 1)
            pe.wait_ge(turn_step, 1)
            pe.wait_ge(ident_set, 3)
            for c in range(NM // P):
                mm = nc.tensor.transpose(ps[:, 2 * c:2 * c + 2], row_sb[:, c * P:(c + 1) * P], g.ident[0:2, 0:2])
            mm.then_inc(turn_step, 1)


def stage_project(nc, g, a):
    with ExitStack() as ctx:
        sb = lambda n, s, d=F32: ctx.enter_context(nc.sbuf_tensor(n, s, d))
        ps = lambda n, s: ctx.enter_context(nc.psum_tensor(n, s, F32))
        sem = lambda n: ctx.enter_context(nc.semaphore("p_" + n))
        w_hi, w_lo = g.w_hi, g.w_lo
        xt = g.xt
        u_hi = [sb(f"u_hi{i}", [P, KD, P], F32R) for i in range(2)]
        u_lo = [sb(f"u_lo{i}", [P, KD, P], F32R) for i in range(2)]
        h = [sb(f"h{i}", [P, NCOL]) for i in range(2)]
        sq = sb("sq", [P, NORM])
        g_row = sb("g_row", [P, 8 * DH])
        cs = sb("cs", [P, TT, 96])
        rt = sb("rope_t", [P, 4, 256])
        kpt = sb("kpe_t", [P, 4, 16])
        rot = sb("rot", [P, 8 * DH])
        kper = sb("kper", [P, ROPE])
        conv_p = sb("conv_p", [P, CW])
        ss, var, rstd, tmp = (sb(n, [P, 10]) for n in ("ss", "var", "rstd", "ntmp"))
        inv_n = sb("inv_n", [P, 10])
        a_hi, a_lo = sb("a_hi", [P, 3, P], F32R), sb("a_lo", [P, 3, P], F32R)
        b_hi, b_lo = sb("b_hi", [P, 4, P], F32R), sb("b_lo", [P, 4, P], F32R)
        c_st = sb("c_st", [P, 4, P])
        k_hi, k_lo = sb("k_hi", [ROPE, P], F32R), sb("k_lo", [ROPE, P], F32R)
        v_st = sb("v_st", [P, 2, P], F32R)
        main = ps("p_main", [P, 4, 512])
        tr_a, tr_b, tr_c, tr_k = (ps(n, [P, 512]) for n in ("tr_a", "tr_b", "tr_c", "tr_k"))

        tables_in = sem("tables_in")
        x_in = [sem(f"x_in{s}") for s in range(2)]
        modulated, uhi_set, ulo_set = sem("modulated"), sem("uhi"), sem("ulo")
        bank_done, bank_out = sem("bank_done"), sem("bank_out")
        squared, var_set, std_set, step = sem("squared"), sem("var_set"), sem("std_set"), sem("dve_step")
        normed, rotated, pool_step, pool_done = sem("normed"), sem("rotated"), sem("pool_step"), sem("pool_done")
        turned, hi_out, lo_out, stored = sem("turned"), sem("hi_out"), sem("lo_out"), sem("stored")
        v_hi_set, v_lo_set = sem("v_hi"), sem("v_lo")
        block = ctx.enter_context(nc.Block())

        STORES_C, STORES_X = 7, 13
        STEPS_C, STEPS_X = 9, 11

        def before(n, per_ctx, per_x):
            if isinstance(n, int) and n < CT:
                return per_ctx * n
            return (n - CT) * per_x + per_ctx * CT

        banks_before = lambda n: before(n, 1, len(BANKS))
        stores_before = lambda n: before(n, 16 * STORES_C, 16 * STORES_X)

        def schedule(eng, split, work, out, in_halves=False):
            split(0, 0, 0)

            def step(i, c):
                n = i * 2 + c
                if c < CT + TT - 1:
                    split(n + 1, c + 1, i + (c + 1) // 2)
                work(n, c, c >= CT)
                if c:
                    out(n - 1, c - 1, c > CT)
            for c in range(CT + 1):
                step(0, c)
            with eng.Fori(0, (TT - 2) // 2) as i:
                step(i, CT + 1)
                step(i, CT + 2)
            n = CT + TT - 1
            if in_halves:
                work(n, n, True, 0)
            out(n - 1, n - 1, True)
            if in_halves:
                work(n, n, True, 1)
            else:
                work(n, n, True)
            out(n, n, True)

        @block.sync
        def _(sp):
            sp.dma_start(g_row[:, :], a["g_heads"]).then_inc(tables_in, 16)
            sp.dma_start(inv_n[:, :], a["inv_n"]).then_inc(tables_in, 16)
            sp.dma_start(cs[:, :, :], a["cs_tok"]).then_inc(tables_in, 16)
            for n in range(CT):
                sp.sem_inc(x_in[n], 16)

            def load(n, c):
                sp.wait_ge(ulo_set, n - 1)
                s = c % 2
                sp.dma_start(xt[s][:, :, :], a["x_t"][bass.ds(n - CT, 1)].rearrange("o p k t -> p (o k) t")).then_inc(x_in[s], 16)

            def store(n, is_x):
                sp.wait_ge(hi_out, n + 1)
                sp.wait_ge(lo_out, n + 1)
                sp.wait_ge(v_lo_set, n + 1)
                raw = lambda t: t.bitcast(F32)
                tok = bass.ds(n * P, P)
                for part, (ta, tb, tk) in enumerate(((a_hi, b_hi, k_hi), (a_lo, b_lo, k_lo))):
                    sp.dma_start(g.ckv[part][:, tok], raw(ta[:, 0])).then_inc(stored, 16)
                    sp.dma_start(g.kg[part][:, tok], raw(tb[:, 0])).then_inc(stored, 16)
                    sp.dma_start(g.kpe[part][:, tok], raw(tk[:, :])).then_inc(stored, 16)
                sp.dma_start(g.vg[:, bass.ds(n, 1)].rearrange("p o a c -> p (o a) c"), raw(v_st[:, :, :])).then_inc(stored, 16)
                if is_x:
                    q = bass.ds((n - CT) * P, P)
                    for part, (ta, tb) in enumerate(((a_hi, b_hi), (a_lo, b_lo))):
                        sp.dma_start(g.cq[part][:, :, q].rearrange("c p t -> p c t"), raw(ta[:, 1:3])).then_inc(stored, 16)
                        sp.dma_start(g.qg[part][:, q].rearrange("(c p) t -> p c t", p=P), raw(tb[:, 1:4])).then_inc(stored, 16)
                    sp.dma_start(g.conv_p[:, :, q].rearrange("c p t -> p c t"), c_st[:, 0:2]).then_inc(stored, 16)
                    sp.dma_start(g.conv_b[:, :, q].rearrange("c p t -> p c t"), c_st[:, 2:4]).then_inc(stored, 16)

            def step(i, c):
                n = i * 2 + c
                if c < CT + TT - 2:
                    load(n + 2, c)
                if c:
                    store(n - 1, c > CT)
            for c in range(CT + 1):
                step(0, c)
            with sp.Fori(0, (TT - 4) // 2) as i:
                step(i, CT + 1)
                step(i, CT + 2)
            for c in range(CT + TT - 3, CT + TT):
                step(0, c)
            store(CT + TT - 1, True)
            sp.wait_ge(stored, stores_before(CT + TT))

        @block.scalar
        def _(act):
            def split(n, c, pair):
                act.wait_ge(modulated, n + 1)
                need(act, bank_done, banks_before(n - 1))
                nc.scalar.activation(u_hi[c % 2][:, :, :], xt[c % 2][:, :, :], ACT.Copy).then_inc(uhi_set, 1)

            def work(n, c, is_x):
                at, hs = banks_before(n), h[c % 2]
                banks = len(BANKS) if is_x else 1
                need(act, turned, n - 1)
                need(act, v_lo_set, n - 1)
                for b in range(banks):
                    act.wait_ge(bank_done, at + (b + 1))
                    c0, cn = BANKS[b]
                    nc.scalar.activation(hs[:, c0:c0 + cn], main[:, b, 0:cn], ACT.Copy).then_inc(bank_out, 1)
                act.wait_ge(bank_out, at + banks)
                need(act, var_set, n)
                width = NORM if is_x else KVR + HKV * DH
                nc.scalar.activation(sq[:, 0:width], hs[:, O_CKV:O_CKV + width], ACT.Square).then_inc(squared, 1)
                act.wait_ge(var_set, n + 1)
                nc.scalar.activation(rstd[:, :], var[:, :], ACT.Sqrt).then_inc(std_set, 1)

            def out(n, c, is_x):
                act.wait_ge(turned, n + 1)
                need(act, stored, stores_before(n))
                for q in range(3 if is_x else 1):
                    nc.scalar.activation(a_hi[:, q], tr_a[:, q * P:(q + 1) * P], ACT.Copy, scale=g.gcol[:, q:q + 1])
                nb = 4 if is_x else 1
                nc.scalar.activation(b_hi[:, 0:nb], tr_b[:, 0:nb * P].rearrange("p (c t) -> p c t", t=P), ACT.Copy)
                if is_x:
                    nc.scalar.activation(c_st[:, :], tr_c[:, :].rearrange("p (c t) -> p c t", t=P), ACT.Copy)
                nc.scalar.activation(k_hi[:, :], tr_k[0:ROPE, 0:P], ACT.Copy).then_inc(hi_out, 1)
                nc.scalar.activation(v_st[:, 0, :], h[c % 2][:, O_GV:O_GV + P], ACT.Copy).then_inc(v_hi_set, 1)
            schedule(act, split, work, out)

        @block.vector
        def _(dve):
            nc.vector.memset(ss[:, :], 1.0).then_inc(normed, 1)
            dve.wait_ge(normed, 1)

            def split(n, c, pair):
                s, who = c % 2, 1 if c < CT else 0
                dve.wait_ge(x_in[s], pair * 16 + 16)
                for k in range(KD):
                    last = nc.vector.tensor_scalar(xt[s][:, k], xt[s][:, k], g.mods[:, 8 + k, who:who + 1],
                                                   g.mods[:, k, who:who + 1], ALU.mult, ALU.add)
                last.then_inc(modulated, 1)

            def work(n, c, is_x):
                if isinstance(n, int) and n == 0:
                    dve.wait_ge(tables_in, 48)
                at, seen = before(n, STEPS_C, STEPS_X), [0]

                def link(ins):
                    seen[0] += 1
                    ins.then_inc(step, 1)
                    dve.wait_ge(step, at + seen[0])
                hs, heads = h[c % 2], 8 if is_x else HKV
                by_head = lambda t: t.rearrange("p (h d) -> p h d", d=DH)
                dve.wait_ge(squared, n + 1)
                link(nc.vector.reduce_sum(ss[:, 0:1], sq[:, 0:KVR], AX.X))
                link(nc.vector.reduce_sum(ss[:, 1:1 + heads], by_head(sq[:, KVR:KVR + heads * DH]), AX.X))
                if is_x:
                    link(nc.vector.reduce_sum(ss[:, 9:10], sq[:, NORM - QR:NORM], AX.X))
                link(nc.vector.tensor_tensor(tmp[:, :], ss[:, :], inv_n[:, :], ALU.mult))
                nc.vector.tensor_scalar(var[:, :], tmp[:, :], EPS, None, ALU.add).then_inc(var_set, 1)
                dve.wait_ge(std_set, n + 1)
                link(nc.vector.reciprocal(rstd[:, :], rstd[:, :]))
                link(nc.vector.tensor_tensor(tmp[:, :], rstd[:, :], rstd[:, :], ALU.mult))
                link(nc.vector.tensor_tensor(tmp[:, :], tmp[:, :], var[:, :], ALU.mult))
                link(nc.vector.tensor_scalar(tmp[:, :], tmp[:, :], -0.5, 1.5, ALU.mult, ALU.add))
                link(nc.vector.tensor_tensor(rstd[:, :], rstd[:, :], tmp[:, :], ALU.mult))
                ghs = hs[:, O_GK:O_GK + heads * DH]
                link(nc.vector.tensor_tensor(by_head(ghs), by_head(ghs), rstd[:, 1:1 + heads, None].to_broadcast([P, heads, DH]), ALU.mult))
                ckv, cq = hs[:, O_CKV:O_CKV + KVR], hs[:, O_CQ:O_CQ + QR]
                nc.vector.tensor_scalar(ckv, ckv, rstd[:, 0:1], None, ALU.mult)
                need(dve, turned, n)
                if not is_x:
                    nc.vector.tensor_tensor(rot[:, 0:heads * DH], ghs, g_row[:, 0:heads * DH], ALU.mult).then_inc(rotated, 1)
                    assert seen[0] == STEPS_C
                    return
                nc.vector.tensor_scalar(cq, cq, rstd[:, 9:10], None, ALU.mult)
                nc.vector.tensor_tensor(ghs, ghs, g_row[:, :], ALU.mult).then_inc(normed, 1)
                dve.wait_ge(normed, n - CT + 2)
                pairs = ghs.rearrange("p (h f two) -> p h f two", h=8, two=2)
                cos = cs[:, bass.ds(n - CT, 1), 0:32].to_broadcast([P, 8, 32])
                sin = cs[:, bass.ds(n - CT, 1), 32:64].to_broadcast([P, 8, 32])
                part = lambda q: rt[:, q].rearrange("p (h f) -> p h f", h=8)
                nc.vector.tensor_tensor(part(0), pairs[:, :, :, 0], cos, ALU.mult)
                link(nc.vector.tensor_tensor(part(1), pairs[:, :, :, 1], sin, ALU.mult))
                turned_pairs = rot[:, :].rearrange("p (h f two) -> p h f two", h=8, two=2)
                nc.vector.tensor_tensor(turned_pairs[:, :, :, 0], part(0), part(1), ALU.subtract).then_inc(rotated, 1)
                assert seen[0] == STEPS_X

            def out(n, c, is_x):
                dve.wait_ge(hi_out, n + 1)
                for q in range(3 if is_x else 1):
                    nc.vector.scalar_tensor_tensor(out=a_lo[:, q], in0=tr_a[:, q * P:(q + 1) * P], scalar=g.gcol[:, q:q + 1],
                                                   in1=a_hi[:, q], op0=ALU.mult, op1=ALU.subtract)
                nb = 4 if is_x else 1
                nc.vector.tensor_tensor(b_lo[:, 0:nb], tr_b[:, 0:nb * P].rearrange("p (c t) -> p c t", t=P), b_hi[:, 0:nb], ALU.subtract)
                nc.vector.tensor_tensor(k_lo[:, :], tr_k[0:ROPE, 0:P], k_hi[:, :], ALU.subtract).then_inc(lo_out, 1)
            schedule(dve, split, work, out)

        @block.gpsimd
        def _(pool):

            def split(n, c, pair):
                pool.wait_ge(uhi_set, n + 1)
                nc.gpsimd.tensor_tensor(u_lo[c % 2][:, :, :], xt[c % 2][:, :, :], u_hi[c % 2][:, :, :], ALU.subtract).then_inc(ulo_set, 1)

            def work(n, c, is_x):
                if isinstance(n, int) and n == 0:
                    pool.wait_ge(tables_in, 48)
                hs = h[c % 2]
                pool.wait_ge(squared, n + 1)
                need(pool, turned, n)
                key = hs[:, O_KPE:O_KPE + ROPE].rearrange("p (f two) -> p f two", two=2)
                if not is_x:
                    nc.gpsimd.tensor_copy(kper[:, 0:16], key[:, :, 0])
                    nc.gpsimd.tensor_copy(kper[:, 16:32], key[:, :, 1]).then_inc(pool_done, 1)
                    return
                nc.gpsimd.tensor_tensor(conv_p[:, :], hs[:, O_CC:O_CC + CW], hs[:, O_CH:O_CH + CW], ALU.mult)
                kcos, ksin = (cs[:, bass.ds(n - CT, 1), f:f + 16].rearrange("p o f -> p (o f)") for f in (64, 80))
                nc.gpsimd.tensor_tensor(kpt[:, 0], key[:, :, 0], kcos, ALU.mult)
                nc.gpsimd.tensor_tensor(kpt[:, 1], key[:, :, 1], ksin, ALU.mult)
                nc.gpsimd.tensor_tensor(kpt[:, 2], key[:, :, 0], ksin, ALU.mult)
                nc.gpsimd.tensor_tensor(kpt[:, 3], key[:, :, 1], kcos, ALU.mult).then_inc(pool_step, 1)
                pool.wait_ge(pool_step, (n - CT) * 2 + 1)
                nc.gpsimd.tensor_tensor(kper[:, 0:16], kpt[:, 0], kpt[:, 1], ALU.subtract)
                nc.gpsimd.tensor_tensor(kper[:, 16:32], kpt[:, 2], kpt[:, 3], ALU.add)
                pool.wait_ge(normed, n - CT + 2)
                pairs = hs[:, O_GK:O_GK + 8 * DH].rearrange("p (h f two) -> p h f two", h=8, two=2)
                cos = cs[:, bass.ds(n - CT, 1), 0:32].to_broadcast([P, 8, 32])
                sin = cs[:, bass.ds(n - CT, 1), 32:64].to_broadcast([P, 8, 32])
                part = lambda q: rt[:, q].rearrange("p (h f) -> p h f", h=8)
                nc.gpsimd.tensor_tensor(part(2), pairs[:, :, :, 0], sin, ALU.mult)
                nc.gpsimd.tensor_tensor(part(3), pairs[:, :, :, 1], cos, ALU.mult).then_inc(pool_step, 1)
                pool.wait_ge(pool_step, (n - CT) * 2 + 2)
                turned_pairs = rot[:, :].rearrange("p (h f two) -> p h f two", h=8, two=2)
                nc.gpsimd.tensor_tensor(turned_pairs[:, :, :, 1], part(2), part(3), ALU.add).then_inc(pool_done, 1)

            def out(n, c, is_x):
                pool.wait_ge(v_hi_set, n + 1)
                nc.gpsimd.tensor_tensor(v_st[:, 1, :], h[c % 2][:, O_GV:O_GV + P], v_st[:, 0, :], ALU.subtract).then_inc(v_lo_set, 1)
            schedule(pool, split, work, out)

        @block.tensor
        def _(pe):

            def split(n, c, pair):
                pass

            def work(n, c, is_x, half=None):
                s = c % 2
                pe.wait_ge(uhi_set, n + 1)
                pe.wait_ge(ulo_set, n + 1)
                for b, (c0, cn) in enumerate(BANKS if is_x else BANKS[:1]):
                    if half is not None and b // 2 != half:
                        continue
                    if c > CT:
                        pe.wait_ge(bank_out, banks_before(n - 1) + (b + 1))
                    elif b == 0:
                        need(pe, bank_out, c)
                    for k in range(KD):
                        for lhs, rhs in ((u_hi, w_hi), (u_hi, w_lo), (u_lo, w_hi)):
                            mm = nc.tensor.matmul(main[:, b, 0:cn], lhs[s][:, k], rhs[:, k, c0:c0 + cn],
                                                  start=(k == 0 and rhs is w_hi and lhs is u_hi),
                                                  stop=(k == KD - 1 and lhs is u_lo))
                    mm.then_inc(bank_done, 1)

            def out(n, c, is_x):
                hs = h[c % 2]
                pe.wait_ge(rotated, n + 1)
                pe.wait_ge(pool_done, n + 1)
                need(pe, hi_out, n)
                need(pe, lo_out, n)
                turn = lambda ps_, src, m=P: nc.tensor.transpose(ps_, src, g.ident[:, :])
                turn(tr_a[:, 0:P], hs[:, O_CKV:O_CKV + P])
                turn(tr_b[:, 0:P], rot[:, 0:P])
                if is_x:
                    for q in range(2):
                        turn(tr_a[:, (1 + q) * P:(2 + q) * P], hs[:, O_CQ + q * P:O_CQ + (q + 1) * P])
                        turn(tr_c[:, q * P:(q + 1) * P], conv_p[:, q * P:(q + 1) * P])
                        turn(tr_c[:, (2 + q) * P:(3 + q) * P], hs[:, O_CB + q * P:O_CB + (q + 1) * P])
                    for q in range(1, 4):
                        turn(tr_b[:, q * P:(q + 1) * P], rot[:, q * P:(q + 1) * P])
                turn(tr_k[0:ROPE, 0:P], kper[:, :]).then_inc(turned, 1)
            schedule(pe, split, work, out, in_halves=True)


def stage_expand(nc, g, a):
    with ExitStack() as ctx:
        sb = lambda n, s, d=F32: ctx.enter_context(nc.sbuf_tensor("e_" + n, s, d))
        ps = lambda n, s: ctx.enter_context(nc.psum_tensor("e_" + n, s, F32))
        sem = lambda n: ctx.enter_context(nc.semaphore("e_" + n))
        UQ, UKV = 640, 768
        ckv_hi, ckv_lo = sb("ckv_hi", [P, KEYS], F32R), sb("ckv_lo", [P, KEYS], F32R)
        cq_hi = [sb(f"cq_hi{i}", [P, 2, QB], F32R) for i in range(NQB)]
        cq_lo = [sb(f"cq_lo{i}", [P, 2, QB], F32R) for i in range(NQB)]
        cs = [sb(f"cs{i}", [6 * 16, 2, QB]) for i in range(NQB)]
        raw_q, raw_kv = sb("raw_q", [P, 2, UQ]), sb("raw_kv", [P, UKV])
        uq_hi, uq_lo = sb("uq_hi", [P, 2, UQ], F32R), sb("uq_lo", [P, 2, UQ], F32R)
        ukv_hi, ukv_lo = sb("ukv_hi", [P, UKV], F32R), sb("ukv_lo", [P, UKV], F32R)
        st_hi, st_lo = sb("st_hi", [P, 2, 3, QB], F32R), sb("st_lo", [P, 2, 3, QB], F32R)
        rt, ro = sb("rt", [6 * 16, 4, QB]), sb("ro", [6 * 16, 2, QB])
        ro_hi, ro_lo = sb("ro_hi", [6 * 16, 2, QB], F32R), sb("ro_lo", [6 * 16, 2, QB], F32R)
        VG = 6
        NVG = KT // VG
        v_hi, v_lo = sb("v_hi", [P, 2, HM, VG, DH], F32R), sb("v_lo", [P, 2, HM, VG, DH], F32R)
        assert NVG < NQB and VG * P == CTX + QB
        M0, M1 = 40, 48
        HALVES = 2
        MH = (M1 - M0) // HALVES
        wa, ada_row = sb("wa", [P, KD, MH * P]), sb("ada_row", [2, MH * P])
        ring, rope_ps, v_ps, ada_ps = ps("ring", [P, 3, QB]), ps("rope", [P, 2, QB]), ps("v", [P, 2, QB]), ps("ada", [P, QB])

        w_in, ckv_in = sem("w_in"), [sem(f"ckv_in{i}") for i in range(2)]
        blk_in = [sem(f"blk_in{i}") for i in range(NQB)]
        wa_in = sem("wa_in")
        w_hi_set, w_lo_set = sem("w_hi_set"), sem("w_lo_set")
        tile_done, hi_set, lo_set = sem("tile_done"), sem("hi_set"), sem("lo_set")
        st_stored = [sem(f"st_stored{i}") for i in range(2)]
        rope_done, rope_mults, rope_set, rope_hi, rope_lo, rope_stored = (sem(n) for n in (
            "rope_done", "rope_mults", "rope_set", "rope_hi", "rope_lo", "rope_stored"))
        v_done, v_hi_set, v_lo_set = sem("v_done"), sem("v_hi_set"), sem("v_lo_set")
        v_stored = [sem(f"v_stored{i}") for i in range(2)]
        wa_used, ada_set = sem("wa_used"), sem("ada_set")
        block = ctx.enter_context(nc.Block())
        raw = lambda t: t.bitcast(F32)
        ITEMS = 6
        items_before = lambda b: b * ITEMS + 3

        @block.sync
        def _(sp):
            sp.dma_start(raw_kv[:, :], a["w_ukv"]).then_inc(w_in, 16)
            sp.dma_start(raw_q[:, :, :], a["w_uq"].rearrange("(k p) c -> p k c", p=P)).then_inc(w_in, 16)

            def load_ckv(part, cols):
                for half, t in enumerate((ckv_hi, ckv_lo)):
                    sp.dma_start(raw(t[:, cols]), g.ckv[half][:, cols]).then_inc(ckv_in[part], 16)

            def load(b):
                tok = slice(b * QB, (b + 1) * QB)
                for half, t in enumerate((cq_hi, cq_lo)):
                    sp.dma_start(raw(t[b][:, :, :]), g.cq[half][:, :, tok].rearrange("c p t -> p c t")).then_inc(blk_in[b], 16)
                sp.dma_start(cs[b][:, :, :], a["cs_rope"][:, :, tok]).then_inc(blk_in[b], 16)

            def load_wa(half):
                sp.dma_start(wa[:, :, :], a["w_ada"][:, (M0 + half * MH) * P:(M0 + (half + 1) * MH) * P].rearrange("(k p) c -> p k c", p=P)).then_inc(wa_in, 16)
            load_ckv(0, slice(0, CTX + QB))
            load(0)

            def store_set(kind, items, dst, tok):
                sp.wait_ge(lo_set, items)
                for half, t in enumerate((st_hi, st_lo)):
                    sp.dma_start(dst[half][:, tok].rearrange("(c p) t -> p c t", p=P), raw(t[:, kind, :, 0:tok.stop - tok.start])).then_inc(st_stored[kind], 16)
            store_set(1, 3, g.kn, slice(0, CTX))
            load_ckv(1, slice(CTX + QB, KEYS))
            load(1)
            for b in range(NQB):
                store_set(0, items_before(b) + 3, g.qn, slice(b * QB, (b + 1) * QB))
                store_set(1, items_before(b) + 6, g.kn, slice(CTX + b * QB, CTX + (b + 1) * QB))
                if b + 2 < NQB:
                    load(b + 2)
                if b == 0:
                    load_wa(0)
                sp.wait_ge(rope_lo, b + 1)
                for half, t in enumerate((ro_hi, ro_lo)):
                    sp.dma_start(g.qr[half][:, :, b * QB:(b + 1) * QB].rearrange("s p t -> p s t"), raw(t[:, :, :])).then_inc(rope_stored, 16)
                if b < NVG:
                    sp.wait_ge(v_lo_set, VG * (b + 1))
                    for half, t in enumerate((v_hi, v_lo)):
                        sp.dma_start(g.vm[half][:, :, b * VG:(b + 1) * VG, :].rearrange("h p t v -> p h (t v)"),
                                     raw(t[:, b % 2]).rearrange("p h t v -> p h (t v)")).then_inc(v_stored[b % 2], 16)
                if b == 1:
                    sp.wait_ge(wa_used, 1)
                    load_wa(1)
            sp.wait_ge(st_stored[0], 32 * NQB)
            sp.wait_ge(st_stored[1], 32 * (NQB + 1))
            sp.wait_ge(rope_stored, 32 * NQB)
            for s in range(2):
                sp.wait_ge(v_stored[s], 32 * ((NVG + 1 - s) // 2))

        @block.scalar
        def _(act):
            act.wait_ge(w_in, 32)
            nc.scalar.activation(ukv_hi[:, :], raw_kv[:, :], ACT.Copy).then_inc(w_hi_set, 1)
            nc.scalar.activation(uq_hi[:, :, :], raw_q[:, :, :], ACT.Copy).then_inc(w_hi_set, 1)

            def item(n, kind, c, former, width=QB):
                act.wait_ge(tile_done, n + 1)
                need(act, st_stored[kind], 32 * former)
                nc.scalar.activation(st_hi[:, kind, c, 0:width], ring[:, c, 0:width], ACT.Copy).then_inc(hi_set, 1)
            for c in range(3):
                item(c, 1, c, 0, CTX)
            for b in range(NQB):
                for c in range(ITEMS):
                    item(items_before(b) + c, c // 3, c % 3, b + c // 3)
                act.wait_ge(rope_set, b + 1)
                need(act, rope_stored, b * 32)
                nc.scalar.activation(ro_hi[:, :, :], ro[:, :, :], ACT.Copy).then_inc(rope_hi, 1)
                for t in range(b * VG, (b + 1) * VG) if b < NVG else ():
                    act.wait_ge(v_done, t + 1)
                    if b >= 2:
                        act.wait_ge(v_stored[b % 2], 32 * (b // 2))
                    nc.scalar.activation(v_hi[:, b % 2, :, t % VG, :], v_ps[:, t % 2, 0:HM * DH].rearrange("p (h v) -> p h v", v=DH), ACT.Copy).then_inc(v_hi_set, 1)

        @block.vector
        def _(dve):
            dve.wait_ge(w_hi_set, 2)
            nc.vector.tensor_tensor(ukv_lo[:, :], raw_kv[:, :], ukv_hi[:, :], ALU.subtract).then_inc(w_lo_set, 1)
            nc.vector.tensor_tensor(uq_lo[:, :, :], raw_q[:, :, :], uq_hi[:, :, :], ALU.subtract).then_inc(w_lo_set, 1)

            def item(n, kind, c, width=QB):
                dve.wait_ge(hi_set, n + 1)
                nc.vector.tensor_tensor(st_lo[:, kind, c, 0:width], ring[:, c, 0:width], st_hi[:, kind, c, 0:width], ALU.subtract).then_inc(lo_set, 1)
            for c in range(3):
                item(c, 1, c, CTX)

            def copy_row(half):
                dve.wait_ge(wa_used, 2 * half + 1)
                nc.vector.tensor_copy(ada_row[:, :], ada_ps[0:2, :]).then_inc(ada_set, 1)

            def add_bias(half):
                dve.wait_ge(wa_used, 2 * half + 2)
                m = slice(M0 + half * MH, M0 + (half + 1) * MH)
                nc.vector.tensor_tensor(g.mods[:, m, :], ada_ps[:, 0:2 * MH].rearrange("p (m c) -> p m c", c=2),
                                        g.b_ada[:, m, None].to_broadcast([P, MH, 2]), ALU.add).then_inc(ada_set, 1)
            for b in range(NQB):
                for c in range(ITEMS):
                    item(items_before(b) + c, c // 3, c % 3)
                dve.wait_ge(rope_done, b + 1)
                ev, od = rope_ps[0:96, 0, :], rope_ps[0:96, 1, :]
                cos, sin = cs[b][:, 0, :], cs[b][:, 1, :]
                need(dve, rope_lo, b)
                nc.vector.tensor_tensor(rt[:, 0], ev, cos, ALU.mult)
                nc.vector.tensor_tensor(rt[:, 1], od, sin, ALU.mult)
                nc.vector.tensor_tensor(rt[:, 2], ev, sin, ALU.mult)
                nc.vector.tensor_tensor(rt[:, 3], od, cos, ALU.mult).then_inc(rope_mults, 1)
                dve.wait_ge(rope_mults, b + 1)
                nc.vector.tensor_tensor(ro[:, 0], rt[:, 0], rt[:, 1], ALU.subtract)
                nc.vector.tensor_tensor(ro[:, 1], rt[:, 2], rt[:, 3], ALU.add).then_inc(rope_set, 1)
                dve.wait_ge(rope_hi, b + 1)
                need(dve, rope_stored, b * 32)
                nc.vector.tensor_tensor(ro_lo[:, :, :], ro[:, :, :], ro_hi[:, :, :], ALU.subtract).then_inc(rope_lo, 1)
                for t in range(b * VG, (b + 1) * VG) if b < NVG else ():
                    dve.wait_ge(v_hi_set, t + 1)
                    nc.vector.tensor_tensor(v_lo[:, b % 2, :, t % VG, :], v_ps[:, t % 2, 0:HM * DH].rearrange("p (h v) -> p h v", v=DH),
                                            v_hi[:, b % 2, :, t % VG, :], ALU.subtract).then_inc(v_lo_set, 1)
                if b >= 2:
                    add_bias(b - 2)
                if 1 <= b <= HALVES:
                    copy_row(b - 1)

        @block.tensor
        def _(pe):
            pe.wait_ge(w_lo_set, 2)
            pe.wait_ge(ckv_in[0], 32)

            def products(out, parts):
                for q, (sh, sl, mh, ml) in enumerate(parts):
                    for m, (x, y) in enumerate(((sh, mh), (sh, ml), (sl, mh))):
                        mm = nc.tensor.matmul(out, x, y, start=(q == 0 and m == 0), stop=(q == len(parts) - 1 and m == 2))
                return mm

            def k_tile(n, c, col, width):
                need(pe, lo_set, n - 2)
                w, tok = slice(c * P, (c + 1) * P), slice(col, col + width)
                products(ring[:, c, 0:width], [(ukv_hi[:, w], ukv_lo[:, w], ckv_hi[:, tok], ckv_lo[:, tok])]).then_inc(tile_done, 1)
            for c in range(3):
                k_tile(c, c, 0, CTX)

            def q_parts(b, c0):
                return [(uq_hi[:, k, c0:c0 + P], uq_lo[:, k, c0:c0 + P], cq_hi[b][:, k], cq_lo[b][:, k]) for k in range(2)]
            for b in range(NQB):
                pe.wait_ge(blk_in[b], 48)
                for c in range(3):
                    pe.wait_ge(lo_set, items_before(b) + c - 2)
                    products(ring[:, c, :], q_parts(b, c * P)).then_inc(tile_done, 1)
                if b == 1:
                    pe.wait_ge(ckv_in[1], 32)
                for c in range(3):
                    k_tile(items_before(b) + 3 + c, c, CTX + b * QB, QB)
                need(pe, rope_mults, b)
                products(rope_ps[:, 0, :], q_parts(b, 384))
                products(rope_ps[:, 1, :], q_parts(b, 512)).then_inc(rope_done, 1)
                for t in range(b * VG, (b + 1) * VG) if b < NVG else ():
                    need(pe, v_lo_set, t - 1)
                    k = slice(t * P, (t + 1) * P)
                    products(v_ps[:, t % 2, 0:HM * DH], [(ckv_hi[:, k], ckv_lo[:, k], ukv_hi[:, 384:], ukv_lo[:, 384:])]).then_inc(v_done, 1)
                if b >= 2:
                    pe.wait_ge(ada_set, 2 * (b - 2) + 1)
                    for c in range(MH):
                        mm = nc.tensor.transpose(ada_ps[:, 2 * c:2 * c + 2], ada_row[:, c * P:(c + 1) * P], g.ident[0:2, 0:2])
                    mm.then_inc(wa_used, 1)
                if 1 <= b <= HALVES:
                    need(pe, ada_set, 2 * (b - 1))
                    pe.wait_ge(wa_in, 16 * b)
                    for k in range(KD):
                        mm = nc.tensor.matmul(ada_ps[0:2, :], g.cond[:, 2 * k:2 * k + 2], wa[:, k, :], start=(k == 0), stop=(k == KD - 1))
                    mm.then_inc(wa_used, 1)



def stage_attend(nc, g, a):
    with ExitStack() as ctx:
        sb = lambda n, s, d=F32: ctx.enter_context(nc.sbuf_tensor("a_" + n, s, d))
        ps = lambda n, s: ctx.enter_context(nc.psum_tensor("a_" + n, s, F32))
        sem = lambda n: ctx.enter_context(nc.semaphore("a_" + n))
        STEPS = KT // 2
        HEAD = STEPS * NQB
        BODY = 2 * HEAD
        NB = 2 * NQB
        HEADS = HM
        mk_hi, mk_lo = sb("mk_hi", [QK + 1, KEYS], F32R), sb("mk_lo", [QK, KEYS], F32R)
        mq_hi, mq_lo = sb("mq_hi", [QK + 1, T], F32R), sb("mq_lo", [QK, T], F32R)
        gk_hh, gk_lo = sb("gk_hh", [P, KEYS], F32R), sb("gk_lo", [DH + 1, KEYS], F32R)
        gq_hl, gq_hm = sb("gq_hl", [P, T], F32R), sb("gq_hm", [DH + 1, T], F32R)
        v1 = [sb(f"v1_{i}", [P, KT, P], F32R) for i in range(2)]
        v0 = [sb(f"v0_{i}", [P, KT, P], F32R) for i in range(2)]
        pf = [sb(f"pf{i}", [P, 2 * QB]) for i in range(2)]
        p_hi = [sb(f"p_hi{i}", [P, 2 * QB], F32R) for i in range(3)]
        p_lo = [sb(f"p_lo{i}", [P, 2 * QB], F32R) for i in range(3)]
        o_sb = sb("o_sb", [P, QB])
        o_out = sb("o_out", [P, 4, DH])
        rden = sb("rden", [P, 4])
        mpart, mneg = sb("mpart", [P, 4, 5]), sb("mneg", [P, 4])
        mcol = [sb("mcol_m", [P, 4, P], F32R), sb("mcol_g", [P, 4, P], F32R)]
        M0, MT = 16, 4
        wa, ada_row = sb("wa", [P, KD, MT * P]), sb("ada_row", [2, MT * P])
        CQ = 512
        cp = [sb(f"cp{i}", [P, CQ + 2]) for i in range(2)]
        cb, cy = ([sb(f"{n}{i}", [P, CQ]) for i in range(2)] for n in ("cb", "cy"))
        c_hi, ct = [sb(f"c_hi{i}", [P, CQ], F32R) for i in range(2)], sb("ct", [P, CQ])
        sc = [ps(f"sc{i}", [P, 2 * QB]) for i in range(2)]
        mx = [ps(f"mx{i}", [P, QB]) for i in range(2)]
        o_ps, t_ps = ps("o", [P, QB]), ps("t", [P, QB])
        CHUNKS = [(k, min(QB, KEYS - k)) for k in range(0, KEYS, QB)]
        ITEMS = [(s, k) for s in range(4) for k in range(len(CHUNKS))]
        NI = len(ITEMS) + 1
        assert NI % 2 == 1 and BODY % 6 == 0

        consts = sem("consts")
        in_mh, in_ml, in_mv, in_g = sem("in_mh"), sem("in_ml"), sem("in_mv"), sem("in_g")
        scored, exped, hi_set, lo_set, pv_done = sem("scored"), sem("exped"), sem("hi_set"), sem("lo_set"), sem("pv_done")
        mx_done, mx_read, max_set, col_set, row_set = (sem(n) for n in ("mx_done", "mx_read", "max_set", "col_set", "row_set"))
        o_copied, o_turned, den_set, o_set, o_stored = (sem(n) for n in ("o_copied", "o_turned", "den_set", "o_set", "o_stored"))
        wa_in = sem("wa_in")
        cv_in = [sem(f"cv_in{i}") for i in range(2)]
        cv_step, cv_stored = sem("cv_step"), [sem(f"cv_stored{i}") for i in range(2)]
        ada_done, ada_set = sem("ada_done"), sem("ada_set")
        block = ctx.enter_context(nc.Block())
        raw = lambda t: t.bitcast(F32)
        SCALES = (float(QK) ** -0.5, float(DH) ** -0.5)
        LOADS_MQ, LOADS_MV, LOADS_G = 4, 2, 8
        KPE = 2

        @block.sync
        def _(sp):
            sp.dma_start(raw(mk_hi[NOPE:QK, :]), g.kpe[0]).then_inc(in_mh, 16)
            sp.dma_start(raw(mk_lo[NOPE:QK, :]), g.kpe[1]).then_inc(in_mh, 16)

            def load_m(h):
                rows = slice(h * NOPE, (h + 1) * NOPE)
                for part, (k, q, done) in enumerate(((mk_hi, mq_hi, in_mh), (mk_lo, mq_lo, in_ml))):
                    sp.dma_start(raw(k[0:NOPE, :]), g.kn[part][rows]).then_inc(done, 16)
                    sp.dma_start(raw(q[0:NOPE, :]), g.qn[part][rows]).then_inc(done, 16)
                    for r in range(2):
                        sp.dma_start(raw(q[NOPE + 16 * r:NOPE + 16 * (r + 1), :]), g.qr[part][r][h * 16:(h + 1) * 16]).then_inc(done, 16)
                for part, v in enumerate((v1[0], v0[0])):
                    sp.dma_start(raw(v[:, :, 0:DH]), g.vm[part][h]).then_inc(in_mv, 16)

            def load_g(h):
                kv = h // (HG // HKV)
                rows, krows = slice(h * DH, (h + 1) * DH), slice(kv * DH, (kv + 1) * DH)
                sp.dma_start(raw(gk_hh[0:DH, :]), g.kg[0][krows]).then_inc(in_g, 16)
                sp.dma_start(raw(gk_hh[DH:P, :]), g.kg[0][krows]).then_inc(in_g, 16)
                sp.dma_start(raw(gk_lo[0:DH, :]), g.kg[1][krows]).then_inc(in_g, 16)
                sp.dma_start(raw(gq_hl[0:DH, :]), g.qg[0][rows]).then_inc(in_g, 16)
                sp.dma_start(raw(gq_hl[DH:P, :]), g.qg[1][rows]).then_inc(in_g, 16)
                sp.dma_start(raw(gq_hm[0:DH, :]), g.qg[0][rows]).then_inc(in_g, 16)
                for part, v in enumerate((v1[1], v0[1])):
                    sp.dma_start(raw(v[:, :, 0:DH]), g.vg[:, :, part, krows]).then_inc(in_g, 16)

            def store(i, nb):
                sp.wait_ge(o_set, i * NB + nb + 1)
                col = (i if nb < NQB else HM + i) * DH
                row = (nb % NQB) * QB
                sp.dma_start(g.mix[row:row + QB, col:col + DH].rearrange("(s p) v -> p s v", p=P), o_out[:, :, :]).then_inc(o_stored, 16)
            def load_wa(i):
                col = (M0 + MT * i) * P
                sp.dma_start(wa[:, :, :], a["w_ada"][:, col:col + MT * P].rearrange("(k p) c -> p k c", p=P)).then_inc(wa_in, 16)
            sp.sem_inc(o_stored, 16)
            load_m(0)
            load_g(0)
            load_wa(0)
            for i in range(HEADS):
                for nb in range(NQB):
                    store(i, nb)
                sp.wait_ge(pv_done, i * BODY + HEAD)
                load_m((i + 1) % HEADS)
                if i == HEADS - 1:
                    for k, row in enumerate(g.rows):
                        sp.dma_start(row[:, :], a["w_o"][k * P:(k + 1) * P, :]).then_inc(in_g, 16)
                for nb in range(NQB, NB):
                    store(i, nb)
                if i + 1 < HEADS:
                    sp.wait_ge(ada_done, 2 * i + 2)
                    load_wa(i + 1)
                    load_g(i + 1)
            sp.wait_ge(o_stored, 16 * HEADS * NB + 16)
            sp.wait_ge(in_mh, 16 * (LOADS_MQ * (HEADS + 1) + KPE))
            sp.wait_ge(in_ml, 16 * LOADS_MQ * (HEADS + 1))
            sp.wait_ge(in_mv, 16 * LOADS_MV * (HEADS + 1))
            sp.wait_ge(in_g, 16 * (LOADS_G * HEADS + len(g.rows)))

        @block.gpsimd
        def _(pool):
            for i in range(2):
                nc.gpsimd.memset(raw(v1[i][:, :, DH:P]), 1.0)
                nc.gpsimd.memset(raw(v0[i][:, :, DH:P]), 0.0).then_inc(consts, 1)

            parts = [(c, q) for c in range(CW // P) for q in range(T // CQ)]
            steps = [0]

            def link(ins):
                steps[0] += 1
                ins.then_inc(cv_step, 1)
                pool.wait_ge(cv_step, steps[0])

            def load_part(n):
                (c, q), s = parts[n], n % 2
                first, last = q * CQ - 1, (q + 1) * CQ + 1
                lo, hi = max(first, 0), min(last, T)
                if n >= 2:
                    pool.wait_ge(cv_stored[s], 32 * (n // 2))
                for missing in ([0] if first < 0 else []) + ([CQ + 1] if last > T else []):
                    link(nc.gpsimd.memset(cp[s][:, missing:missing + 1], 0.0))
                pool.dma_start(cp[s][:, lo - first:hi - first], g.conv_p[c][:, lo:hi]).then_inc(cv_in[s], 16)
                pool.dma_start(cb[s][:, :], g.conv_b[c][:, q * CQ:(q + 1) * CQ]).then_inc(cv_in[s], 16)
            load_part(0)
            for n, (c, q) in enumerate(parts):
                s = n % 2
                tap = lambda k: g.gcol[:, 3 + 3 * c + k:4 + 3 * c + k].to_broadcast([P, CQ])
                if n + 1 < len(parts):
                    load_part(n + 1)
                pool.wait_ge(cv_in[s], 32 * (n // 2 + 1))
                y = cy[s]
                link(nc.gpsimd.tensor_tensor(y[:, :], cp[s][:, 0:CQ], tap(0), ALU.mult))
                for k in (1, 2):
                    link(nc.gpsimd.tensor_tensor(ct[:, :], cp[s][:, k:k + CQ], tap(k), ALU.mult))
                    link(nc.gpsimd.tensor_tensor(y[:, :], y[:, :], ct[:, :], ALU.add))
                link(nc.gpsimd.tensor_tensor(y[:, :], y[:, :], cb[s][:, :], ALU.mult))
                link(nc.gpsimd.tensor_copy(c_hi[s][:, :], y[:, :]))
                link(nc.gpsimd.tensor_tensor(y[:, :], y[:, :], c_hi[s][:, :], ALU.subtract))
                tok = slice(q * CQ, (q + 1) * CQ)
                pool.dma_start(g.co[0][c][:, tok], raw(c_hi[s][:, :])).then_inc(cv_stored[s], 16)
                pool.dma_start(g.co[1][c][:, tok], y[:, :]).then_inc(cv_stored[s], 16)
            for s in range(2):
                pool.wait_ge(cv_stored[s], 32 * (len(parts) // 2))

        def each_turn(eng, body):
            with eng.Fori(0, HEADS) as i:
                body(i)

        item_no = lambda i, nb, c: i * (NI * NB) + (NI * (nb + 1) + c)
        reads_no = lambda i, nb, c: i * ((NI - 1) * NB) + ((NI - 1) * (nb + 1) + c)
        ITEM_STEPS = [range(3 * t, min(3 * t + 3, NI - 1)) for t in range(7)]
        ADA = 2
        is_mla = lambda nb: nb % NB < NQB

        @block.scalar
        def _(act):
            def row(i, nb):
                n = item_no(i, nb, NI - 1)
                act.wait_ge(mx_done, n + 1)
                q = slice(((nb + 1) % NQB) * QB, ((nb + 1) % NQB + 1) * QB)
                bank = mx[(NI * (nb + 1) + NI - 1) % 2]
                if is_mla(nb + 1):
                    nc.scalar.activation(mq_hi[QK:QK + 1, q], bank[QK:QK + 1, :], ACT.Copy).then_inc(row_set, 1)
                else:
                    nc.scalar.activation(gq_hm[DH:DH + 1, q], bank[DH:DH + 1, :], ACT.Copy).then_inc(row_set, 1)
            row(0, -1)

            def copy_o(i, nb):
                act.wait_ge(pv_done, i * BODY + STEPS * (nb + 1))
                if nb:
                    act.wait_ge(o_turned, i * NB + nb)
                nc.scalar.activation(o_sb[:, :], o_ps[:, :], ACT.Copy).then_inc(o_copied, 1)

            def body(i):
                for st in range(BODY):
                    nb, kp = divmod(st, STEPS)
                    n = i * BODY + st
                    if kp == 2 and nb:
                        copy_o(i, nb - 1)
                    if kp == 8:
                        row(i, nb)
                    act.wait_ge(scored, n + 1)
                    if st >= 2:
                        act.wait_ge(lo_set, n - 1)
                    nc.scalar.activation(pf[st % 2][:, :], sc[st % 2][:, :], ACT.Exp, scale=SCALES[nb // NQB]).then_inc(exped, 1)
                    act.wait_ge(exped, n + 1)
                    if st >= 3:
                        act.wait_ge(pv_done, n - 2)
                    nc.scalar.activation(p_hi[st % 3][:, :], pf[st % 2][:, :], ACT.Copy).then_inc(hi_set, 1)
                copy_o(i, NB - 1)
            each_turn(act, body)

        @block.vector
        def _(dve):
            nc.vector.memset(raw(mcol[0][:, :, :]), 0.0)
            nc.vector.memset(raw(mcol[1][:, :, :]), 0.0).then_inc(col_set, 1)
            nc.vector.memset(raw(mk_hi[QK:QK + 1, :]), 1.0)
            nc.vector.memset(raw(gk_lo[DH:DH + 1, :]), 1.0).then_inc(consts, 1)
            dve.wait_ge(col_set, 1)

            def read_max(i, nb, c):
                s, k = ITEMS[c]
                dve.wait_ge(mx_done, item_no(i, nb, c) + 1)
                width = CHUNKS[k][1]
                ins = nc.vector.reduce_max(mpart[:, s, k:k + 1], mx[(NI * (nb + 1) + c) % 2][:, 0:width], AX.X)
                ins.then_inc(mx_read, 1)

            def columns(i, nb):
                b = i * NB + nb
                dve.wait_ge(mx_read, reads_no(i, nb, NI - 1))
                nc.vector.reduce_max(mneg[:, :], mpart[:, :, :], AX.X).then_inc(max_set, 1)
                dve.wait_ge(max_set, b + 2)
                col = QK if is_mla(nb + 1) else DH
                nc.vector.tensor_scalar(mcol[0 if is_mla(nb + 1) else 1][:, :, col], mneg[:, :], -1.0, None, ALU.mult).then_inc(col_set, 1)
            for c in range(NI - 1):
                read_max(0, -1, c)
            columns(0, -1)

            def low(i, st):
                n = i * BODY + st
                dve.wait_ge(hi_set, n + 1)
                nc.vector.tensor_tensor(p_lo[st % 3][:, :], pf[st % 2][:, :], p_hi[st % 3][:, :], ALU.subtract).then_inc(lo_set, 1)

            def norm_o(i, nb):
                b = i * NB + nb
                dve.wait_ge(o_turned, b + 1)
                t = t_ps[:, :].rearrange("p (s v) -> p s v", s=4)
                nc.vector.reciprocal(rden[:, :], t[:, :, DH]).then_inc(den_set, 1)
                dve.wait_ge(den_set, b + 1)
                dve.wait_ge(o_stored, b * 16 + 16)
                nc.vector.tensor_tensor(o_out[:, :, :], t[:, :, 0:DH], rden[:, :, None].to_broadcast([P, 4, DH]), ALU.mult).then_inc(o_set, 1)

            def body(i):
                for st in range(BODY):
                    nb, kp = divmod(st, STEPS)
                    its = list(ITEM_STEPS[kp]) if kp < 7 else []
                    for c in its[:2]:
                        read_max(i, nb, c)
                    if st:
                        low(i, st - 1)
                    for c in its[2:]:
                        read_max(i, nb, c)
                    if kp == 6:
                        columns(i, nb)
                    if kp == 4 and nb:
                        norm_o(i, nb - 1)
                    if kp == 0 and nb == ADA + 1:
                        dve.wait_ge(ada_done, i * 2 + 1)
                        nc.vector.tensor_copy(ada_row[:, :], t_ps[0:2, :]).then_inc(ada_set, 1)
                    if kp == 2 and nb == ADA + 1:
                        dve.wait_ge(ada_done, i * 2 + 2)
                        m = bass.ds(i * MT + M0, MT)
                        nc.vector.tensor_tensor(g.mods[:, m, :], t_ps[:, 0:2 * MT].rearrange("p (m c) -> p m c", c=2),
                                                g.b_ada[:, m, None].to_broadcast([P, MT, 2]), ALU.add).then_inc(ada_set, 1)
                low(i, BODY - 1)
                norm_o(i, NB - 1)
            each_turn(dve, body)
            dve.wait_ge(ada_set, 2 * HEADS)
            nc.vector.tensor_scalar(g.mods[:, 32:40, :], g.mods[:, 32:40, :], 1.0, None, ALU.add).then_inc(ada_set, 1)

        @block.tensor
        def _(pe):

            def items(i, nb, cs_):
                q0 = ((nb + 1) % NQB) * QB
                for c in cs_:
                    s, k = ITEMS[c]
                    k0, width = CHUNKS[k]
                    if c >= 2:
                        pe.wait_ge(mx_read, reads_no(i, nb, c - 1))
                    elif c == 0:
                        need(pe, mx_read, reads_no(i, nb, 0) if nb >= 0 else 0)
                    elif nb >= 0:
                        pe.wait_ge(row_set, i * NB + nb + 1)
                    queries = slice(q0 + s * P, q0 + (s + 1) * P)
                    lhs, rhs = (mq_hi[0:QK, queries], mk_hi[0:QK, k0:k0 + width]) if is_mla(nb + 1) else (gq_hl[:, queries], gk_hh[:, k0:k0 + width])
                    nc.tensor.matmul(mx[(NI * (nb + 1) + c) % 2][:, 0:width], lhs, rhs, start=True, stop=True).then_inc(mx_done, 1)

            def lay_row(i, nb):
                pe.wait_ge(mx_read, reads_no(i, nb, NI - 2))
                pe.wait_ge(col_set, i * NB + nb + 3)
                for s in range(4):
                    mm = nc.tensor.matmul(mx[(NI * (nb + 1) + NI - 1) % 2][:, s * P:(s + 1) * P], mcol[0 if is_mla(nb + 1) else 1][:, s], g.ident_r[:, :],
                                          start=True, stop=True)
                mm.then_inc(mx_done, 1)

            def scores(i, st, half):
                nb, kp = divmod(st, STEPS)
                n = i * BODY + st
                if st >= 2 and half == 0:
                    pe.wait_ge(exped, n - 1)
                if kp == 0 and half == 0:
                    pe.wait_ge(row_set, i * NB + nb + 1)
                q = slice((nb % NQB) * QB, (nb % NQB + 1) * QB)
                k = slice((2 * kp + half) * P, (2 * kp + half + 1) * P)
                out = sc[st % 2][:, half * QB:(half + 1) * QB]
                if nb < NQB:
                    ops = ((mk_hi[:, k], mq_hi[:, q]), (mk_hi[0:QK, k], mq_lo[:, q]), (mk_lo[:, k], mq_hi[0:QK, q]))
                else:
                    ops = ((gk_hh[:, k], gq_hl[:, q]), (gk_lo[:, k], gq_hm[:, q]))
                for m, (x, y) in enumerate(ops):
                    mm = nc.tensor.matmul(out, x, y, start=(m == 0), stop=(m == len(ops) - 1))
                if half == 1:
                    mm.then_inc(scored, 1)

            def values(i, st, half):
                nb, kp = divmod(st, STEPS)
                n = i * BODY + st
                if half == 0:
                    pe.wait_ge(lo_set, n + 1)
                if kp == 0 and nb and half == 0:
                    pe.wait_ge(o_copied, i * NB + nb)
                if st == 0 and half == 0:
                    pe.wait_ge(in_mv, i * (16 * LOADS_MV) + 16 * LOADS_MV)
                kind = nb // NQB
                kt, cols = 2 * kp + half, slice(half * QB, (half + 1) * QB)
                ops = ((v1[kind][:, kt], p_hi[st % 3][:, cols]), (v1[kind][:, kt], p_lo[st % 3][:, cols]), (v0[kind][:, kt], p_hi[st % 3][:, cols]))
                for m, (x, y) in enumerate(ops):
                    mm = nc.tensor.matmul(o_ps[:, :], x, y, start=(kt == 0 and m == 0), stop=(kt == KT - 1 and m == 2))
                if half == 1:
                    mm.then_inc(pv_done, 1)

            def turn_o(i, nb):
                b = i * NB + nb
                pe.wait_ge(o_copied, b + 1)
                if nb:
                    pe.wait_ge(o_set, b)
                if nb == ADA:
                    pe.wait_ge(ada_set, i * 2 + 2)
                for s in range(4):
                    mm = nc.tensor.transpose(t_ps[:, s * P:(s + 1) * P], o_sb[:, s * P:(s + 1) * P], g.ident[:, :])
                mm.then_inc(o_turned, 1)

            def modulations(i, ks):
                for k in ks:
                    if k == 0:
                        pe.wait_ge(wa_in, i * 16 + 16)
                        pe.wait_ge(o_set, i * NB + ADA)
                    mm = nc.tensor.matmul(t_ps[0:2, :], g.cond[:, 2 * k:2 * k + 2], wa[:, k, :], start=(k == 0), stop=(k == KD - 1))
                    if k == KD - 1:
                        mm.then_inc(ada_done, 1)

            def modulation_columns(i):
                for c in range(MT):
                    mm = nc.tensor.transpose(t_ps[:, 2 * c:2 * c + 2], ada_row[:, c * P:(c + 1) * P], g.ident[0:2, 0:2])
                mm.then_inc(ada_done, 1)

            pe.wait_ge(in_mh, 16 * (LOADS_MQ + KPE))
            items(0, -1, range(NI - 1))
            lay_row(0, -1)
            pe.wait_ge(consts, 3)
            pe.wait_ge(in_ml, 16 * LOADS_MQ)

            def body(i):
                for st in range(BODY):
                    nb, kp = divmod(st, STEPS)
                    its = list(ITEM_STEPS[kp]) if kp < 7 else []
                    scores(i, st, 0)
                    if kp == 0 and nb == NQB - 1:
                        pe.wait_ge(in_g, i * (16 * LOADS_G) + 16 * LOADS_G)
                    if kp == 0 and nb == NB - 1:
                        pe.wait_ge(in_mh, i * (16 * LOADS_MQ) + 16 * (2 * LOADS_MQ + KPE))
                        pe.wait_ge(in_ml, i * (16 * LOADS_MQ) + 32 * LOADS_MQ)
                    items(i, nb, its[:1])
                    scores(i, st, 1)
                    items(i, nb, its[1:2])
                    if kp == 3 and nb:
                        turn_o(i, nb - 1)
                    if st >= 2:
                        values(i, st - 2, 0)
                    items(i, nb, its[2:3])
                    if nb == ADA + 1 and kp == 1:
                        pe.wait_ge(ada_set, i * 2 + 1)
                    if st >= 2:
                        values(i, st - 2, 1)
                    if nb == ADA and kp >= 5:
                        modulations(i, range(2 * (kp - 5), 2 * (kp - 4)))
                    if nb == ADA + 1 and kp == 1:
                        modulation_columns(i)
                    if kp == 7:
                        lay_row(i, nb)
                for st in (BODY - 2, BODY - 1):
                    for half in range(2):
                        values(i, st, half)
                turn_o(i, NB - 1)
            each_turn(pe, body)


def gate_row(nc, pe, g, ps_pair, m0):
    for k in range(KD):
        mm = nc.tensor.matmul(ps_pair[:, k * P:(k + 1) * P], g.mods[:, m0 + k, 0:1].to_broadcast([P, P]), g.ident[:, :],
                              start=True, stop=True)
    return mm


def w1_slice(w1, g, j):
    n = KD // g.W1S
    return w1[:, n * j:n * (j + 1)].rearrange("p k c -> p (k c)")


def load_w1(sp, g, a, j, q):
    n = KD // g.W1S
    return sp.dma_start(g.rows[j][:, :].rearrange("p (k c) -> p k c", k=n),
                        a["w1"][j * n * P:(j + 1) * n * P, bass.ds(q * g.GF, g.GF)].rearrange("(k p) c -> p k c", p=P))


def stage_mix(nc, g, a):
    with ExitStack() as ctx:
        sb = lambda n, s, d=F32: ctx.enter_context(nc.sbuf_tensor("o_" + n, s, d))
        ps = lambda n, s: ctx.enter_context(nc.psum_tensor("o_" + n, s, F32))
        sem = lambda n: ctx.enter_context(nc.semaphore("o_" + n))
        KO = 2 * HM * DH // P
        wo_hi, wo_lo = sb("wo_hi", [P, KD, D], F32R), sb("wo_lo", [P, KD, D], F32R)
        stage = g.rows
        N = len(stage)
        mix = [sb(f"mix{i}", [P, KO * P]) for i in range(2)]
        m_hi = [sb(f"m_hi{i}", [P, KD, P], F32R) for i in range(2)]
        m_lo = [sb(f"m_lo{i}", [P, KD, P], F32R) for i in range(2)]
        x = [sb(f"x{i}", [P, D]) for i in range(2)]
        gate, ln_g, ln_b = sb("gate", [P, D]), sb("ln_g", [P, D]), sb("ln_b", [P, D])
        r = [sb(f"r{i}", [P, D]) for i in range(2)]
        x1 = [sb(f"x1{i}", [P, D]) for i in range(2)]
        u = sb("u", [P, KD, P])
        u_hi, u_lo = sb("u_hi", [P, KD, P], F32R), sb("u_lo", [P, KD, P], F32R)
        stats, mv, var, rstd, tmp = sb("stats", [P, 2, 6]), sb("mv", [P, 2]), sb("var", [P, 1]), sb("rstd", [P, 1]), sb("tmp", [P, 1])
        t_mix, t_x = ps("t_mix", [P, 2, 512]), ps("t_x", [P, 2, 512])
        y = [ps(f"y{i}", [P, 2, 512]) for i in range(2)]

        rows_in, gate_step = sem("rows_in"), sem("gate_step")
        w_in = [sem(f"w_in{i}") for i in range(N)]
        w_hi_set, w_lo_set = sem("w_hi_set"), sem("w_lo_set")
        mix_in = [sem(f"mix_in{i}") for i in range(2)]
        x_in = [sem(f"x_in{i}") for i in range(2)]
        turned, m_hi_set, m_lo_set, y_done, y_read = sem("turned"), sem("m_hi_set"), sem("m_lo_set"), sem("y_done"), sem("y_read")
        step, var_set, std_set, normed, x1_set = sem("step"), sem("var_set"), sem("std_set"), sem("normed"), sem("x1_set")
        x_turned, u_set, u_hi_set, u_lo_set = sem("x_turned"), sem("u_set"), sem("u_hi_set"), sem("u_lo_set")
        x1_stored = [sem(f"x1_stored{i}") for i in range(2)]
        u_stored, mlp_in = sem("u_stored"), sem("mlp_in")
        block = ctx.enter_context(nc.Block())
        raw = lambda t: t.bitcast(F32)
        STEPS = 9

        def schedule(eng, first, work, out):
            def step_(i, c, n):
                t = i * 2 + c
                if n > 1:
                    first(t + 1, (c + 1) % 2, i + (c + 1) // 2, n > 3)
                work(t, c % 2, i + c // 2, n > 2)
                if c > 0:
                    out(t - 1, (c - 1) % 2, i + (c - 1) // 2)
            first(0, 0, 0, True)
            step_(0, 0, TT)
            with eng.Fori(0, (TT - 4) // 2) as i:
                step_(i, 1, TT)
                step_(i, 2, TT)
            for n in (3, 2, 1):
                step_(0, TT - n, n)
            out(TT - 1, 1, (TT - 1) // 2)

        @block.sync
        def _(sp):
            for k in range(KD):
                if k >= N:
                    sp.wait_ge(w_lo_set, k - N + 1)
                    sp.dma_start(stage[k % N][:, :], a["w_o"][k * P:(k + 1) * P, :]).then_inc(w_in[k % N], 16)
                else:
                    sp.sem_inc(w_in[k], 16)


            def store(t, s):
                tok = bass.ds(t * P, P)
                sp.wait_ge(u_lo_set, t + 1)
                sp.dma_start(g.x1[tok, :], x1[s][:, :]).then_inc(x1_stored[s], 16)
                for part, t_ in enumerate((u_hi, u_lo)):
                    sp.dma_start(g.u2[part][:, :, tok].rearrange("k p t -> p k t"), raw(t_[:, :, :])).then_inc(u_stored, 16)
            for row, name in ((ln_g, "ln1_g"), (ln_b, "ln1_b")):
                sp.dma_start(row[:, :], a[name]).then_inc(rows_in, 16)
            sp.wait_ge(rows_in, 32)
            sp.wait_ge(w_lo_set, KD)
            for j in range(g.W1S):
                load_w1(sp, g, a, j, 0).then_inc(mlp_in, 16)
            for half in range(2):
                with sp.Fori(0, TT // 4) as i:
                    for s in range(2):
                        store(i * 2 + (half * (TT // 2) + s), s)
                if half == 0:
                    sp.wait_ge(u_stored, 32 * (TT // 2))
                    for part in range(2):
                        sp.dma_start(raw(g.u0[part][:, :, :]), g.u2[part][:, :, 0:512].rearrange("k p t -> p k t")).then_inc(mlp_in, 16)
            sp.wait_ge(u_stored, 32 * TT)
            sp.wait_ge(mlp_in, 16 * (g.W1S + 2))
            for s in range(2):
                sp.wait_ge(x1_stored[s], 16 * (TT // 2))

        @block.scalar
        def _(act):
            for t in range(2):
                act.dma_start(mix[t][:, :], g.mix[t * P:(t + 1) * P, :]).then_inc(mix_in[t], 16)
                act.dma_start(x[t][:, :], a["x"][t * P:(t + 1) * P, :]).then_inc(x_in[t], 16)
                for part, m in enumerate((m_hi, m_lo)):
                    act.dma_start(raw(m[t][:, KO:KD]), g.co[part][:, :, t * P:(t + 1) * P].rearrange("c p t -> p c t")).then_inc(x_in[t], 16)
            for k in range(KD):
                act.wait_ge(w_in[k % N], 16 * (k // N + 1))
                nc.scalar.activation(wo_hi[:, k], stage[k % N][:, :], ACT.Copy).then_inc(w_hi_set, 1)

            def load_mix(t, s):
                act.dma_start(mix[s][:, :], g.mix[bass.ds(t * P, P), :]).then_inc(mix_in[s], 16)

            def load_x(t, s):
                tok = bass.ds(t * P, P)
                if not isinstance(t, int) or t >= 2:
                    act.wait_ge(y_done, t - 1)
                    act.wait_ge(y_read, t - 1)
                act.dma_start(x[s][:, :], a["x"][tok, :]).then_inc(x_in[s], 16)
                for part, m in enumerate((m_hi, m_lo)):
                    act.dma_start(raw(m[s][:, KO:KD]), g.co[part][:, :, tok].rearrange("c p t -> p c t")).then_inc(x_in[s], 16)

            def first(t, s, pair, more=True):
                act.wait_ge(turned, t + 1)
                if more:
                    load_mix(t + 2, s)
                if not isinstance(t, int) or t >= 2:
                    act.wait_ge(y_done, t - 1)
                nc.scalar.activation(m_hi[s][:, 0:4], t_mix[:, 0, :].rearrange("p (k t) -> p k t", t=P), ACT.Copy)
                nc.scalar.activation(m_hi[s][:, 4:KO], t_mix[:, 1, 0:2 * P].rearrange("p (k t) -> p k t", t=P), ACT.Copy).then_inc(m_hi_set, 1)

            def work(t, s, pair, more=True):
                act.wait_ge(var_set, t + 1)
                nc.scalar.activation(rstd[:, :], var[:, :], ACT.Sqrt).then_inc(std_set, 1)
                if more:
                    load_x(t + 2, s)

            def out(t, s, pair):
                act.wait_ge(x_turned, t + 1)
                need(act, u_lo_set, t)
                for k in range(KD):
                    last = nc.scalar.activation(u[:, k], t_x[:, k // 4, (k % 4) * P:(k % 4 + 1) * P], ACT.Identity,
                                                scale=g.mods[:, 32 + k, 0:1], bias=g.mods[:, 24 + k, 0:1])
                last.then_inc(u_set, 1)
                act.wait_ge(u_set, t + 1)
                need(act, u_stored, t * 32)
                nc.scalar.activation(u_hi[:, :, :], u[:, :, :], ACT.Copy).then_inc(u_hi_set, 1)
            schedule(act, first, work, out)
            act.wait_ge(mlp_in, 16 * (g.W1S + 2))
            for j in range(g.W1S):
                nc.scalar.activation(w1_slice(g.w1_hi, g, j), stage[j][:, :], ACT.Copy).then_inc(w_hi_set, 1)

        @block.vector
        def _(dve):
            for k in range(KD):
                dve.wait_ge(w_hi_set, k + 1)
                nc.vector.tensor_tensor(wo_lo[:, k], stage[k % N][:, :], wo_hi[:, k], ALU.subtract).then_inc(w_lo_set, 1)
            dve.wait_ge(gate_step, 1)
            nc.vector.tensor_copy(gate[:, :], t_x[:, :, :].rearrange("p b n -> p (b n)")).then_inc(gate_step, 1)
            dve.wait_ge(gate_step, 2)

            def first(t, s, pair, more):
                dve.wait_ge(m_hi_set, t + 1)
                nc.vector.tensor_tensor(m_lo[s][:, 0:4], t_mix[:, 0, :].rearrange("p (k t) -> p k t", t=P), m_hi[s][:, 0:4], ALU.subtract)
                nc.vector.tensor_tensor(m_lo[s][:, 4:KO], t_mix[:, 1, 0:2 * P].rearrange("p (k t) -> p k t", t=P), m_hi[s][:, 4:KO],
                                        ALU.subtract).then_inc(m_lo_set, 1)

            def work(t, s, pair, more):
                seen = [0]

                def link(ins):
                    seen[0] += 1
                    ins.then_inc(step, 1)
                    dve.wait_ge(step, t * STEPS + seen[0])
                dve.wait_ge(y_done, t + 1)
                dve.wait_ge(x_in[s], pair * 48 + 48)
                if not isinstance(t, int) or t >= 2:
                    dve.wait_ge(x1_set, t - 1)
                link(nc.vector.tensor_tensor(r[s][:, :], y[s][:, :, :].rearrange("p b n -> p (b n)"), gate[:, :], ALU.mult))
                nc.vector.scalar_tensor_tensor(out=r[s][:, :], in0=x[s][:, :], scalar=ALPHA, in1=r[s][:, :], op0=ALU.mult, op1=ALU.add).then_inc(y_read, 1)
                dve.wait_ge(y_read, t + 1)
                for b in range(2):
                    ins = nc.vector.bn_stats(stats[:, b, :], r[s][:, b * 512:(b + 1) * 512])
                link(ins)
                nc.vector.memset(tmp[:, :], 0.0)
                link(nc.vector.bn_aggr(mv[:, :], stats[:, :, :]))
                nc.vector.tensor_scalar(var[:, :], mv[:, 1:2], EPS, None, ALU.add).then_inc(var_set, 1)
                dve.wait_ge(std_set, t + 1)
                link(nc.vector.reciprocal(rstd[:, :], rstd[:, :]))
                link(nc.vector.tensor_tensor(tmp[:, :], rstd[:, :], rstd[:, :], ALU.mult))
                link(nc.vector.tensor_tensor(tmp[:, :], tmp[:, :], var[:, :], ALU.mult))
                link(nc.vector.tensor_scalar(tmp[:, :], tmp[:, :], -0.5, 1.5, ALU.mult, ALU.add))
                link(nc.vector.tensor_tensor(rstd[:, :], rstd[:, :], tmp[:, :], ALU.mult))
                link(nc.vector.tensor_scalar(r[s][:, :], r[s][:, :], mv[:, 0:1], rstd[:, 0:1], ALU.subtract, ALU.mult))
                dve.wait_ge(rows_in, 32)
                if not isinstance(t, int) or t >= 2:
                    dve.wait_ge(x1_stored[s], pair * 16)
                    dve.wait_ge(x_turned, t - 1)
                nc.vector.tensor_tensor(x1[s][:, :], r[s][:, :], ln_g[:, :], ALU.mult).then_inc(normed, 1)
                assert seen[0] == STEPS, seen

            def out(t, s, pair):
                dve.wait_ge(u_hi_set, t + 1)
                nc.vector.tensor_tensor(u_lo[:, :, :], u[:, :, :], u_hi[:, :, :], ALU.subtract).then_inc(u_lo_set, 1)
            schedule(dve, first, work, out)

        @block.gpsimd
        def _(pool):
            pool.wait_ge(rows_in, 32)

            def work(t, s, pair, more):
                pool.wait_ge(normed, t + 1)
                nc.gpsimd.tensor_tensor(x1[s][:, :], x1[s][:, :], ln_b[:, :], ALU.add).then_inc(x1_set, 1)
            schedule(pool, lambda *_: None, work, lambda *_: None)
            for j in range(g.W1S):
                pool.wait_ge(w_hi_set, KD + j + 1)
                nc.gpsimd.tensor_tensor(w1_slice(g.w1_lo, g, j), stage[j][:, :], w1_slice(g.w1_hi, g, j), ALU.subtract)

        @block.tensor
        def _(pe):
            gate_row(nc, pe, g, t_x[:, :, :].rearrange("p b n -> p (b n)"), 16).then_inc(gate_step, 1)

            def first(t, s, pair, more):
                pe.wait_ge(mix_in[s], pair * 16 + 16)
                need(pe, m_lo_set, t)
                for k in range(KO):
                    mm = nc.tensor.transpose(t_mix[:, k // 4, (k % 4) * P:(k % 4 + 1) * P], mix[s][:, k * P:(k + 1) * P], g.ident[:, :])
                mm.then_inc(turned, 1)

            def work(t, s, pair, more):
                pe.wait_ge(m_lo_set, t + 1)
                pe.wait_ge(x_in[s], pair * 48 + 48)
                need(pe, y_read, t - 1)
                for k in range(KD):
                    if isinstance(t, int) and t == 0:
                        pe.wait_ge(w_lo_set, k + 1)
                    for n, (x_, w_) in enumerate(((m_hi, wo_hi), (m_hi, wo_lo), (m_lo, wo_hi))):
                        for half in range(2):
                            mm = nc.tensor.matmul(y[s][:, half, :], x_[s][:, k], w_[:, k, half * 512:(half + 1) * 512],
                                                  start=(k == 0 and n == 0), stop=(k == KD - 1 and n == 2))
                mm.then_inc(y_done, 1)

            def out(t, s, pair):
                pe.wait_ge(x1_set, t + 1)
                pe.wait_ge(gate_step, 2)
                need(pe, u_set, t)
                for k in range(KD):
                    mm = nc.tensor.transpose(t_x[:, k // 4, (k % 4) * P:(k % 4 + 1) * P], x1[s][:, k * P:(k + 1) * P], g.ident[:, :])
                mm.then_inc(x_turned, 1)
            schedule(pe, first, work, out)


def stage_mlp(nc, g, a):
    with ExitStack() as ctx:
        sb = lambda n, s, d=F32: ctx.enter_context(nc.sbuf_tensor("f_" + n, s, d))
        ps = lambda n, s: ctx.enter_context(nc.psum_tensor("f_" + n, s, F32))
        sem = lambda n: ctx.enter_context(nc.semaphore("f_" + n))
        HALF = T // 2
        GF = g.GF
        NG = FF // GF
        NF = GF // P
        TB = HALF // 512
        YT = HALF // P
        u_hi, u_lo = [g.u0[0], sb("u_hi1", [P, KD, 512], F32R)], [g.u0[1], sb("u_lo1", [P, KD, 512], F32R)]
        yacc = sb("yacc", [P, YT, D])
        w1_hi, w1_lo = g.w1_hi, g.w1_lo
        w2_hi, w2_lo = sb("w2_hi", [P, NF, D], F32R), sb("w2_lo", [P, NF, D], F32R)
        h_hi, h_lo = sb("h_hi", [P, NF, HALF], F32R), sb("h_lo", [P, NF, HALF], F32R)
        W1S, W2S = g.W1S, NF
        SL = W1S + W2S
        stage = g.rows
        assert len(stage) == SL
        rl = [sb(f"relu{i}", [P, 512]) for i in range(2)]
        gate, ln_g, ln_b = sb("gate", [P, D]), sb("ln_g", [P, D]), sb("ln_b", [P, D])
        r = sb("ln_r", [P, D])
        stats, mv, var, rstd, tmp = sb("stats", [P, 2, 6]), sb("mv", [P, 2]), sb("var", [P, 1]), sb("rstd", [P, 1]), sb("tmp", [P, 1])
        LB = 4
        mv_e, var_e, rstd_e, tmp_e, mean_e = sb("mv_e", [P, YT, 2]), sb("var_e", [P, YT]), sb("rstd_e", [P, YT]), sb("tmp_e", [P, YT]), sb("mean_e", [P, YT])
        one = [ps(f"one{i}", [P, 512]) for i in range(4)]
        two = ps("two", [P, 4, 512])

        u_in = [sem(f"u_in{i}") for i in range(TB)]
        st_in = [sem(f"st_in{i}") for i in range(SL)]
        w_hi_set, w_lo_set = sem("w_hi_set"), sem("w_lo_set")
        one_done, relu_set, sq_set, h_hi_set, h_lo_set = sem("one_done"), sem("relu_set"), sem("sq_set"), sem("h_hi_set"), sem("h_lo_set")
        two_done, two_read = sem("two_done"), sem("two_read")
        y_stored, y_in = ([sem(f"{n}{i}") for i in range(2)] for n in ("y_stored", "y_in"))
        rows_in, gate_step = sem("rows_in"), sem("gate_step")
        ln_in, step, var_set, std_set, normed, ln_out, ln_stored = (sem(n) for n in (
            "ln_in", "ln_step", "var_set", "std_set", "normed", "ln_out", "ln_stored"))
        gated, centred, scaled, out_even, out_odd, out_stored = (sem(n) for n in (
            "gated", "centred", "scaled", "out_even", "out_odd", "out_stored"))
        block = ctx.enter_context(nc.Block())
        raw = lambda t: t.bitcast(F32)
        ONES, TWOS = TB * NF, YT * 2
        LN_STEPS = 8

        def groups(eng, group):
            for hf in range(2):
                group(hf * NG, True, None, False)
                if hf == 0:
                    with eng.Fori(0, NG - 1) as q:
                        group(q + 1, False, None, False)
                else:
                    with eng.Fori(0, YT) as q:
                        group(q + (NG + 1), False, q, False)
                    with eng.Fori(0, NG - YT - 2) as q:
                        group(q + (NG + YT + 1), False, None, False)
            group(2 * NG - 1, False, None, True)

        @block.sync
        def _(sp):
            def weights(gn, q):
                for j in range(SL) if not isinstance(gn, int) or gn else range(W1S, SL):
                    if not isinstance(gn, int) or gn:
                        sp.wait_ge(w_lo_set, gn * SL + (j - SL + 1))
                    if j < W1S:
                        load_w1(sp, g, a, j, q).then_inc(st_in[j], 16)
                    else:
                        sp.dma_start(stage[j][:, :], a["w2"][bass.ds(q * GF + (j - W1S) * P, P), :]).then_inc(st_in[j], 16)

            def load_u(hf, tb):
                for part, t in enumerate((u_hi[tb], u_lo[tb])):
                    sp.dma_start(raw(t[:, :, :]), g.u2[part][:, :, hf * HALF + tb * 512:hf * HALF + (tb + 1) * 512].rearrange("k p t -> p k t")).then_inc(u_in[tb], 16)

            for j in range(W1S):
                sp.sem_inc(st_in[j], 16)
            def load_y(hf, part):
                n = YT // 2
                sp.dma_start(yacc[:, part * n:(part + 1) * n, :],
                             g.x1[hf * HALF + part * n * P:hf * HALF + (part + 1) * n * P, :].rearrange("(t p) d -> p t d", p=P)).then_inc(y_in[part], 16)
            load_u(0, 1)
            weights(0, 0)
            load_y(0, 0)
            load_y(0, 1)
            weights(1, 1)
            for row, name in ((ln_g, "ln2_g"), (ln_b, "ln2_b")):
                sp.dma_start(row[:, :], a[name]).then_inc(rows_in, 16)
            with sp.Fori(0, NG - 2) as q:
                weights(q + 2, q + 2)
            sp.wait_ge(one_done, (NG - 1) * ONES + NF)
            load_u(1, 0)
            weights(NG, 0)
            sp.wait_ge(one_done, NG * ONES)
            load_u(1, 1)
            for part in range(2):
                n = YT // 2
                sp.wait_ge(two_read, (NG - 1) * TWOS + (part + 1) * 2 * n)
                sp.dma_start(g.y[part * n * P:(part + 1) * n * P, :].rearrange("(t p) d -> p t d", p=P), yacc[:, part * n:(part + 1) * n, :]).then_inc(y_stored[part], 16)
            for part in range(2):
                sp.wait_ge(y_stored[part], 16)
                load_y(1, part)

            def with_tile(t):
                weights(t + (NG + 1), t + 1)
                need(sp, ln_stored, t * 16)
                sp.dma_start(r[:, :], g.y[bass.ds(t * P, P), :]).then_inc(ln_in, 16)
            with_tile(0)
            with sp.Fori(0, YT - 1) as t:
                with_tile(t + 1)
            with sp.Fori(0, NG - YT - 1) as q:
                weights(q + (NG + YT + 1), q + (YT + 1))
            for t in range(YT):
                sp.wait_ge(out_odd if t % 2 else out_even, t // 2 + 1)
                sp.dma_start(a["out"][0, HALF + t * P:HALF + (t + 1) * P, :], yacc[:, t, :]).then_inc(out_stored, 16)
            sp.wait_ge(out_stored, 16 * YT)
            sp.wait_ge(ln_stored, 16 * YT)

        @block.scalar
        def _(act):
            def slice_hi(gn, j, dst):
                act.wait_ge(st_in[j], gn * 16 + 16)
                if j >= W1S:
                    act.wait_ge(gated, gn * W2S + (j - W1S + 1))
                nc.scalar.activation(dst, stage[j][:, :], ACT.Copy).then_inc(w_hi_set, 1)

            def w1_of(gn):
                for j in range(W1S):
                    slice_hi(gn, j, w1_slice(w1_hi, g, j))

            def hidden(gn, o):
                tb, f = divmod(o, NF)
                n = gn * ONES + o
                act.wait_ge(one_done, n + 1)
                nc.scalar.activation(rl[o % 2][:, :], one[o % 4][:, :], ACT.Relu).then_inc(relu_set, 1)
                act.wait_ge(sq_set, n + 1)
                nc.scalar.activation(h_hi[:, f, tb * 512:(tb + 1) * 512], rl[o % 2][:, :], ACT.Copy).then_inc(h_hi_set, 1)

            def group(gn, first, ln, last):
                for o in range(ONES):
                    if o < W2S:
                        act.wait_ge(one_done, gn * ONES + 1)
                        slice_hi(gn, W1S + o, w2_hi[:, o])
                    hidden(gn, o)
                if not last:
                    act.wait_ge(one_done, gn * ONES + ONES)
                    w1_of(gn + 1)
                if ln is not None:
                    act.wait_ge(var_set, ln + 1)
                    nc.scalar.activation(rstd[:, :], var[:, :], ACT.Sqrt).then_inc(std_set, 1)
            act.sem_inc(w_hi_set, W1S)
            act.wait_ge(gate_step, 1)
            nc.scalar.activation(gate[:, :], two[:, 0:2, :].rearrange("p b n -> p (b n)"), ACT.Copy).then_inc(gate_step, 1)
            groups(act, group)
            for b in range(YT // LB):
                act.wait_ge(var_set, YT + 2 * (b + 1))
                nc.scalar.activation(rstd_e[:, b * LB:(b + 1) * LB], var_e[:, b * LB:(b + 1) * LB], ACT.Sqrt).then_inc(std_set, 1)
                for t in range(b * LB, (b + 1) * LB):
                    nc.scalar.activation(yacc[:, t, :], yacc[:, t, :], ACT.Identity, bias=mean_e[:, t:t + 1]).then_inc(centred, 1)

        @block.gpsimd
        def _(pool):
            def slice_lo(gn, j, hi, lo):
                pool.wait_ge(w_hi_set, gn * SL + (j + 1))
                nc.gpsimd.tensor_tensor(lo, stage[j][:, :], hi, ALU.subtract).then_inc(w_lo_set, 1)

            def w1_of(gn):
                for j in range(W1S):
                    slice_lo(gn, j, w1_slice(w1_hi, g, j), w1_slice(w1_lo, g, j))

            def group(gn, first, ln, last):
                for j in range(W2S):
                    slice_lo(gn, W1S + j, w2_hi[:, j], w2_lo[:, j])
                if not last:
                    w1_of(gn + 1)
                if first and gn:
                    pool.wait_ge(rows_in, 32)
                if ln is not None:
                    pool.wait_ge(normed, ln + 1)
                    nc.gpsimd.tensor_tensor(r[:, :], r[:, :], ln_b[:, :], ALU.add).then_inc(ln_out, 1)
                    pool.wait_ge(ln_out, ln + 1)
                    pool.dma_start(a["out"][0, bass.ds(ln * P, P), :], r[:, :]).then_inc(ln_stored, 16)
            pool.sem_inc(w_lo_set, W1S)
            groups(pool, group)
            for t in range(0, YT, 2):
                pool.wait_ge(scaled, t + 1)
                nc.gpsimd.tensor_tensor(yacc[:, t, :], yacc[:, t, :], ln_b[:, :], ALU.add).then_inc(out_even, 1)

        @block.vector
        def _(dve):
            def newton(link, rstd, var, tmp):
                link(nc.vector.reciprocal(rstd, rstd))
                link(nc.vector.tensor_tensor(tmp, rstd, rstd, ALU.mult))
                link(nc.vector.tensor_tensor(tmp, tmp, var, ALU.mult))
                link(nc.vector.tensor_scalar(tmp, tmp, -0.5, 1.5, ALU.mult, ALU.add))
                link(nc.vector.tensor_tensor(rstd, rstd, tmp, ALU.mult))

            def layer_norm(t):
                seen = [0]

                def link(ins):
                    seen[0] += 1
                    ins.then_inc(step, 1)
                    dve.wait_ge(step, t * LN_STEPS + seen[0])
                dve.wait_ge(ln_in, t * 16 + 16)
                nc.vector.bn_stats(stats[:, 0, :], r[:, 0:512])
                link(nc.vector.bn_stats(stats[:, 1, :], r[:, 512:]))
                nc.vector.memset(tmp[:, :], 0.0)
                link(nc.vector.bn_aggr(mv[:, :], stats[:, :, :]))
                nc.vector.tensor_scalar(var[:, :], mv[:, 1:2], EPS, None, ALU.add).then_inc(var_set, 1)
                dve.wait_ge(std_set, t + 1)
                newton(link, rstd[:, :], var[:, :], tmp[:, :])
                link(nc.vector.tensor_scalar(r[:, :], r[:, :], mv[:, 0:1], rstd[:, 0:1], ALU.subtract, ALU.mult))
                nc.vector.tensor_tensor(r[:, :], r[:, :], ln_g[:, :], ALU.mult).then_inc(normed, 1)
                assert seen[0] == LN_STEPS, seen

            def add_up(gn, o, first):
                t, half = divmod(o, 2)
                dve.wait_ge(two_done, gn * TWOS + (o + 1))
                acc = yacc[:, t, half * 512:(half + 1) * 512]
                if first:
                    if half == 0 and t % (YT // 2) == 0:
                        dve.wait_ge(y_in[t // (YT // 2)], 16 * (1 + gn // NG))
                    nc.vector.scalar_tensor_tensor(out=acc, in0=acc, scalar=ALPHA, in1=two[:, o % 4, :], op0=ALU.mult, op1=ALU.add).then_inc(two_read, 1)
                else:
                    nc.vector.tensor_tensor(acc, two[:, o % 4, :], acc, ALU.add).then_inc(two_read, 1)

            def group(gn, first, ln, last):
                for j in range(W2S):
                    dve.wait_ge(st_in[W1S + j], gn * 16 + 16)
                    nc.vector.tensor_tensor(stage[W1S + j][:, :], stage[W1S + j][:, :], gate[:, :], ALU.mult).then_inc(gated, 1)
                for o in range(ONES):
                    tb, f = divmod(o, NF)
                    n = gn * ONES + o
                    dve.wait_ge(relu_set, n + 1)
                    nc.vector.tensor_tensor(rl[o % 2][:, :], rl[o % 2][:, :], rl[o % 2][:, :], ALU.mult).then_inc(sq_set, 1)
                    dve.wait_ge(h_hi_set, n + 1)
                    cols = slice(tb * 512, (tb + 1) * 512)
                    nc.vector.tensor_tensor(h_lo[:, f, cols], rl[o % 2][:, :], h_hi[:, f, cols], ALU.subtract).then_inc(h_lo_set, 1)
                if first and gn:
                    dve.wait_ge(rows_in, 32)
                if last:
                    return
                for o in range(TWOS):
                    add_up(gn, o, first)
                if ln is not None:
                    layer_norm(ln)
            dve.wait_ge(gate_step, 2)
            groups(dve, group)

            steps = [0]

            def link(ins):
                steps[0] += 1
                ins.then_inc(step, 1)
                dve.wait_ge(step, YT * LN_STEPS + steps[0])

            def statistics(t):
                dve.wait_ge(two_read, (2 * NG - 1) * TWOS + 2 * (t + 1))
                nc.vector.bn_stats(stats[:, 0, :], yacc[:, t, 0:512])
                link(nc.vector.bn_stats(stats[:, 1, :], yacc[:, t, 512:]))
                link(nc.vector.bn_aggr(mv_e[:, t, :], stats[:, :, :]))

            def chain(b):
                c = slice(b * LB, (b + 1) * LB)
                nc.vector.tensor_scalar(var_e[:, c], mv_e[:, c, 1], EPS, None, ALU.add).then_inc(var_set, 1)
                nc.vector.tensor_scalar(mean_e[:, c], mv_e[:, c, 0], -1.0, None, ALU.mult).then_inc(var_set, 1)
                dve.wait_ge(std_set, YT + b + 1)
                newton(link, rstd_e[:, c], var_e[:, c], tmp_e[:, c])

            def finish(t):
                dve.wait_ge(centred, t + 1)
                ins = nc.vector.scalar_tensor_tensor(out=yacc[:, t, :], in0=yacc[:, t, :], scalar=rstd_e[:, t:t + 1], in1=ln_g[:, :], op0=ALU.mult, op1=ALU.mult)
                ins.then_inc(scaled, 1)
                if t % 2:
                    dve.wait_ge(scaled, t + 1)
                    nc.vector.tensor_tensor(yacc[:, t, :], yacc[:, t, :], ln_b[:, :], ALU.add).then_inc(out_odd, 1)
            for t in range(YT + 1):
                if t < YT:
                    add_up(2 * NG - 1, 2 * t, False)
                    add_up(2 * NG - 1, 2 * t + 1, False)
                if t:
                    statistics(t - 1)
                if t > LB:
                    finish(t - 1 - LB)
                if t and t % LB == 0:
                    chain(t // LB - 1)
            for t in range(YT - LB, YT):
                finish(t)

        @block.tensor
        def _(pe):
            gate_row(nc, pe, g, two[:, 0:2, :].rearrange("p b n -> p (b n)"), 40).then_inc(gate_step, 1)

            def group(gn, first, ln, last):
                pe.wait_ge(w_lo_set, gn * SL + W1S)
                for o in range(ONES):
                    tb, f = divmod(o, NF)
                    if first and f == 0:
                        need(pe, u_in[tb], 32 * ((gn > 0) + tb))
                    if o >= 4:
                        pe.wait_ge(relu_set, gn * ONES + (o - 3))
                    for k in range(KD):
                        w = slice(f * P, (f + 1) * P)
                        for n, (x_, y_) in enumerate(((w1_hi, u_hi), (w1_hi, u_lo), (w1_lo, u_hi))):
                            mm = nc.tensor.matmul(one[o % 4][:, :], x_[:, k, w], y_[tb][:, k], start=(k == 0 and n == 0), stop=(k == KD - 1 and n == 2))
                    mm.then_inc(one_done, 1)
                pe.wait_ge(w_lo_set, gn * SL + SL)
                if first and gn == 0:
                    pe.wait_ge(gate_step, 2)
                for o in range(TWOS):
                    t, half = divmod(o, 2)
                    if t % 4 == 0 and half == 0:
                        pe.wait_ge(h_lo_set, gn * ONES + NF * (t // 4 + 1))
                    if o >= 4:
                        pe.wait_ge(two_read, gn * TWOS + (o - 3))
                    for f in range(NF):
                        tok, cols = slice(t * P, (t + 1) * P), slice(half * 512, (half + 1) * 512)
                        for n, (x_, y_) in enumerate(((h_hi, w2_hi), (h_hi, w2_lo), (h_lo, w2_hi))):
                            mm = nc.tensor.matmul(two[:, o % 4, :], x_[:, f, tok], y_[:, f, cols], start=(f == 0 and n == 0), stop=(f == NF - 1 and n == 2))
                    mm.then_inc(two_done, 1)
            groups(pe, group)


def make_shared(nc, ctx, a):
    g = Shared()
    sb = lambda n, s, d=F32: ctx.enter_context(nc.sbuf_tensor(n, s, d))
    g.ident, g.ident_r = sb("ident", [P, P]), sb("ident_r", [P, P], F32R)
    g.ones = sb("ones_f", [P, P])
    g.cond = sb("cond_silu", [P, KD * 2])
    g.b_ada = sb("b_ada_c", [P, 48])
    g.mods = sb("mods", [P, 48, 2])
    g.gcol = sb("gcol", [P, 9])
    dram = lambda n, s: nc.dram_tensor(n, s, F32, kind="Internal").ap()
    g.ckv = dram("s_ckv", [2, P, KEYS])
    g.cq = dram("s_cq", [2, 2, P, T])
    g.kg = dram("s_kg", [2, HKV * DH, KEYS])
    g.kpe = dram("s_kpe", [2, ROPE, KEYS])
    g.vg = dram("s_vg", [P, KT, 2, HKV * DH])
    g.qg = dram("s_qg", [2, HG * DH, T])
    g.conv_p, g.conv_b = dram("s_conv_p", [2, P, T]), dram("s_conv_b", [2, P, T])
    g.qn, g.qr = dram("s_qn", [2, HM * NOPE, T]), dram("s_qr", [2, 2, HM * 16, T])
    g.kn = dram("s_kn", [2, HM * NOPE, KEYS])
    g.vm = dram("s_vm", [2, HM, P, KT, DH])
    g.co = dram("s_co", [2, 2, P, T])
    g.mix = dram("s_mix", [T, 2 * HM * DH])
    g.x1, g.u2, g.y = dram("s_x1", [T, D]), dram("s_u2", [2, KD, P, T]), dram("s_y", [T, D])
    return g


STAGES = [stage_modulate, stage_project, stage_expand, stage_attend, stage_mix, stage_mlp]


def build(nc, a, stages=None):
    with ExitStack() as ctx:
        g = make_shared(nc, ctx, a)
        w_in = ctx.enter_context(ExitStack())
        g.w_hi, g.w_lo = (w_in.enter_context(nc.sbuf_tensor(f"win_{part}", [P, KD, NCOL], F32R)) for part in ("hi", "lo"))
        g.xt = [w_in.enter_context(nc.sbuf_tensor(f"xt{i}", [P, KD, P], F32)) for i in range(2)]
        for stage in stages or STAGES:
            if stage is stage_expand:
                w_in.close()
            if stage is stage_attend:
                g.GF = 256
                g.W1S = KD * g.GF // D
                g.rows = [ctx.enter_context(nc.sbuf_tensor(f"w_rows{i}", [P, D], F32)) for i in range(g.W1S + g.GF // P)]
            if stage is stage_mix:
                sb = lambda n, s: ctx.enter_context(nc.sbuf_tensor(n, s, F32R))
                g.u0 = [sb(f"u0_{part}", [P, KD, 512]) for part in ("hi", "lo")]
                g.w1_hi, g.w1_lo = sb("w1_hi", [P, KD, g.GF]), sb("w1_lo", [P, KD, g.GF])
            stage(nc, g, a)


def rope_tables():
    t = np.arange(T)
    row, col = (t // 64).astype(np.float32), (t % 64).astype(np.float32)
    out = []
    for dim in (DH, ROPE):
        n = dim // 4
        inv = (np.float32(10000.0) ** (-np.arange(n, dtype=np.float32) / np.float32(n))).astype(np.float32)
        ang = np.concatenate([row[:, None] * inv, col[:, None] * inv], axis=-1)
        out += [np.cos(ang).astype(np.float32), np.sin(ang).astype(np.float32)]
    return out


def lay_out(x, c, ctx, c_ctx, w_ada, b_ada, w_in, g_cq, w_uq, g_ckv, w_ukv, g_qn, g_kn,
            w_conv, w_o, ln1_g, ln1_b, w_mlp1, w_mlp2, ln2_g, ln2_b):
    f = lambda t: np.ascontiguousarray(t)
    tiles = lambda t: f(t.reshape(-1, P, KD, P).transpose(0, 3, 2, 1))
    rep = lambda row: f(np.broadcast_to(row, (P, row.size)))
    cg, sg, cr, sr = rope_tables()
    w = w_in[0]
    kv, q = 416, 640
    cols = [w[:, 128:160], w[:, 288:416], w[:, 0:128], w[:, 160:288], w[:, kv + 256:kv + q], w[:, kv:kv + 256], w[:, kv + q:]]
    uq, ukv, pad = w_uq[0].reshape(QR, HM, QK), w_ukv[0].reshape(KVR, HM, 2 * DH), np.zeros((QR, 32), np.float32)
    out = {
        "x_t": tiles(x[0]), "ctx_t": tiles(ctx[0]),
        "cond": f(np.stack([c[0].reshape(KD, P).T, c_ctx.reshape(KD, P).T], axis=2).reshape(P, 2 * KD)),
        "w_ada": f(w_ada[0]), "b_ada": f(b_ada[0].reshape(48, P).T),
        "w_in": f(np.concatenate(cols, axis=1)),
        "gcol": f(np.concatenate([g_ckv[0][:, None], g_cq[0].reshape(2, P).T, w_conv[0].reshape(3, 2, P).transpose(2, 1, 0).reshape(P, 6)], axis=1)),
        "g_heads": rep(np.concatenate([g_kn[0]] * HKV + [g_qn[0]] * HG)),
        "inv_n": rep(np.array([1 / KVR] + [1 / DH] * 8 + [1 / QR], np.float32)),
        "cs_tok": f(np.concatenate([cg, sg, cr, sr], axis=1).reshape(TT, P, 96).transpose(1, 0, 2)),
        "w_uq": f(np.concatenate([uq[:, :, :NOPE].reshape(QR, -1), uq[:, :, NOPE::2].reshape(QR, -1), pad,
                                  uq[:, :, NOPE + 1::2].reshape(QR, -1), pad], axis=1)),
        "w_ukv": f(np.concatenate([ukv[:, :, :NOPE].reshape(KVR, -1), ukv[:, :, NOPE:].reshape(KVR, -1)], axis=1)),
        "x": f(x[0]), "w_o": f(w_o[0]), "w1": f(w_mlp1[0]), "w2": f(w_mlp2[0]),
        "ln1_g": rep(ln1_g[0]), "ln1_b": rep(ln1_b[0]), "ln2_g": rep(ln2_g[0]), "ln2_b": rep(ln2_b[0]),
        "cs_rope": f(np.stack([np.tile(cr.T, (HM, 1)), np.tile(sr.T, (HM, 1))], axis=1)),
    }
    return out


def kernel(**inputs):
    import concourse.bacc as bacc
    from concourse.bass_utils import run_bass_kernel_spmd

    arrays = {f"in_{n}": v for n, v in lay_out(**{k: np.asarray(v) for k, v in inputs.items()}).items()}
    nc = bacc.Bacc("TRN2", target_bir_lowering=False, num_devices=1)
    a = {n[3:]: nc.dram_tensor(n, v.shape, mybir.dt.from_np(v.dtype), kind="ExternalInput").ap() for n, v in arrays.items()}
    a["out"] = nc.dram_tensor("out_0", (1, T, D), F32, kind="ExternalOutput").ap()
    build(nc, a)
    r = run_bass_kernel_spmd(nc, [arrays], core_ids=[0])
    return r.results[0]["out_0"]
```
